# Optimizing a Trainium2 kernel written in Bass

```python
import numpy as np
import jax
import jax.numpy as jnp
from jax import lax

D_MODEL = 1024
BATCH = 1
SEQ = 256
DEPTH = 1

SSM_EXPAND = 1
D_INNER = SSM_EXPAND * D_MODEL
SSM_HEAD_DIM = 64
SSM_HEADS = D_INNER // SSM_HEAD_DIM
SSM_GROUPS = 4
D_STATE = 128
CONV_K = 4
CONV_DIM = D_INNER + 2 * SSM_GROUPS * D_STATE
SSD_CHUNK = 128
DT_MIN = 1e-3
DT_MAX = 1e-1
NSA_HEAD_DIM = 64
NSA_HEADS = D_MODEL // NSA_HEAD_DIM
NSA_GROUPS = 4
NSA_REP = NSA_HEADS // NSA_GROUPS
NSA_WIDTH = NSA_HEADS * NSA_HEAD_DIM
NSA_KV_WIDTH = NSA_GROUPS * NSA_HEAD_DIM
CMP_BLOCK = 32
CMP_STRIDE = 16
CMP_HIDDEN = 2 * NSA_HEAD_DIM
SEL_BLOCK = 64
SEL_TOPN = 8
WINDOW = 256
Q_BLOCK = 64
N_EXPERTS = 32
TOP_K = 4
D_EXPERT = D_MODEL
SWIGLU_ALPHA = 1.702
SWIGLU_LIMIT = 7.0
NORM_EPS = 1e-5

IN_WIDTHS = (
    D_INNER,
    CONV_DIM,
    SSM_HEADS,
    NSA_WIDTH,
    NSA_KV_WIDTH, NSA_KV_WIDTH,
    NSA_KV_WIDTH, NSA_KV_WIDTH,
    NSA_KV_WIDTH, NSA_KV_WIDTH,
    3 * NSA_HEADS,
    2 * D_MODEL,
)
IN_DIM = int(sum(IN_WIDTHS))
IN_OFFSETS = [int(o) for o in np.cumsum(IN_WIDTHS)[:-1]]

kernel_name = 'hybrid_ssd_nsa_moe_block'

def rms_norm(x, w):
    xf = x.astype(jnp.float32)
    y = xf * lax.rsqrt(jnp.mean(xf * xf, axis=-1, keepdims=True) + NORM_EPS)
    return (y * w.astype(jnp.float32)).astype(x.dtype)

def masked_softmax(logits, mask):
    l = jnp.where(mask, logits.astype(jnp.float32), -jnp.inf)
    m = jnp.max(l, axis=-1, keepdims=True)
    m = jnp.where(jnp.isfinite(m), m, 0.0)
    e = jnp.where(mask, jnp.exp(l - m), 0.0)
    return e / jnp.maximum(jnp.sum(e, axis=-1, keepdims=True), 1e-30)

def segsum(a):
    t = a.shape[-1]
    cs = jnp.cumsum(a, axis=-1)
    diff = cs[..., :, None] - cs[..., None, :]
    return jnp.where(jnp.tril(jnp.ones((t, t), dtype=bool)), diff, -jnp.inf)

def ssd_chunked_scan(xh, dt, a, b_mat, c_mat):
    bsz, s, nh, hp = xh.shape
    nc = s // SSD_CHUNK

    def chunk(t):
        return t.reshape((bsz, nc, SSD_CHUNK) + t.shape[2:])

    xc = chunk(xh * dt[..., None])
    bc = chunk(b_mat)
    cc = chunk(c_mat)
    a_dt = jnp.moveaxis(chunk(dt * a), -1, 1)
    a_cs = jnp.cumsum(a_dt, axis=-1)
    decay_in = jnp.exp(segsum(a_dt))
    y_diag = jnp.einsum('bclhn,bcshn,bhcls,bcshp->bclhp', cc, bc, decay_in, xc)
    decay_to_end = jnp.exp(a_cs[..., -1:] - a_cs)
    states = jnp.einsum('bclhn,bhcl,bclhp->bchpn', bc, decay_to_end, xc)
    chunk_decay = jnp.exp(a_cs[..., -1])

    def step(carry, inp):
        st, dec = inp
        return carry * dec[..., None, None] + st, carry

    init = jnp.zeros((bsz, nh, hp, D_STATE), xc.dtype)
    _, prev = lax.scan(step, init, (jnp.moveaxis(states, 1, 0), jnp.moveaxis(chunk_decay, 2, 0)))
    prev = jnp.moveaxis(prev, 0, 1)
    y_off = jnp.einsum('bclhn,bchpn,bhcl->bclhp', cc, prev, jnp.exp(a_cs))
    return (y_diag + y_off).reshape(bsz, s, nh, hp)

def mamba2_mixer(z, xbc, dt_raw, conv_w, conv_b, dt_bias, a_log, d_skip, norm_w):
    bsz, s, _ = xbc.shape
    xbc = lax.conv_general_dilated(
        xbc, conv_w[:, None, :], window_strides=(1,), padding=[(CONV_K - 1, 0)],
        dimension_numbers=('NWC', 'WIO', 'NWC'), feature_group_count=CONV_DIM)
    xbc = jax.nn.silu(xbc + conv_b)
    xs, b_mat, c_mat = jnp.split(xbc, [D_INNER, D_INNER + SSM_GROUPS * D_STATE], axis=-1)
    f32 = jnp.float32
    xh = xs.reshape(bsz, s, SSM_HEADS, SSM_HEAD_DIM).astype(f32)
    rep = SSM_HEADS // SSM_GROUPS
    b_mat = jnp.repeat(b_mat.reshape(bsz, s, SSM_GROUPS, D_STATE), rep, axis=2).astype(f32)
    c_mat = jnp.repeat(c_mat.reshape(bsz, s, SSM_GROUPS, D_STATE), rep, axis=2).astype(f32)
    dt = jax.nn.softplus(dt_raw.astype(f32) + dt_bias.astype(f32))
    a = -jnp.exp(a_log.astype(f32))
    y = ssd_chunked_scan(xh, dt, a, b_mat, c_mat) + d_skip.astype(f32)[:, None] * xh
    y = y.reshape(bsz, s, D_INNER) * jax.nn.silu(z.astype(f32))
    yg = y.reshape(bsz, s, SSM_GROUPS, D_INNER // SSM_GROUPS)
    yg = yg * lax.rsqrt(jnp.mean(yg * yg, axis=-1, keepdims=True) + NORM_EPS)
    return (yg.reshape(bsz, s, D_INNER) * norm_w.astype(f32)).astype(z.dtype)

def compress_blocks(kv, pos, w1, w2):
    bsz, s = kv.shape[:2]
    n_cmp = (s - CMP_BLOCK) // CMP_STRIDE + 1
    idx = np.arange(n_cmp)[:, None] * CMP_STRIDE + np.arange(CMP_BLOCK)[None, :]
    blocks = kv[:, idx] + pos[None, None, :, None, :]
    flat = jnp.moveaxis(blocks, 3, 2).reshape(bsz, n_cmp, NSA_GROUPS, CMP_BLOCK * NSA_HEAD_DIM)
    return jax.nn.gelu(flat @ w1) @ w2

def nsa_mixer(q, k_cmp, v_cmp, k_sel, v_sel, k_win, v_win, gate_logits,
              cmp_pos_k, cmp_w1_k, cmp_w2_k, cmp_pos_v, cmp_w1_v, cmp_w2_v):
    bsz, s, _ = q.shape
    G, R, DH = NSA_GROUPS, NSA_REP, NSA_HEAD_DIM
    q = q.reshape(bsz, s, G, R, DH) * (DH ** -0.5)
    kvshape = (bsz, s, G, DH)
    k_cmp, v_cmp, k_sel, v_sel, k_win, v_win = [
        t.reshape(kvshape) for t in (k_cmp, v_cmp, k_sel, v_sel, k_win, v_win)]
    t_pos = jnp.arange(s)

    kc = compress_blocks(k_cmp, cmp_pos_k, cmp_w1_k, cmp_w2_k)
    vc = compress_blocks(v_cmp, cmp_pos_v, cmp_w1_v, cmp_w2_v)
    n_cmp = kc.shape[1]
    cmp_end = jnp.arange(n_cmp) * CMP_STRIDE + CMP_BLOCK - 1
    cmp_mask = cmp_end[None, :] <= t_pos[:, None]
    p_cmp = masked_softmax(jnp.einsum('bsgrd,bcgd->bgrsc', q, kc), cmp_mask)
    o_cmp = jnp.einsum('bgrsc,bcgd->bsgrd', p_cmp.astype(vc.dtype), vc)

    n_sel = s // SEL_BLOCK
    c_start = np.arange(n_cmp) * CMP_STRIDE
    s_start = np.arange(n_sel) * SEL_BLOCK
    overlap = (c_start[:, None] < s_start[None, :] + SEL_BLOCK) & (c_start[:, None] + CMP_BLOCK > s_start[None, :])
    imp = jnp.einsum('bgrsc,cj->bgsj', p_cmp, jnp.asarray(overlap, p_cmp.dtype))
    cur = t_pos // SEL_BLOCK
    j = jnp.arange(n_sel)[None, :]
    forced = (j == 0) | (j == cur[:, None]) | (j == cur[:, None] - 1)
    valid = j <= cur[:, None]
    imp = jnp.where(forced, jnp.inf, jnp.where(valid, imp, -jnp.inf))
    n_top = min(SEL_TOPN, n_sel)
    _, sel_idx = lax.top_k(imp, n_top)

    ks = jnp.transpose(k_sel.reshape(bsz, n_sel, SEL_BLOCK, G, DH), (0, 3, 1, 2, 4))
    vs = jnp.transpose(v_sel.reshape(bsz, n_sel, SEL_BLOCK, G, DH), (0, 3, 1, 2, 4))
    pad = ((0, 0), (WINDOW, 0), (0, 0), (0, 0))
    kwp = jnp.pad(k_win, pad)
    vwp = jnp.pad(v_win, pad)
    bi = jnp.arange(bsz)[:, None, None, None]
    gi = jnp.arange(G)[None, :, None, None]
    sb_off = jnp.arange(SEL_BLOCK)
    w_off = jnp.arange(Q_BLOCK + WINDOW)

    def query_block(i):
        q0 = i * Q_BLOCK
        qb = lax.dynamic_slice_in_dim(q, q0, Q_BLOCK, axis=1)
        tq = q0 + jnp.arange(Q_BLOCK)
        idx = lax.dynamic_slice_in_dim(sel_idx, q0, Q_BLOCK, axis=2)
        kg = ks[bi, gi, idx].reshape(bsz, G, Q_BLOCK, n_top * SEL_BLOCK, DH)
        vg = vs[bi, gi, idx].reshape(bsz, G, Q_BLOCK, n_top * SEL_BLOCK, DH)
        kpos = (idx[..., None] * SEL_BLOCK + sb_off).reshape(bsz, G, Q_BLOCK, n_top * SEL_BLOCK)
        smask = (kpos <= tq[None, None, :, None])[:, :, None]
        p_sel = masked_softmax(jnp.einsum('bqgrd,bgqmd->bgrqm', qb, kg), smask)
        o_sel = jnp.einsum('bgrqm,bgqmd->bqgrd', p_sel.astype(vg.dtype), vg)
        kw = lax.dynamic_slice_in_dim(kwp, q0, Q_BLOCK + WINDOW, axis=1)
        vw = lax.dynamic_slice_in_dim(vwp, q0, Q_BLOCK + WINDOW, axis=1)
        wpos = q0 - WINDOW + w_off
        wmask = (wpos[None, :] <= tq[:, None]) & (wpos[None, :] > tq[:, None] - WINDOW) & (wpos[None, :] >= 0)
        p_win = masked_softmax(jnp.einsum('bqgrd,bkgd->bgrqk', qb, kw), wmask)
        o_win = jnp.einsum('bgrqk,bkgd->bqgrd', p_win.astype(vw.dtype), vw)
        return o_sel, o_win

    o_sel, o_win = lax.map(query_block, jnp.arange(s // Q_BLOCK))
    o_sel = jnp.moveaxis(o_sel, 0, 1).reshape(bsz, s, G, R, DH)
    o_win = jnp.moveaxis(o_win, 0, 1).reshape(bsz, s, G, R, DH)

    g = jax.nn.sigmoid(gate_logits.reshape(bsz, s, G, R, 3))
    o = g[..., 0, None] * o_cmp + g[..., 1, None] * o_sel + g[..., 2, None] * o_win
    return o.reshape(bsz, s, NSA_WIDTH).astype(q.dtype)

def clamped_swiglu(h):
    x_glu = jnp.minimum(h[..., ::2], SWIGLU_LIMIT)
    x_lin = jnp.clip(h[..., 1::2], -SWIGLU_LIMIT, SWIGLU_LIMIT)
    return x_glu * jax.nn.sigmoid(SWIGLU_ALPHA * x_glu) * (x_lin + 1.0)

def moe_ffn(h, router_w, router_b, w_gate_up, b_gate_up, w_down, b_down):
    bsz, s, d = h.shape
    t = h.reshape(bsz * s, d)
    logits = (t @ router_w + router_b).astype(jnp.float32)
    top_v, top_i = lax.top_k(logits, TOP_K)
    top_w = jax.nn.softmax(top_v, axis=-1)
    combine = jnp.einsum('tk,tke->te', top_w, jax.nn.one_hot(top_i, N_EXPERTS, dtype=jnp.float32)).astype(h.dtype)
    out = jnp.zeros_like(t)
    for e in range(N_EXPERTS):
        a = clamped_swiglu(t @ w_gate_up[e] + b_gate_up[e])
        out = out + combine[:, e:e + 1] * (a @ w_down[e] + b_down[e])
    return out.reshape(bsz, s, d)

def setup_inputs(seed: int = 0) -> dict:
    key = jax.random.key(seed)
    ks = jax.random.split(key, 32)
    f32 = jnp.float32
    L = DEPTH

    def nrm(k, shape, scale):
        return jax.random.normal(k, shape, f32) * scale

    dt = jnp.exp(jax.random.uniform(ks[4], (L, SSM_HEADS), f32) * (np.log(DT_MAX) - np.log(DT_MIN)) + np.log(DT_MIN))
    return {
        'x': nrm(ks[0], (BATCH, SEQ, D_MODEL), 1.0),
        'mix_norm_w': 1.0 + nrm(ks[1], (L, D_MODEL), 0.05),
        'w_in': nrm(ks[2], (L, D_MODEL, IN_DIM), D_MODEL ** -0.5),
        'conv_w': nrm(ks[3], (L, CONV_K, CONV_DIM), CONV_K ** -0.5),
        'conv_b': nrm(ks[5], (L, CONV_DIM), 0.02),
        'dt_bias': dt + jnp.log(-jnp.expm1(-dt)),
        'a_log': jnp.log(jax.random.uniform(ks[6], (L, SSM_HEADS), f32, 1.0, 16.0)),
        'd_skip': 1.0 + nrm(ks[7], (L, SSM_HEADS), 0.05),
        'ssm_norm_w': 1.0 + nrm(ks[8], (L, D_INNER), 0.05),
        'cmp_pos_k': nrm(ks[9], (L, CMP_BLOCK, NSA_HEAD_DIM), 0.1),
        'cmp_w1_k': nrm(ks[10], (L, CMP_BLOCK * NSA_HEAD_DIM, CMP_HIDDEN), (CMP_BLOCK * NSA_HEAD_DIM) ** -0.5),
        'cmp_w2_k': nrm(ks[11], (L, CMP_HIDDEN, NSA_HEAD_DIM), CMP_HIDDEN ** -0.5),
        'cmp_pos_v': nrm(ks[12], (L, CMP_BLOCK, NSA_HEAD_DIM), 0.1),
        'cmp_w1_v': nrm(ks[13], (L, CMP_BLOCK * NSA_HEAD_DIM, CMP_HIDDEN), (CMP_BLOCK * NSA_HEAD_DIM) ** -0.5),
        'cmp_w2_v': nrm(ks[14], (L, CMP_HIDDEN, NSA_HEAD_DIM), CMP_HIDDEN ** -0.5),
        'w_branch_ssm': nrm(ks[15], (L, D_INNER, D_MODEL), D_INNER ** -0.5),
        'w_branch_nsa': nrm(ks[16], (L, NSA_WIDTH, D_MODEL), NSA_WIDTH ** -0.5),
        'w_out': nrm(ks[17], (L, D_MODEL, D_MODEL), D_MODEL ** -0.5),
        'ffn_norm_w': 1.0 + nrm(ks[18], (L, D_MODEL), 0.05),
        'router_w': nrm(ks[19], (L, D_MODEL, N_EXPERTS), D_MODEL ** -0.5),
        'router_b': nrm(ks[20], (L, N_EXPERTS), 0.01),
        'w_gate_up': nrm(ks[21], (L, N_EXPERTS, D_MODEL, 2 * D_EXPERT), D_MODEL ** -0.5),
        'b_gate_up': nrm(ks[22], (L, N_EXPERTS, 2 * D_EXPERT), 0.01),
        'w_down': nrm(ks[23], (L, N_EXPERTS, D_EXPERT, D_MODEL), D_EXPERT ** -0.5),
        'b_down': nrm(ks[24], (L, N_EXPERTS, D_MODEL), 0.01),
        'final_norm_w': 1.0 + nrm(ks[25], (D_MODEL,), 0.05),
    }

def reference(x, mix_norm_w, w_in, conv_w, conv_b, dt_bias, a_log, d_skip, ssm_norm_w,
              cmp_pos_k, cmp_w1_k, cmp_w2_k, cmp_pos_v, cmp_w1_v, cmp_w2_v,
              w_branch_ssm, w_branch_nsa, w_out, ffn_norm_w, router_w, router_b,
              w_gate_up, b_gate_up, w_down, b_down, final_norm_w):
    for l in range(DEPTH):
        h = rms_norm(x, mix_norm_w[l])
        proj = h @ w_in[l]
        (z, xbc, dt_raw, q, k_c, v_c, k_s, v_s, k_w, v_w,
         nsa_gate, merge_gate) = jnp.split(proj, IN_OFFSETS, axis=-1)
        y_ssm = mamba2_mixer(z, xbc, dt_raw, conv_w[l], conv_b[l], dt_bias[l], a_log[l],
                             d_skip[l], ssm_norm_w[l])
        y_nsa = nsa_mixer(q, k_c, v_c, k_s, v_s, k_w, v_w, nsa_gate,
                          cmp_pos_k[l], cmp_w1_k[l], cmp_w2_k[l], cmp_pos_v[l], cmp_w1_v[l], cmp_w2_v[l])
        g_ssm, g_nsa = jnp.split(jax.nn.sigmoid(merge_gate), 2, axis=-1)
        merged = g_ssm * (y_ssm @ w_branch_ssm[l]) + g_nsa * (y_nsa @ w_branch_nsa[l])
        x = x + merged @ w_out[l]
        h = rms_norm(x, ffn_norm_w[l])
        x = x + moe_ffn(h, router_w[l], router_b[l], w_gate_up[l], b_gate_up[l], w_down[l], b_down[l])
    return rms_norm(x, final_norm_w)


_drawn_inputs = setup_inputs


def setup_inputs(seed=0):
    import zlib

    import numpy as np

    out = dict(_drawn_inputs(seed))
    spreads = {}
    factors = {'cmp_pos_k': 13.275, 'b_gate_up': 8.0, 'b_down': 8.0}
    for name, (base, spread) in spreads.items():
        noise = np.random.default_rng([zlib.crc32(name.encode()), seed]).standard_normal(out[name].shape)
        drawn = base * np.exp(spread * noise) if base else spread * noise
        out[name] = jnp.asarray(drawn.astype(out[name].dtype))
    for name, factor in factors.items():
        out[name] = (out[name] * factor).astype(out[name].dtype)
    return out
```

```python
from contextlib import ExitStack

import concourse.bass as bass
from concourse import mybir

F32 = mybir.dt.float32
I32 = mybir.dt.int32
U32 = mybir.dt.uint32
ALU = mybir.AluOpType
ACT = mybir.ActivationFunctionType
AX = mybir.AxisListType

P = 128
D = 1024
SEQ = 256
T = SEQ // P
KT = D // P
HEADS = 16
GROUPS = 4
REP = HEADS // GROUPS
DH = 64
CMP_BLOCK, CMP_STRIDE = 32, 16
NCMP = (SEQ - CMP_BLOCK) // CMP_STRIDE + 1
EXPERTS = 32
TOPK = 4
EPS = 1e-5
NEG = -1e30
CAP = 64
RING = 12
SLOT = 2048

OFF_Z, OFF_XBC, OFF_DT, OFF_Q = 0, 1024, 3072, 3088
OFF_KC, OFF_VC, OFF_KS, OFF_VS, OFF_KW, OFF_VW = 4112, 4368, 4624, 4880, 5136, 5392
OFF_NG, OFF_MG = 5648, 5696

UNITS = ([("xbc", m) for m in range(8)] + [("small", 0), ("kc", 0), ("vc", 0), ("w1k", 0), ("w1v", 0),
         ("ks", 0), ("kw", 0), ("vs", 0), ("vw", 0)] + [("q", m) for m in range(4)]
         + [("z", m) for m in range(4)] + [("mg", m) for m in range(8)]
         + [("bs", m) for m in range(4)] + [("bn", m) for m in range(4)] + [("wo", m) for m in range(4)])
NU = len(UNITS)


def token_order():
    u = {x: n for n, x in enumerate(UNITS)}
    out = []

    def unit(kind, m=0):
        out.append(("P", u[(kind, m)]))

    for m in range(8):
        unit("xbc", m)
        if m >= 1:
            out.append(("F", m - 1))
    unit("small")
    out += [("F", 7), ("XD", 0), ("DT", 0)]
    unit("kc")
    out += [("S1", 0)]
    unit("vc")
    out += [("XT", 0)]
    out += [("HID", 0), ("XT", 1), ("HID", 1), ("BT", 0)]
    unit("ks")
    out += [("K2", 0), ("A", 0), ("XT", 2)]
    unit("kw")
    out += [("A", 1), ("XT", 3)]
    unit("vs")
    out += [("Y", 0), ("A", 2), ("ST", 0)]
    unit("vw")
    out += [("Y", 1), ("A", 3), ("ST", 1)]
    for m in range(4):
        unit("q", m)
        out += [("Y", m + 2), ("A", m + 4)]
    unit("z", 0)
    out += [("Y", 6)]
    unit("z", 1)
    out += [("Y", 7), ("V2", 0), ("CS", 0), ("GY", 0)]
    unit("z", 2)
    out += [("CP", 0), ("GY", 1), ("GN", 0)]
    unit("z", 3)
    out += [("GY", 2), ("GN", 1)]
    k = 0
    for m in range(8):
        unit("mg", m)
        if m == 0:
            out += [("GY", 3), ("GN", 2), ("SC", 0), ("GN", 3)]
        n = 2
        for _ in range(n):
            out += attn_step(k)
            k += 1
    for m in range(4):
        unit("bs", m)
        if k < 17:
            out += attn_step(k)
            k += 1
    assert k >= 17
    for m in range(4):
        unit("bn", m)
        if m >= 1:
            out.append(("MT", m - 1))
    out.append(("MT", 3))
    for m in range(4):
        unit("wo", m)
    return out


def attn_step(k):
    out = []
    if k + 1 < 16:
        out.append(("SC", k + 1))
    if k < 16:
        out.append(("RW", k))
    if k >= 1:
        out.append(("PV", k - 1))
    if k < 16:
        out.append(("PT", k))
    return out


TOKENS = token_order()


def hybrid_block(nc, x, mix_norm_w, w_in, conv_w, conv_b, dt_bias, a_log, d_skip, ssm_norm_w,
                 cmp_pos_k, cmp_w1_k, cmp_w2_k, cmp_pos_v, cmp_w1_v, cmp_w2_v,
                 w_branch_ssm, w_branch_nsa, w_out, ffn_norm_w, router_w, router_b,
                 w_gate_up, b_gate_up, w_down, b_down, final_norm_w, out):
    with ExitStack() as ctx:
        def sb(name, shape, dt=F32):
            return ctx.enter_context(nc.sbuf_tensor(name, shape, dt))

        def sem(name):
            return ctx.enter_context(nc.semaphore(name))

        def part(t, off, *dims):
            n = 1
            for d in dims:
                n *= d
            names = "abcde"[:len(dims)]
            rank = len(t.shape) - 1
            flat = t[:] if rank == 1 else t[:].rearrange(
                "p " + " ".join("wxyz"[:rank]) + " -> p (" + " ".join("wxyz"[:rank]) + ")")
            v = flat[:, off:off + n]
            if len(dims) == 1:
                return v
            return v.rearrange("p (" + " ".join(names) + ") -> p " + " ".join(names),
                               **{c: d for c, d in zip(names[1:], dims[1:])})

        ring = sb("ring", [P, RING, SLOT])
        X = sb("X", [P, T, D])
        HT = sb("HT", [P, KT, SEQ])
        XC = sb("XC", [P, 16, SEQ])
        YV = sb("YV", [P, 8, SEQ])
        ZS = sb("ZS", [P, 8, SEQ])
        XDT = sb("XDT", [P, 3 * D])
        ST = sb("ST", [P, D])
        E = sb("E", [P, 2, 512])
        GM = sb("GM", [P, 2, P])
        EC = sb("EC", [P, 2, 512])
        CTE = sb("CTE", [P, 2, 512])
        TH = sb("TH", [P, 2, 512])
        QT = sb("QT", [P, 8, SEQ])
        KD = sb("KD", [P, 2, GROUPS, SEQ])
        VT = sb("VT", [P, 2, T, 256])
        PR = sb("PR", [P, P])
        PC = sb("PC", [P, P])
        PH = sb("PH", [P, 96])
        IDN = sb("IDN", [P, P])
        UPP = sb("UPP", [P, P])
        UST = sb("UST", [P, P])
        ONE = sb("ONE", [P, P])
        CM = sb("CM", [P, 256])
        CMC = sb("CMC", [P, T, 16])
        IOI = sb("IOI", [P, P], I32)
        IOT = sb("IOT", [P, P])
        EIO = sb("EIO", [P, EXPERTS])
        TH3 = sb("TH3", [P, 3])
        HM = sb("HM", [P, 8])
        W2K = sb("W2K", [P, 2, DH])
        W2V = sb("W2V", [P, DH])
        DTB = sb("DTB", [P, HEADS])
        ALG = sb("ALG", [P, HEADS])
        DCOL = sb("DCOL", [P, 8])
        RB = sb("RB", [P, EXPERTS])
        SM = sb("SM", [P, T, 64])
        DT = sb("DT", [P, 8, T, HEADS])
        ADT = sb("ADT", [P, T, HEADS])
        CS = sb("CS", [P, T, HEADS])
        DE = sb("DE", [P, HEADS])
        NG = sb("NG", [P, T, 48])
        ss = sb("ss", [P, 8])
        HID = sb("HID", [P, 2, GROUPS, 16])
        BDK = sb("BDK", [P, GROUPS, 2, 16])
        AMX = sb("AMX", [P, 2, 4, 4])

        VBD = part(ST, 0, 2, 8, DH)
        PCS = part(E, 0, T, HEADS, 16)
        PCT = part(E, 512, T, 2, P)
        BTK = part(ZS, 0, GROUPS, P)
        HIDT = part(EC, 0, 2, 5, 64)
        CST = part(GM, 0, 6, T, HEADS)
        RW_ = part(GM, 0, KT, EXPERTS)
        HVR = part(CTE, 0, 2, 2, REP, 16)
        KC2 = part(ZS, 0, GROUPS, SEQ)
        VC2 = part(ZS, 1024, GROUPS, SEQ)
        HN = part(ZS, 0, T, D)
        OT = part(ZS, 0, 8, SEQ)
        GA = part(XC, 0, T, 2048)
        SQ = EC
        SP = part(XDT, 0, 2, 2, 2, 256)
        PTS = part(XDT, 2048, 2, 512)
        MG = part(QT, 0, T, D)
        H2 = part(XC, 0, T, D)
        H2T = part(XC, 2048, KT, SEQ)
        WFF = part(YV, 0, D)
        WFN = part(YV, 1024, D)
        BGU = part(KD, 0, 2048)
        BDN = part(VT, 0, D)
        XTS = part(ZS, 0, KT, 2, CAP)
        SGA = part(ZS, 1024, 512)
        GBU = part(ZS, 1536, 512)
        LBU = part(HT, 0, 512)
        ABU = part(HT, 512, 512)
        ATS = part(HT, 1024, 4, P)
        YSB = part(HT, 1536, 512)
        CTS = part(QT, 0, 2, T, P)
        SPR = part(QT, 512, T, 2, CAP)
        CPR = part(QT, 768, T, 2, P)
        OHE = part(QT, 1280, 2, CAP)
        C2 = part(QT, 1408, 2, T, 2)
        SLT = part(QT, 1424, T, EXPERTS)
        CW = part(QT, 1488, T, EXPERTS)
        MSK = part(QT, 1552, T, EXPERTS)
        LG = part(QT, 1616, T, EXPERTS)
        MX8 = part(QT, 1680, T, 8)
        CWT = part(QT, 1712, T, P)
        OH4 = part(XDT, 0, T, TOPK, EXPERTS)
        OW4 = part(XDT, 256, T, TOPK, EXPERTS)
        RT = part(XDT, 512, 16, T, 8)
        RJ = part(XDT, 1024, T, D)
        IX8 = sb("IX8", [P, T, 8], U32)
        RCI = sb("RCI", [P, 1], I32)

        psum = ctx.enter_context(nc.psum_tensor("psum", [P, 8, 512], F32))

        ring_full = [sem(f"ring_full{i}") for i in range(RING)]
        unit_done = sem("unit_done")
        proj_free = [sem(f"proj_free{i}") for i in range(3)]
        (x_in, rows_in, small_in, late_in, const_done, dve_own, act_own, pool_own, hn_ready, ht_full,
         ht_act, ht_dve, par_full, par_ready, hv_done, th_ready, th_used, xd_done, sm_ready, dt_e, dt_w,
         dt_l, adt_ready, s1_full, cs_ready, de_ready, xt_full, xdt_ready, bt_ready, xde_ready, a_full,
         csb_read, gm_ready, e_exp, ecs_done, m_done, cte_done, y_full, y_read, st_full, st_ready,
         kv_act, kv_dve, hid_full, hid_t3, hid_th, hid_ready, hvr_ready, k2_full, k2_ready, v2_full, v2_ready,
         q_ready, v_ready, z_used, gy_ready, sq_ready, gn_full, rb_ready, yn_ready, ga_ready, cs_full,
         cs_sub, cs_exp, cp_ready, cp_full, cp_read, sc_full, nm_ready, ex_done, w_ready, p_ready,
         pt_full, pt_act, pt_dve, pv_full, pv_read, mg_ready, mt_full, mt_ready, x2_ready, ss_ready,
         sq_root, h2_ready, h2t_full, h2t_act, h2t_dve, rt_full, lg_ready, mx_ready, te_ready, msk_ready,
         rk_full, slot_ready, round_ready, acc_ready, cwt_full, bd_full, final_in, norm_ready, stored,
         prep_done, xte_full, xte_ready, gu_read, ct_full, ct_ready, y_ready, o_full, o_read, g_ready,
         sig_ready, act_ready, at_full, at_ready, zero_ready) = [sem(n) for n in (
            "x_in rows_in small_in late_in const_done dve_own act_own pool_own hn_ready ht_full "
            "ht_act ht_dve par_full par_ready hv_done th_ready th_used xd_done sm_ready dt_e dt_w "
            "dt_l adt_ready s1_full cs_ready de_ready xt_full xdt_ready bt_ready xde_ready a_full "
            "csb_read gm_ready e_exp ecs_done m_done cte_done y_full y_read st_full st_ready "
            "kv_act kv_dve hid_full hid_t3 hid_th hid_ready hvr_ready k2_full k2_ready v2_full v2_ready "
            "q_ready v_ready z_used gy_ready sq_ready gn_full rb_ready yn_ready ga_ready cs_full "
            "cs_sub cs_exp cp_ready cp_full cp_read sc_full nm_ready ex_done w_ready p_ready "
            "pt_full pt_act pt_dve pv_full pv_read mg_ready mt_full mt_ready x2_ready ss_ready "
            "sq_root h2_ready h2t_full h2t_act h2t_dve rt_full lg_ready mx_ready te_ready msk_ready "
            "rk_full slot_ready round_ready acc_ready cwt_full bd_full final_in norm_ready stored "
            "prep_done xte_full xte_ready gu_read ct_full ct_ready y_ready o_full o_read g_ready "
            "sig_ready act_ready at_full at_ready zero_ready").split()]

        loads = {u: 2 if UNITS[u][0] == "small" else 1 for u in range(NU)}
        full_at, slot_total = {}, [0] * RING
        for u in range(NU):
            slot_total[u % RING] += 16 * loads[u]
            full_at[u] = slot_total[u % RING]
        bank_of, freed, uses = {}, {}, [0] * 3
        n = 0
        for u, (kind, _) in enumerate(UNITS):
            if kind in ("w1k", "w1v"):
                continue
            bank_of[u], freed[u] = n % 3, uses[n % 3]
            uses[n % 3] += 1
            n += 1

        def slot_view(u, *dims):
            return part(ring, (u % RING) * SLOT, *dims)

        def bank(b, *dims, off=0):
            n = 1
            for d in dims:
                n *= d
            v = psum[:, b, off:off + n]
            if len(dims) == 1:
                return v
            names = "abcde"[:len(dims)]
            return v.rearrange("p (" + " ".join(names) + ") -> p " + " ".join(names),
                               **{c: d for c, d in zip(names[1:], dims[1:])})

        at_unit = {x: n for n, x in enumerate(UNITS)}

        def taken(eng, kind, m=0):
            u = at_unit[(kind, m)]
            eng.wait_ge(proj_free[bank_of[u]], freed[u] + 1)

        class Own:

            def __init__(self, eng, s):
                self.eng, self.s, self.n = eng, s, 0

            def mark(self, ins):
                self.n += 1
                ins.then_inc(self.s, 1)

            def settle(self):
                self.eng.wait_ge(self.s, self.n)

        EX2 = EXPERTS // 2

        def rounds(eng):
            eng.wait_ge(round_ready, 1)
            r = eng.value_load(RCI[0:1, 0:1], min_val=1, max_val=4)
            return r

        block = ctx.enter_context(nc.Block())

        @block.sync
        def _(sp):
            sp.dma_start(X[:], x[0].rearrange("(t p) d -> p t d", p=P)).then_inc(x_in, 16)

            def w_cols(w, c0, n):
                return w[0, :, c0:c0 + n].rearrange("(k p) n -> p k n", p=P)

            first = {"z": OFF_Z, "xbc": OFF_XBC, "q": OFF_Q, "kc": OFF_KC, "vc": OFF_VC, "ks": OFF_KS,
                     "vs": OFF_VS, "kw": OFF_KW, "vw": OFF_VW, "mg": OFF_MG}
            for u, (kind, m) in enumerate(UNITS):
                if u >= RING:
                    sp.wait_ge(unit_done, u - RING + 1)
                full = ring_full[u % RING]
                if kind == "small":
                    v = slot_view(u, KT, 64)
                    sp.dma_start(v[:, :, 0:16], w_cols(w_in, OFF_DT, 16)).then_inc(full, 16)
                    sp.dma_start(v[:, :, 16:64], w_cols(w_in, OFF_NG, 48)).then_inc(full, 16)
                elif kind in ("w1k", "w1v"):
                    w1 = cmp_w1_k if kind == "w1k" else cmp_w1_v
                    sp.dma_start(slot_view(u, 16, P), w1[0].rearrange("(k p) n -> p k n", p=P)).then_inc(full, 16)
                else:
                    w = {"bs": w_branch_ssm, "bn": w_branch_nsa, "wo": w_out}.get(kind, w_in)
                    sp.dma_start(slot_view(u, KT, 256), w_cols(w, first.get(kind, 0) + 256 * m, 256)
                                 ).then_inc(full, 16)

            def expert(e, n):
                for j in range(RING):
                    sp.wait_ge(unit_done, n * RING + (NU + j - RING + 1))
                    s = (NU + j) % RING
                    if j < 8:
                        src = w_gate_up[0, e, P * j:P * j + P, :].rearrange("(k p) n -> p k n", p=P)
                        dst = part(ring, s * SLOT, 1, 2048)
                    else:
                        src = w_down[0, e, 256 * (j - 8):256 * (j - 8) + 256, :].rearrange("(k p) n -> p k n", p=P)
                        dst = part(ring, s * SLOT, 2, 1024)
                    sp.dma_start(dst, src).then_inc(ring_full[s], 16)

            expert(0, 0)
            r = rounds(sp)
            with sp.Fori(1, r * EXPERTS) as n:
                expert(n % EXPERTS, n)
            sp.wait_ge(norm_ready, 1)
            sp.dma_start(out[0].rearrange("(t p) d -> p t d", p=P), RJ).then_inc(stored, 16)
            sp.wait_ge(stored, 16)

        @block.gpsimd
        def _(pool):
            own = Own(pool, pool_own)
            g = nc.gpsimd
            own.mark(g.memset(IDN[:], 0.0))
            own.mark(g.memset(UPP[:], 1.0))
            own.mark(g.memset(UST[:], 1.0))
            own.mark(g.memset(CM[:], 0.0))
            own.mark(g.memset(CMC[:], 0.0))
            own.mark(g.memset(HM[:], 0.5))
            own.mark(g.memset(ONE[:], 1.0))
            own.settle()
            own.mark(g.affine_select(out=IDN[:], in_=IDN[:], pattern=[[-1, P]], compare_op=ALU.not_equal,
                                     fill=1.0, base=0, channel_multiplier=1))
            own.settle()
            pool.sem_inc(const_done, 1)
            own.mark(g.affine_select(out=UPP[:], in_=UPP[:], pattern=[[1, P]], compare_op=ALU.is_ge,
                                     fill=0.0, base=0, channel_multiplier=-1))
            own.mark(g.affine_select(out=UST[:], in_=UST[:], pattern=[[1, P]], compare_op=ALU.is_gt,
                                     fill=0.0, base=0, channel_multiplier=-1))
            own.mark(g.affine_select(out=CM[:, P:256], in_=CM[:, P:256], pattern=[[-1, P]],
                                     compare_op=ALU.is_ge, fill=NEG, base=0, channel_multiplier=1))
            for t in range(T):
                own.mark(g.affine_select(out=CMC[:, t], in_=CMC[:, t], pattern=[[-CMP_STRIDE, 16]],
                                         compare_op=ALU.is_ge, fill=NEG, base=P * t - CMP_BLOCK + 1,
                                         channel_multiplier=1))
            own.mark(g.affine_select(out=HM[:], in_=HM[:], pattern=[[-16, 8]], compare_op=ALU.is_ge,
                                     fill=0.0, base=0, channel_multiplier=1))
            own.settle()
            own.mark(g.affine_select(out=HM[:], in_=HM[:], pattern=[[16, 8]], compare_op=ALU.is_ge,
                                     fill=0.0, base=15, channel_multiplier=-1))
            own.mark(g.iota(IOI[:], pattern=[[0, 2], [1, CAP]], base=0, channel_multiplier=0))
            own.settle()
            own.mark(g.tensor_copy(IOT[:], IOI[:]))
            own.settle()
            own.mark(g.iota(IOI[:, 0:EXPERTS], pattern=[[1, EXPERTS]], base=0, channel_multiplier=0))
            own.mark(g.iota(IOI[:, 64:67], pattern=[[CAP, 3]], base=CAP, channel_multiplier=0))
            own.settle()
            own.mark(g.tensor_copy(EIO[:], IOI[:, 0:EXPERTS]))
            own.mark(g.tensor_copy(TH3[:], IOI[:, 64:67]))
            own.mark(g.memset(HID[:], 0.0))
            own.mark(g.memset(BDK[:], 0.0))
            own.settle()
            pool.sem_inc(const_done, 1)

            for kind, k in TOKENS:
                if kind == "XD":
                    pool.wait_ge(th_used, 4)
                    pool.wait_ge(small_in, 16 * 8)
                    for j in range(8):
                        ins = g.tensor_scalar(YV[:, j], XC[:, j], DCOL[:, j:j + 1], None, ALU.mult)
                        if j == 7:
                            own.mark(ins)
                    own.settle()
                    pool.sem_inc(xd_done, 1)
                elif kind == "XT" and k < 2:
                    if k == 0:
                        pool.wait_ge(de_ready, 1)
                    pool.wait_ge(xdt_ready, k + 1)
                    g.tensor_tensor(part(XDT, 2048 + 512 * k, 8, DH), part(XDT, 512 * k, 8, DH),
                                    DE[:, 8 * k:8 * k + 8].unsqueeze(2).to_broadcast([P, 8, DH]),
                                    ALU.mult).then_inc(xde_ready, 1)
                elif kind == "A":
                    c, gr, b = k // 4, k % 4, k % 2
                    pool.wait_ge(e_exp, k + 1)
                    pool.wait_ge(gm_ready, k + 1)
                    ev = E[:, b].rearrange("p (r l) -> p r l", r=REP)
                    g.tensor_tensor(ev, ev, GM[:, b].unsqueeze(1).to_broadcast([P, REP, P]),
                                    ALU.mult).then_inc(m_done, 1)
                    if c == 1:
                        pool.wait_ge(ecs_done, k - 3)
                        if k >= 6:
                            pool.wait_ge(y_full, k - 1)
                        g.tensor_tensor(CTE[:, b].rearrange("p (r l) -> p r l", r=REP),
                                        EC[:, b].rearrange("p (r l) -> p r l", r=REP),
                                        XC[:, 12 + gr, P:2 * P].unsqueeze(1).to_broadcast([P, REP, P]),
                                        ALU.mult).then_inc(cte_done, 1)
                elif kind == "RW":
                    b, nk = k % 2, P * (k // 8 + 1)
                    pool.wait_ge(w_ready, k + 1)
                    v = SP[:, b, :, :, 0:nk]
                    g.tensor_tensor(v, v, AMX[:, b, 3].rearrange("p (h y) -> p h y", h=2).unsqueeze(3)
                                    .to_broadcast([P, 2, 2, nk]), ALU.mult).then_inc(p_ready, 1)
            pool.wait_ge(slot_ready, 1)
            own.mark(g.memset(YSB, 0.0))
            own.mark(g.memset(CTS[:, 1], 0.0))
            own.settle()
            pool.sem_inc(zero_ready, 1)

        @block.tensor
        def _(pe):
            mm = nc.tensor.matmul

            def tr(o, i):
                return nc.tensor.transpose(o, i, IDN[:, :])

            pe.wait_ge(const_done, 1)
            pe.wait_ge(rows_in, 16 * 6)
            tr(bank(4, P), PR[:]).then_inc(par_full, 1)
            for b in range(4):
                for kk in range(2):
                    for t in range(T):
                        if b == 0 and kk == 0:
                            pe.wait_ge(hn_ready, t + 1)
                        ins = tr(bank(b, 2, T, P)[:, kk, t], HN[:, t, P * (2 * b + kk):P * (2 * b + kk + 1)])
                ins.then_inc(ht_full, 1)
            pe.wait_ge(const_done, 2)

            def unit(u):
                kind, m = UNITS[u]
                if kind == "xbc" and m == 0:
                    pe.wait_ge(ht_act, 2)
                    pe.wait_ge(ht_dve, 2)
                pe.wait_ge(ring_full[u % RING], full_at[u])
                b = bank_of[u]
                if freed[u]:
                    pe.wait_ge(proj_free[b], freed[u])
                if kind == "bs" and m == 0:
                    pe.wait_ge(yn_ready, 4)
                if kind == "bn" and m == 0:
                    pe.wait_ge(pv_read, 16)
                if kind == "wo" and m == 0:
                    pe.wait_ge(mt_ready, 4)
                src = {"bs": YV[:], "bn": OT}.get(kind, HT[:])
                if kind in ("xbc", "kc", "vc", "ks", "kw", "q", "z"):
                    w = slot_view(u, KT, 256)
                    for f in range(2):
                        for k in range(KT):
                            ins = mm(bank(b, 2, SEQ)[:, f], w[:, k, P * f:P * f + P], src[:, k, :],
                                     start=(k == 0), stop=(k == KT - 1))
                else:
                    nco = 64 if kind == "small" else 256
                    w = slot_view(u, KT, nco)
                    for t in range(T):
                        for k in range(KT):
                            ins = mm(bank(b, 2, nco)[:, t], src[:, k, P * t:P * t + P], w[:, k, :],
                                     start=(k == 0), stop=(k == KT - 1))
                ins.then_inc(unit_done, 1)

            for kind, k in TOKENS:
                if kind == "P":
                    unit(k)
                elif kind == "S1":
                    pe.wait_ge(adt_ready, 1)
                    pe.wait_ge(par_ready, 1)
                    mm(bank(4, 16), UPP[:], ADT[:, 0], start=True, stop=True)
                    mm(bank(4, 16, off=16), UPP[:], ADT[:, 1], start=True, stop=True)
                    mm(bank(4, 16, off=32), ONE[:], ADT[:, 0], start=True, stop=True).then_inc(s1_full, 1)
                elif kind == "XT":
                    c, half = k // 2, k % 2
                    if k in (1, 3):
                        pe.wait_ge(xdt_ready, k)
                    if k == 2:
                        pe.wait_ge(bt_ready, 1)
                    for j in range(4):
                        ins = tr(bank(5, 4, P)[:, j], XC[:, 4 * half + j, P * c:P * c + P])
                    ins.then_inc(xt_full, 1)
                elif kind == "BT":
                    pe.wait_ge(xdt_ready, 2)
                    for j in range(4):
                        ins = tr(bank(5, 4, P)[:, j], XC[:, 8 + j, 0:P])
                    ins.then_inc(xt_full, 1)
                elif kind == "HID":
                    u = 11 + k
                    if k == 0:
                        taken(pe, "kc")
                        taken(pe, "vc")
                    pe.wait_ge(ring_full[u % RING], full_at[u])
                    w1 = slot_view(u, 16, P)
                    src = KC2 if k == 0 else VC2
                    o = bank(7 - k, GROUPS, NCMP)
                    for j in range(16):
                        span = CMP_STRIDE * (NCMP - 1) + 1
                        mm(o, w1[:, j], src[:, :, 2 * j:2 * j + span:CMP_STRIDE], start=(j == 0), stop=False)
                        ins = mm(o, w1[:, j], PC[:, 96 + 16 * k + j:97 + 16 * k + j].unsqueeze(1)
                                 .to_broadcast([P, GROUPS, NCMP]), start=False, stop=(j == 15))
                    ins.then_inc(unit_done, 1)
                elif kind == "K2":
                    pe.wait_ge(hid_ready, 1)
                    mm(bank(7, 64, off=128), W2K[:].rearrange("p a b -> p (a b)"),
                       HID[:, 0].rearrange("p a b -> p (a b)"), start=True, stop=True).then_inc(k2_full, 1)
                elif kind == "V2":
                    pe.wait_ge(hvr_ready, 1)
                    pe.wait_ge(y_read, 8)
                    for hb in range(2):
                        lhs = HVR[:, hb].rearrange("p g r c -> p (g r c)")
                        ins = mm(bank(6, 64, off=128 + 64 * hb), lhs, W2V[:], start=True, stop=True)
                    ins.then_inc(v2_full, 1)
                elif kind == "A":
                    c, gr = k // 4, k % 4
                    if k == 0:
                        pe.wait_ge(cs_ready, 1)
                    else:
                        pe.wait_ge(csb_read, k)
                        pe.wait_ge(gm_ready, k)
                    if k >= 5:
                        pe.wait_ge(ecs_done, k - 4)
                    for r in range(REP):
                        mm(bank(3, REP, P)[:, r], ADT[:, c, REP * gr + r:REP * gr + r + 1].to_broadcast([P, P]),
                           UPP[:], start=True, stop=True)
                    mm(bank(4, P), XC[:, 8 + gr, P * c:P * c + P], XC[:, 12 + gr, P * c:P * c + P],
                       start=True, stop=True).then_inc(a_full, 1)
                elif kind == "ST":
                    pe.wait_ge(xde_ready, k + 1)
                    if k == 0:
                        pe.wait_ge(bt_ready, 1)
                        pe.wait_ge(k2_ready, 1)
                    else:
                        pe.wait_ge(st_ready, 1)
                    for j in range(2):
                        gr = 2 * k + j
                        ins = mm(bank(7, 2, 256)[:, j], BTK[:, gr], part(XDT, 2048 + 256 * gr, 256),
                                 start=True, stop=True)
                    ins.then_inc(st_full, 1)
                elif kind == "Y":
                    c, gr, b = k // 4, k % 4, k % 2
                    pe.wait_ge(m_done, k + 1)
                    if c == 0:
                        pe.wait_ge(xdt_ready, 2)
                    else:
                        pe.wait_ge(xdt_ready, 4)
                        pe.wait_ge(cte_done, k - 3)
                        pe.wait_ge(st_ready, 2)
                    if k == 0:
                        pe.wait_ge(hid_ready, 2)
                    else:
                        pe.wait_ge(y_read, k)
                    for jj in range(2):
                        for hh in range(2):
                            r = 2 * jj + hh
                            h = REP * gr + r
                            o = psum[64 * hh:64 * hh + 64, 6, P * jj:P * jj + P]
                            ins = mm(o, part(XDT, D * c + DH * h, DH), E[:, b, P * r:P * r + P],
                                     start=True, stop=(c == 0))
                            if c == 1:
                                ins = mm(o, ST[:, DH * h:DH * h + DH], CTE[:, b, P * r:P * r + P],
                                         start=False, stop=True)
                    ins.then_inc(y_full, 1)
                elif kind == "GN":
                    pe.wait_ge(sq_ready, k + 1)
                    if k == 0:
                        pe.wait_ge(v2_ready, 1)
                    else:
                        pe.wait_ge(rb_ready, k)
                    mm(bank(6, SEQ), ONE[:], SQ[:, k % 2, 0:SEQ], start=True, stop=False)
                    mm(bank(6, SEQ), ONE[:], SQ[:, k % 2, SEQ:2 * SEQ], start=False, stop=True
                       ).then_inc(gn_full, 1)
                elif kind == "CS":
                    for m in range(4):
                        taken(pe, "q", m)
                    pe.wait_ge(k2_ready, 1)
                    pe.wait_ge(xdt_ready, 4)
                    for t in range(T):
                        for j in range(8):
                            ins = mm(bank(5, 32, off=256 * t + 32 * j), QT[:, j, P * t:P * t + P],
                                     BDK[:, j // 2].rearrange("p a b -> p (a b)"), start=True, stop=True)
                    ins.then_inc(cs_full, 1)
                elif kind == "CP":
                    pe.wait_ge(cp_ready, 1)
                    for t in range(T):
                        for hb in range(2):
                            ins = tr(bank(5, T, 2, P)[:, t, hb], PCS[:, t, 8 * hb:8 * hb + 8]
                                     .rearrange("p a b -> p (a b)"))
                    ins.then_inc(cp_full, 1)
                elif kind == "SC":
                    t, j = k // 8, k % 8
                    if k == 0:
                        pe.wait_ge(gm_ready, 8)
                        pe.wait_ge(ecs_done, 4)
                        pe.wait_ge(csb_read, 8)
                        taken(pe, "ks")
                        taken(pe, "kw")
                    else:
                        pe.wait_ge(nm_ready, k)
                    nk = P * (t + 1)
                    for y in range(2):
                        for hh in range(2):
                            s = slice(64 * hh, 64 * hh + 64)
                            ins = mm(psum[:, 3 + hh, 256 * y:256 * y + nk], QT[s, j, P * t:P * t + P],
                                     KD[s, y, j // 2, 0:nk], start=True, stop=True)
                    ins.then_inc(sc_full, 1)
                elif kind == "PT":
                    t = k // 8
                    pe.wait_ge(p_ready, k + 1)
                    if k == 0:
                        pe.wait_ge(cp_read, 1)
                        pe.wait_ge(rb_ready, 4)
                    else:
                        pe.wait_ge(pt_act, k)
                        pe.wait_ge(pt_dve, k)
                    for hh in range(2):
                        for y in range(2):
                            for bl in range(t + 1):
                                ins = tr(bank(5 + hh, P, off=P * (y * (t + 1) + bl)),
                                         SP[:, k % 2, hh, y, P * bl:P * bl + P])
                    ins.then_inc(pt_full, 1)
                elif kind == "PV":
                    t, j = k // 8, k % 8
                    if k == 0:
                        taken(pe, "vs")
                        taken(pe, "vw")
                        pe.wait_ge(v2_ready, 1)
                        pe.wait_ge(st_ready, 2)
                        pe.wait_ge(gy_ready, 4)
                    else:
                        pe.wait_ge(pv_read, k)
                    pe.wait_ge(pt_act, k + 1)
                    pe.wait_ge(pt_dve, k + 1)
                    mm(bank(7, P), VBD[:, j // 4, 2 * (j % 4):2 * (j % 4) + 2].rearrange("p a b -> p (a b)"),
                       PCT[:, t, j // 4], start=True, stop=False, skip_group_check=True)
                    for hh in range(2):
                        for y in range(2):
                            for bl in range(t + 1):
                                last = y == 1 and bl == t
                                ins = mm(psum[64 * hh:64 * hh + 64, 7, 0:P],
                                         VT[:, y, bl, DH * (j // 2):DH * (j // 2) + DH],
                                         PTS[:, hh, P * (y * (t + 1) + bl):P * (y * (t + 1) + bl) + P],
                                         start=False, stop=last, skip_group_check=True)
                    ins.then_inc(pv_full, 1)
                elif kind == "MT":
                    pe.wait_ge(mg_ready, k + 1)
                    if k >= 2:
                        pe.wait_ge(mt_ready, k - 1)
                    for kk in range(2):
                        for t in range(T):
                            ins = tr(bank(3 + k % 2, 2, T, P)[:, kk, t],
                                     MG[:, t, P * (2 * k + kk):P * (2 * k + kk) + P])
                    ins.then_inc(mt_full, 1)

            pe.wait_ge(h2_ready, 2)
            for b in range(4):
                for kk in range(2):
                    for t in range(T):
                        ins = tr(bank(3 + b, 2, T, P)[:, kk, t], H2[:, t, P * (2 * b + kk):P * (2 * b + kk + 1)])
                ins.then_inc(h2t_full, 1)
            pe.wait_ge(h2t_act, 2)
            pe.wait_ge(h2t_dve, 2)
            pe.wait_ge(late_in, 16 * 5)
            for t in range(T):
                for k in range(KT):
                    ins = mm(bank(7, EXPERTS, off=EXPERTS * t), H2T[:, k, P * t:P * t + P], RW_[:, k, :],
                             start=(k == 0), stop=(k == KT - 1))
            ins.then_inc(rt_full, 1)
            pe.wait_ge(msk_ready, 1)
            mm(bank(3, EXPERTS), UST[:], MSK[:, 0], start=True, stop=True)
            mm(bank(3, EXPERTS, off=32), ONE[:], MSK[:, 0], start=True, stop=False)
            mm(bank(3, EXPERTS, off=32), UST[:], MSK[:, 1], start=False, stop=True)
            mm(bank(3, EXPERTS, off=64), ONE[:], MSK[:, 0], start=True, stop=False)
            mm(bank(3, EXPERTS, off=64), ONE[:], MSK[:, 1], start=False, stop=True).then_inc(rk_full, 1)
            for t in range(T):
                ins = tr(bank(4, T, P)[0:EXPERTS, t], CW[:, t])
            ins.then_inc(cwt_full, 1)
            pe.wait_ge(late_in, 16 * 5)
            pe.wait_ge(cwt_full, 2)
            for t in range(T):
                for h in range(2):
                    ins = mm(psum[:, 5 + h, :], CWT[0:EXPERTS, t], BDN[0:EXPERTS, 512 * h:512 * h + 512],
                             start=True, stop=True)
                ins.then_inc(bd_full, 1)
                pe.wait_ge(acc_ready, t + 1)

            def gather():
                for k in range(KT):
                    for t in range(T):
                        ins = mm(bank(5 + k // 4, P, off=P * (k % 4)), H2[:, t, P * k:P * k + P],
                                 SPR[:, t].rearrange("p a b -> p (a b)"), start=(t == 0), stop=(t == T - 1))
                ins.then_inc(xte_full, 1)

            def combine(n, s):
                for t in range(T):
                    pe.wait_ge(o_read, n * 2 + (t + 1))
                    for h in range(2):
                        r = slice(64 * h, 64 * h + 64)
                        ins = mm(psum[:, 3 + h, :], CTS[r, 1 - s, t], YSB[r, :], start=True, stop=True)
                    ins.then_inc(o_full, 1)

            pe.wait_ge(prep_done, 1)
            gather()
            pe.wait_ge(zero_ready, 1)
            r = rounds(pe)
            with pe.Fori(0, r * EX2) as i:
                for s in range(2):
                    n = i * 2 + s
                    if s == 0:
                        pe.wait_ge(xte_ready, i + 1)
                        pe.wait_ge(prep_done, i + 1)
                    pe.wait_ge(gu_read, n + 1)
                    for c in range(4):
                        mm(psum[64 * (c % 2):64 * (c % 2) + 64, c // 2, :], OHE[0:EXPERTS, s],
                           BGU[0:EXPERTS, 512 * c:512 * c + 512], start=True, stop=False)
                    for k in range(KT):
                        slot = (NU + k) % RING
                        pe.wait_ge(ring_full[slot], n * 16 + (slot_total[slot] + 16))
                        for c in range(4):
                            ins = mm(psum[64 * (c % 2):64 * (c % 2) + 64, c // 2, :], XTS[:, k, s],
                                     ring[:, slot, 512 * c:512 * c + 512], start=False, stop=(k == KT - 1))
                        ins.then_inc(unit_done, 1)
                    pe.wait_ge(at_ready, n + 1)
                    for t in range(T):
                        ins = tr(bank(7, T, P)[:, t], CPR[:, t, s])
                    ins.then_inc(ct_full, 1)
                    pe.wait_ge(y_ready, n + 1)
                    combine(n, s)
                    pe.wait_ge(act_ready, n + 1)
                    pe.wait_ge(ct_ready, n + 1)
                    for jb in range(4):
                        ins = tr(bank(7, 4, P)[:, jb], ABU[:, P * jb:P * jb + P])
                    ins.then_inc(at_full, 1)
                    if s == 1:
                        pe.wait_ge(prep_done, i + 2)
                        gather()
                    pe.wait_ge(at_ready, n + 2)
                    for k in range(KT):
                        slot = (NU + 8 + k // 2) % RING
                        if k % 2 == 0:
                            pe.wait_ge(ring_full[slot], n * 16 + (slot_total[slot] + 16))
                        q, hf = k // 4, (k // 2) % 2
                        lhs = ATS[:, 2 * q + k % 2, 64 * hf:64 * hf + 64]
                        for h in range(2):
                            ins = mm(psum[64 * h:64 * h + 64, 2, :], lhs,
                                     ring[:, slot, 1024 * (k % 2) + 512 * h:1024 * (k % 2) + 512 * h + 512],
                                     start=(k == 0), stop=(k == KT - 1))
                        if k % 2:
                            ins.then_inc(unit_done, 1)
            pe.wait_ge(y_ready, r * EXPERTS + 1)
            pe.wait_ge(ct_ready, r * EXPERTS)
            combine(r * EXPERTS, 0)

        @block.scalar
        def _(act):
            own = Own(act, act_own)
            a = nc.scalar.activation
            rows = [(mix_norm_w, 8), (ssm_norm_w, 8), (conv_b, 16), (conv_w, 64), (cmp_pos_k, 16),
                    (cmp_pos_v, 16)]
            at = 0
            for w, nrow in rows:
                flat = w[0] if len(w.shape) == 2 else w[0].rearrange("a b -> (a b)")
                act.dma_start(PR[at:at + nrow, :], flat.rearrange("(a b) -> a b", b=P)).then_inc(rows_in, 16)
                at += nrow
            act.dma_start(DTB[:], dt_bias[0].partition_broadcast(P)).then_inc(small_in, 16)
            act.dma_start(ALG[:], a_log[0].partition_broadcast(P)).then_inc(small_in, 16)
            dcol = d_skip[0].rearrange("(j two) -> two j", two=2)
            for hh in range(2):
                act.dma_start(DCOL[64 * hh:64 * hh + 64, :], dcol[hh].partition_broadcast(64),
                              allow_slow_non_contiguous=True).then_inc(small_in, 16)
            act.dma_start(W2K[:, 0], cmp_w2_k[0]).then_inc(small_in, 16)
            act.dma_start(W2K[:, 1], cmp_w2_k[0]).then_inc(small_in, 16)
            act.dma_start(W2V[:], cmp_w2_v[0]).then_inc(small_in, 16)
            act.dma_start(RB[:], router_b[0].partition_broadcast(P)).then_inc(small_in, 16)

            act.wait_ge(x_in, 16)
            for t in range(T):
                a(part(YV, D * t, D), X[:, t], ACT.Square, accum_out=ss[:, t:t + 1]).then_inc(ss_ready, 1)
            act.wait_ge(dve_own, 1)
            a(ss[:, 2:4], ss[:, 0:2], ACT.Sqrt).then_inc(sq_root, 1)
            act.wait_ge(par_ready, 1)
            for b in (0, 2):
                act.wait_ge(ht_full, b + 1)
                for kk in range(2):
                    ins = a(HT[:, 2 * b + kk], bank(b, 2, SEQ)[:, kk], ACT.Copy,
                            scale=PC[:, 2 * b + kk:2 * b + kk + 1])
                ins.then_inc(ht_act, 1)
            act.wait_ge(ht_dve, 2)

            n_th = 0
            for kind, k in TOKENS:
                if kind == "P":
                    what, m = UNITS[k]
                    if what in ("w1k", "w1v", "small", "vs", "bs", "bn", "wo"):
                        continue
                    b = bank_of[k]
                    pv = bank(b, 2, SEQ)
                    act.wait_ge(unit_done, k + 1)
                    if what == "xbc":
                        for f in range(2):
                            ch = 2 * m + f
                            ins = a(XC[:, ch], pv[:, f], ACT.Identity, scale=PH[:, 16 + 48 + ch:16 + 49 + ch],
                                    bias=PH[:, ch:ch + 1])
                        ins.then_inc(hv_done, 1)
                    elif what in ("kc", "ks", "vc", "kw"):
                        if what in ("ks", "kw"):
                            y = 0 if what == "ks" else 1
                            for f in range(2):
                                for src in range(2):
                                    s = slice(64 * src, 64 * src + 64)
                                    a(KD[64 * src:64 * src + 64, y, 2 * f + src], pv[s, f], ACT.Copy)
                                    ins = a(KD[64 * (1 - src):64 * (1 - src) + 64, y, 2 * f + src], pv[s, f],
                                             ACT.Copy)
                            ins.then_inc(proj_free[b], 1)
                        else:
                            dst = KC2 if what == "kc" else VC2
                            for f in range(2):
                                for src in range(2):
                                    s = slice(64 * src, 64 * src + 64)
                                    a(dst[0:64, 2 * f + src, :], pv[s, f], ACT.Copy)
                                    ins = a(dst[64:128, 2 * f + src, 0:SEQ - 1], pv[s, f, 1:SEQ], ACT.Copy)
                            ins.then_inc(proj_free[b], 1)
                    elif what == "vw":
                        a(VT[:, 1], pv, ACT.Copy).then_inc(proj_free[b], 1)
                    elif what == "q":
                        a(QT[:, 2 * m:2 * m + 2], pv, ACT.Copy).then_inc(proj_free[b], 1)
                    elif what == "z":
                        if n_th >= 2:
                            act.wait_ge(th_used, n_th - 1)
                        a(TH[:, n_th % 2], psum[:, b], ACT.Tanh, scale=0.5).then_inc(th_ready, 1)
                        n_th += 1
                    elif what == "mg":
                        if m == 0:
                            act.wait_ge(y_full, 8)
                            act.wait_ge(cte_done, 4)
                        a(GA[:, :, 256 * m:256 * m + 256], pv, ACT.Tanh, scale=0.5).then_inc(proj_free[b], 1)
                elif kind == "F":
                    if n_th >= 2:
                        act.wait_ge(th_used, n_th - 1)
                    b = bank_of[k]
                    act.wait_ge(proj_free[b], freed[k] + 1)
                    a(TH[:, n_th % 2], XC[:, 2 * k:2 * k + 2].rearrange("p a b -> p (a b)"), ACT.Tanh
                      ).then_inc(th_ready, 1)
                    n_th += 1
                elif kind == "DT":
                    taken(act, "small")
                    own.mark(a(NG[:], SM[:, :, 16:64], ACT.Tanh, scale=0.5))
                    act.wait_ge(small_in, 16 * 8)
                    own.mark(a(ALG[:], ALG[:], ACT.Exp))
                    act.wait_ge(dt_e, 1)
                    a(DT[:, 2], DT[:, 1], ACT.Exp, scale=-1.0).then_inc(dt_w, 1)
                    act.wait_ge(dt_e, 2)
                    a(DT[:, 4], DT[:, 3], ACT.Ln).then_inc(dt_l, 1)
                    act.wait_ge(dt_l, 1)
                elif kind == "S1":
                    act.wait_ge(cs_ready, 1)
                    a(DE[:], DE[:], ACT.Exp).then_inc(de_ready, 1)
                elif kind == "HID":
                    act.wait_ge(hid_t3, k + 1)
                    a(HIDT[:, k, 3, 0:60], HIDT[:, k, 2, 0:60], ACT.Tanh, scale=0.7978845608028654
                      ).then_inc(hid_th, 1)
                elif kind == "A":
                    act.wait_ge(csb_read, k + 1)
                    a(E[:, k % 2], E[:, k % 2], ACT.Exp).then_inc(e_exp, 1)
                    if k >= 4:
                        if k >= 6:
                            act.wait_ge(cte_done, k - 5)
                        a(EC[:, k % 2], psum[:, 3], ACT.Exp).then_inc(ecs_done, 1)
                elif kind == "GY":
                    act.wait_ge(gy_ready, k + 1)
                    if k == 0:
                        act.wait_ge(cte_done, 4)
                    if k >= 2:
                        act.wait_ge(gn_full, k - 1)
                    a(SQ[:, k % 2], YV[:, 2 * k:2 * k + 2].rearrange("p a b -> p (a b)"), ACT.Square
                      ).then_inc(sq_ready, 1)
                elif kind == "GN":
                    act.wait_ge(gn_full, k + 1)
                    own.mark(a(CTE[:, k % 2, 0:SEQ], bank(6, SEQ), ACT.Ln, scale=0.25 / 256, bias=ss[:, 6:7]))
                    own.settle()
                    a(CTE[:, k % 2, SEQ:2 * SEQ], CTE[:, k % 2, 0:SEQ], ACT.Exp, scale=-0.5).then_inc(rb_ready, 1)
                elif kind == "CS":
                    act.wait_ge(cs_sub, 1)
                    a(PCS[:], PCS[:], ACT.Exp).then_inc(cs_exp, 1)
                elif kind == "CP":
                    act.wait_ge(cp_full, 1)
                    a(PCT[:], bank(5, T, 2, P), ACT.Copy).then_inc(cp_read, 1)
                elif kind == "SC":
                    b, nk = k % 2, P * (k // 8 + 1)
                    act.wait_ge(nm_ready, k + 1)
                    for hh in range(2):
                        for y in range(2):
                            q = 2 * hh + y
                            ins = a(SP[:, b, hh, y, 0:nk], SP[:, b, hh, y, 0:nk], ACT.Exp,
                                    bias=AMX[:, b, 1, q:q + 1], accum_out=AMX[:, b, 2, q:q + 1])
                    ins.then_inc(ex_done, 1)
                elif kind == "PT":
                    n = 2 * P * (k // 8 + 1)
                    act.wait_ge(pt_full, k + 1)
                    if k >= 1:
                        act.wait_ge(pv_full, k)
                    a(PTS[:, 0, 0:n], psum[:, 5, 0:n], ACT.Copy).then_inc(pt_act, 1)
                elif kind == "PV":
                    t, j = k // 8, k % 8
                    act.wait_ge(pv_full, k + 1)
                    a(OT[:, j, P * t:P * t + P], bank(7, P), ACT.Copy).then_inc(pv_read, 1)
                elif kind == "MT":
                    act.wait_ge(mt_full, k + 1)
                    a(HT[:, 2 * k:2 * k + 2].rearrange("p a b -> p (a b)"), psum[:, 3 + k % 2], ACT.Copy,
                      scale=0.5).then_inc(mt_ready, 1)

            act.wait_ge(mg_ready, 4)
            act.wait_ge(unit_done, NU - 4)
            act.dma_start(RW_, router_w[0].rearrange("(k p) e -> p k e", p=P)).then_inc(late_in, 16)
            act.dma_start(WFF, ffn_norm_w[0].partition_broadcast(P)).then_inc(late_in, 16)
            act.dma_start(WFN, final_norm_w.partition_broadcast(P)).then_inc(late_in, 16)
            act.dma_start(BGU[0:EXPERTS, :], b_gate_up[0]).then_inc(late_in, 16)
            act.dma_start(BDN[0:EXPERTS, :], b_down[0]).then_inc(late_in, 16)

            act.wait_ge(x2_ready, 4)
            for t in range(T):
                a(RJ[:, t], X[:, t], ACT.Square, accum_out=ss[:, t:t + 1]).then_inc(ss_ready, 1)
            act.wait_ge(lg_ready, 1)
            a(ss[:, 2:4], ss[:, 0:2], ACT.Sqrt).then_inc(sq_root, 1)
            for b in (0, 2):
                act.wait_ge(h2t_full, b + 1)
                a(H2T[:, 2 * b:2 * b + 2].rearrange("p a b -> p (a b)"), psum[:, 3 + b], ACT.Copy
                  ).then_inc(h2t_act, 1)
            act.wait_ge(mx_ready, 1)
            for t in range(T):
                ins = a(RT[:, 2, t, 0:TOPK], MX8[:, t, 0:TOPK], ACT.Exp, bias=RT[:, 1, t, 0:1],
                        accum_out=RT[:, 3, t, 0:1])
            ins.then_inc(te_ready, 1)

            def tokens_in():
                for b in range(2):
                    ins = a(XTS[:, 4 * b:4 * b + 4].rearrange("p a b c -> p (a b c)"), psum[:, 5 + b], ACT.Copy)
                ins.then_inc(xte_ready, 1)

            act.wait_ge(xte_full, 1)
            tokens_in()
            act.wait_ge(zero_ready, 1)
            act.sem_inc(y_ready, 1)
            act.sem_inc(at_ready, 1)
            r = rounds(act)
            with act.Fori(0, r * EX2) as i:
                for s in range(2):
                    n = i * 2 + s
                    act.wait_ge(ct_full, n + 1)
                    a(CTS[:, s], bank(7, T, P), ACT.Copy).then_inc(ct_ready, 1)
                    act.wait_ge(g_ready, n + 1)
                    a(SGA, GBU, ACT.Sigmoid, scale=1.702).then_inc(sig_ready, 1)
                    act.wait_ge(at_full, n + 1)
                    a(ATS.rearrange("p a b -> p (a b)"), psum[:, 7], ACT.Copy).then_inc(at_ready, 1)
                    if s == 1:
                        act.wait_ge(xte_full, i + 2)
                        tokens_in()
                    act.wait_ge(unit_done, n * RING + (NU + RING))
                    a(YSB, psum[:, 2], ACT.Copy).then_inc(y_ready, 1)
            act.wait_ge(final_in, 1)
            for t in range(T):
                a(RJ[:, t], X[:, t], ACT.Square, accum_out=ss[:, t:t + 1]).then_inc(ss_ready, 1)
            act.wait_ge(lg_ready, 3)
            a(ss[:, 2:4], ss[:, 0:2], ACT.Sqrt).then_inc(sq_root, 1)

        @block.vector
        def _(dve):
            own = Own(dve, dve_own)
            v = nc.vector

            def inv_rms(n, done):
                dve.wait_ge(ss_ready, 2 * n)
                done(v.tensor_scalar(ss[:, 0:2], ss[:, 0:2], 1.0 / D, EPS, ALU.mult, ALU.add))
                dve.wait_ge(sq_root, n)
                own.mark(v.reciprocal(ss[:, 4:6], ss[:, 2:4]))
                own.settle()

            inv_rms(1, own.mark)
            for t in range(T):
                v.tensor_scalar(HN[:, t], X[:, t], ss[:, 4 + t:5 + t], None, ALU.mult).then_inc(hn_ready, 1)
            own.mark(v.memset(ss[:, 6:7], EPS))
            dve.wait_ge(par_full, 1)
            own.mark(v.tensor_copy(PC[:], bank(4, P)))
            own.settle()
            own.mark(v.tensor_scalar(PH[:, 0:80], PC[:, 16:96], 0.5, None, ALU.mult))
            own.mark(v.tensor_scalar(PH[:, 80:88], PC[:, 8:16], 0.5, None, ALU.mult))
            own.settle()
            dve.sem_inc(par_ready, 1)
            for b in (1, 3):
                dve.wait_ge(ht_full, b + 1)
                for kk in range(2):
                    ins = v.tensor_scalar(HT[:, 2 * b + kk], bank(b, 2, SEQ)[:, kk],
                                          PC[:, 2 * b + kk:2 * b + kk + 1], None, ALU.mult)
                ins.then_inc(ht_dve, 1)

            n_th = 0
            for kind, k in TOKENS:
                if kind == "P":
                    what, m = UNITS[k]
                    if what in ("w1k", "w1v", "kc", "vc", "ks", "kw", "vw", "q", "mg"):
                        continue
                    b = bank_of[k]
                    pv = bank(b, 2, SEQ)
                    dve.wait_ge(unit_done, k + 1)
                    if what == "xbc":
                        dve.wait_ge(hv_done, m + 1)
                        for tap in (2, 1, 0):
                            back = 3 - tap
                            for f in range(2):
                                ch = 2 * m + f
                                w = PH[:, 16 + 16 * tap + ch:17 + 16 * tap + ch]
                                o = XC[:, ch, back:SEQ]
                                ins = v.scalar_tensor_tensor(out=o, in0=pv[:, f, 0:SEQ - back], scalar=w,
                                                             in1=o, op0=ALU.mult, op1=ALU.add)
                                if not (tap == 0 and f == 1):
                                    own.mark(ins)
                                else:
                                    ins.then_inc(proj_free[b], 1)
                                if f == 1 and tap:
                                    own.settle()
                    elif what == "small":
                        v.tensor_copy(SM[:], bank(b, T, 64)).then_inc(proj_free[b], 1)
                    elif what == "vs":
                        v.tensor_copy(VT[:, 0], pv).then_inc(proj_free[b], 1)
                    elif what == "z":
                        dve.wait_ge(th_ready, n_th + 1)
                        zs = ZS[:, 2 * m:2 * m + 2].rearrange("p a b -> p (a b)")
                        own.mark(v.scalar_tensor_tensor(out=zs, in0=TH[:, n_th % 2], scalar=1.0,
                                                        in1=psum[:, b], op0=ALU.add, op1=ALU.mult))
                        own.settle()
                        dve.sem_inc(proj_free[b], 1)
                        dve.sem_inc(th_used, 1)
                        n_th += 1
                    elif what == "bs":
                        v.scalar_tensor_tensor(out=MG[:, :, 256 * m:256 * m + 256],
                                               in0=GA[:, :, 256 * m:256 * m + 256], scalar=1.0, in1=pv,
                                               op0=ALU.add, op1=ALU.mult).then_inc(proj_free[b], 1)
                    elif what == "bn":
                        ga = GA[:, :, D + 256 * m:D + 256 * m + 256]
                        v.scalar_tensor_tensor(out=ga, in0=ga, scalar=1.0, in1=pv,
                                               op0=ALU.add, op1=ALU.mult).then_inc(proj_free[b], 1)
                        dve.wait_ge(proj_free[b], freed[k] + 1)
                        mg = MG[:, :, 256 * m:256 * m + 256]
                        v.tensor_tensor(mg, mg, ga, ALU.add).then_inc(mg_ready, 1)
                    elif what == "wo":
                        xo = X[:, :, 256 * m:256 * m + 256]
                        v.tensor_tensor(xo, xo, pv, ALU.add).then_inc(x2_ready, 1)
                        dve.wait_ge(x2_ready, m + 1)
                        dve.sem_inc(proj_free[b], 1)
                elif kind == "F":
                    dve.wait_ge(th_ready, n_th + 1)
                    dve.wait_ge(proj_free[bank_of[k]], freed[k] + 1)
                    xc = XC[:, 2 * k:2 * k + 2].rearrange("p a b -> p (a b)")
                    v.scalar_tensor_tensor(out=xc, in0=TH[:, n_th % 2], scalar=1.0, in1=xc, op0=ALU.add,
                                           op1=ALU.mult).then_inc(th_used, 1)
                    n_th += 1
                elif kind == "DT":
                    taken(dve, "small")
                    dve.wait_ge(small_in, 16 * 8)
                    b16 = [P, T, HEADS]
                    own.mark(v.tensor_tensor(DT[:, 0], SM[:, :, 0:16], DTB[:].unsqueeze(1).to_broadcast(b16), ALU.add))
                    own.settle()
                    own.mark(v.tensor_scalar(DT[:, 5], DT[:, 0], -1.0, None, ALU.mult))
                    own.settle()
                    v.tensor_tensor(DT[:, 1], DT[:, 0], DT[:, 5], ALU.max).then_inc(dt_e, 1)
                    dve.wait_ge(dt_w, 1)
                    v.tensor_scalar(DT[:, 3], DT[:, 2], 1.0, None, ALU.add).then_inc(dt_e, 1)
                    dve.wait_ge(dt_e, 2)
                    own.mark(v.scalar_tensor_tensor(out=DT[:, 6], in0=DT[:, 3], scalar=-1.0, in1=DT[:, 2],
                                                    op0=ALU.add, op1=ALU.subtract))
                    own.mark(v.reciprocal(DT[:, 7], DT[:, 3]))
                    own.settle()
                    own.mark(v.tensor_tensor(DT[:, 6], DT[:, 6], DT[:, 7], ALU.mult))
                    dve.wait_ge(dt_l, 1)
                    own.settle()
                    own.mark(v.tensor_tensor(DT[:, 4], DT[:, 4], DT[:, 6], ALU.subtract))
                    own.settle()
                    own.mark(v.scalar_tensor_tensor(out=DT[:, 0], in0=DT[:, 0], scalar=0.0, in1=DT[:, 4],
                                                    op0=ALU.max, op1=ALU.add))
                    own.settle()
                    dve.wait_ge(act_own, 2)
                    v.scalar_tensor_tensor(out=ADT[:], in0=DT[:, 0], scalar=-1.0,
                                           in1=ALG[:].unsqueeze(1).to_broadcast(b16), op0=ALU.mult,
                                           op1=ALU.mult).then_inc(adt_ready, 1)
                    own.mark(v.tensor_scalar(NG[:], NG[:], 0.5, 0.5, ALU.mult, ALU.add))
                elif kind == "S1":
                    dve.wait_ge(s1_full, 1)
                    own.mark(v.tensor_copy(CS[:], bank(4, T, 16)))
                    own.settle()
                    own.mark(v.tensor_tensor(DE[:], bank(4, 16, off=32), CS[:, 0], ALU.subtract))
                    own.settle()
                    dve.sem_inc(cs_ready, 1)
                elif kind == "XT":
                    c, half = k // 2, k % 2
                    dve.wait_ge(xt_full, k + 1 + (k >= 2))
                    v.tensor_tensor(part(XDT, D * c + 512 * half, 8, DH), bank(5, 8, DH),
                                    DT[:, 0, c, 8 * half:8 * half + 8].unsqueeze(2).to_broadcast([P, 8, DH]),
                                    ALU.mult).then_inc(xdt_ready, 1)
                elif kind == "BT":
                    dve.wait_ge(xt_full, 3)
                    v.tensor_copy(BTK, bank(5, 4, P)).then_inc(bt_ready, 1)
                elif kind == "HID":
                    dve.wait_ge(unit_done, 12 + k)
                    h = HIDT[:, k, :, 0:60]
                    own.mark(v.tensor_copy(h[:, 0], bank(7 - k, 60)))
                    own.settle()
                    own.mark(v.tensor_tensor(h[:, 1], h[:, 0], h[:, 0], ALU.mult))
                    own.settle()
                    own.mark(v.tensor_scalar(h[:, 1], h[:, 1], 0.044715, 1.0, ALU.mult, ALU.add))
                    own.settle()
                    v.tensor_tensor(h[:, 2], h[:, 1], h[:, 0], ALU.mult).then_inc(hid_t3, 1)
                    dve.wait_ge(hid_th, k + 1)
                    v.scalar_tensor_tensor(out=HID[:, k, :, 0:NCMP],
                                           in0=h[:, 3].rearrange("p (g c) -> p g c", g=GROUPS), scalar=1.0,
                                           in1=h[:, 0].rearrange("p (g c) -> p g c", g=GROUPS), op0=ALU.add,
                                           op1=ALU.mult).then_inc(hid_ready, 1)
                elif kind == "K2":
                    dve.wait_ge(k2_full, 1)
                    dve.wait_ge(const_done, 2)
                    for hh in range(2):
                        s = slice(64 * hh, 64 * hh + 64)
                        own.mark(v.tensor_scalar(BDK[s, :, hh, :], psum[s, 7, 128:192].rearrange(
                            "p (g c) -> p g c", g=GROUPS), 0.5, None, ALU.mult))
                    own.settle()
                    dve.sem_inc(k2_ready, 1)
                elif kind == "V2":
                    dve.wait_ge(y_full, 8)
                    for hb in range(2):
                        for g2 in range(2):
                            own.mark(v.tensor_copy(HVR[:, hb, g2], HID[:, 1, 2 * hb + g2].unsqueeze(1)
                                                   .to_broadcast([P, REP, 16])))
                    own.settle()
                    dve.sem_inc(hvr_ready, 1)
                    dve.wait_ge(v2_full, 1)
                    for hb in range(2):
                        own.mark(v.tensor_tensor(VBD[:, hb], bank(6, DH, off=128 + 64 * hb).unsqueeze(1)
                                                 .to_broadcast([P, 8, DH]),
                                                 HM[:].unsqueeze(2).to_broadcast([P, 8, DH]), ALU.mult))
                    own.settle()
                    dve.sem_inc(v2_ready, 1)
                elif kind == "A":
                    c, gr, b = k // 4, k % 4, k % 2
                    dve.wait_ge(a_full, k + 1)
                    if k >= 2:
                        dve.wait_ge(y_full, k - 1)
                    for r in range(REP):
                        ins = v.tensor_scalar(E[:, b, P * r:P * r + P], bank(3, REP, P)[:, r],
                                              CS[:, c, REP * gr + r:REP * gr + r + 1], 0.0,
                                              ALU.subtract, ALU.min)
                    ins.then_inc(csb_read, 1)
                    if k >= 2:
                        dve.wait_ge(m_done, k - 1)
                    v.tensor_tensor(GM[:, b], bank(4, P), UPP[:], ALU.mult).then_inc(gm_ready, 1)
                elif kind == "ST":
                    dve.wait_ge(st_full, k + 1)
                    v.tensor_copy(ST[:, 512 * k:512 * k + 512], psum[:, 7]).then_inc(st_ready, 1)
                elif kind == "Y":
                    c, gr = k // 4, k % 4
                    dve.wait_ge(y_full, k + 1)
                    if k == 0:
                        dve.wait_ge(xd_done, 1)
                    yv = YV[:, 2 * gr:2 * gr + 2, P * c:P * c + P]
                    v.tensor_tensor(yv, yv, bank(6, 2, P), ALU.add).then_inc(y_read, 1)
                elif kind == "GY":
                    if k == 0:
                        dve.wait_ge(y_read, 8)
                    yv = YV[:, 2 * k:2 * k + 2]
                    v.tensor_tensor(yv, yv, ZS[:, 2 * k:2 * k + 2], ALU.mult).then_inc(gy_ready, 1)
                elif kind == "GN":
                    dve.wait_ge(rb_ready, k + 1)
                    dve.wait_ge(sq_ready, k + 1)
                    for f in range(2):
                        j = 2 * k + f
                        ins = v.scalar_tensor_tensor(out=YV[:, j], in0=YV[:, j], scalar=PH[:, 80 + j:81 + j],
                                                     in1=CTE[:, k % 2, SEQ:2 * SEQ], op0=ALU.mult, op1=ALU.mult)
                        if f == 0:
                            own.mark(ins)
                        else:
                            own.mark(ins)
                    own.settle()
                    dve.sem_inc(yn_ready, 1)
                elif kind == "CS":
                    dve.wait_ge(cs_full, 1)
                    for t in range(T):
                        own.mark(v.scalar_tensor_tensor(
                            out=PCS[:, t], in0=bank(5, HEADS, 16, off=256 * t), scalar=DH ** -0.5,
                            in1=CMC[:, t].unsqueeze(1).to_broadcast([P, HEADS, 16]), op0=ALU.mult, op1=ALU.add))
                    own.settle()
                    own.mark(v.tensor_reduce(CST[:, 0], PCS[:], AX.X, ALU.max))
                    own.settle()
                    own.mark(v.tensor_scalar(CST[:, 0], CST[:, 0], -1e25, None, ALU.max))
                    own.settle()
                    v.tensor_tensor(PCS[:], PCS[:], CST[:, 0].unsqueeze(3).to_broadcast([P, T, HEADS, 16]),
                                    ALU.subtract).then_inc(cs_sub, 1)
                    dve.wait_ge(cs_exp, 1)
                    own.mark(v.tensor_reduce(CST[:, 1], PCS[:], AX.X, ALU.add))
                    own.settle()
                    own.mark(v.tensor_scalar(CST[:, 1], CST[:, 1], 1e-30, None, ALU.max))
                    own.settle()
                    own.mark(v.reciprocal(CST[:, 2], CST[:, 1]))
                    own.settle()
                    own.mark(v.tensor_tensor(CST[:, 3], CST[:, 2],
                                             NG[:].rearrange("p t (h y) -> p t h y", y=3)[:, :, :, 0], ALU.mult))
                    own.settle()
                    v.tensor_tensor(PCS[:], PCS[:], CST[:, 3].unsqueeze(3).to_broadcast([P, T, HEADS, 16]),
                                    ALU.mult).then_inc(cp_ready, 1)
                elif kind == "SC":
                    t, j, b = k // 8, k % 8, k % 2
                    nk = P * (t + 1)
                    dve.wait_ge(sc_full, k + 1)
                    if k == 0:
                        dve.wait_ge(y_full, 8)
                        dve.wait_ge(st_full, 2)
                    if k >= 2:
                        dve.wait_ge(pt_full, k - 1)
                    for hh in range(2):
                        for y in range(2):
                            q = 2 * hh + y
                            own.mark(v.tensor_tensor_reduce(
                                SP[:, b, hh, y, 0:nk], psum[:, 3 + hh, 256 * y:256 * y + nk],
                                CM[:, 256 - nk:256], DH ** -0.5, -3e38, ALU.add, ALU.max,
                                AMX[:, b, 0, q:q + 1]))
                    own.settle()
                    v.tensor_scalar(AMX[:, b, 1], AMX[:, b, 0], -1.0, None, ALU.mult).then_inc(nm_ready, 1)
                elif kind == "RW":
                    t, j, b = k // 8, k % 8, k % 2
                    dve.wait_ge(ex_done, k + 1)
                    own.mark(v.tensor_scalar(AMX[:, b, 2], AMX[:, b, 2], 1e-30, None, ALU.max))
                    own.settle()
                    own.mark(v.reciprocal(AMX[:, b, 2], AMX[:, b, 2]))
                    own.settle()
                    ng = NG[:, t].rearrange("p (h y) -> p h y", y=3)[:, 2 * j:2 * j + 2, 1:3]
                    v.tensor_tensor(AMX[:, b, 3].rearrange("p (h y) -> p h y", h=2),
                                    AMX[:, b, 2].rearrange("p (h y) -> p h y", h=2), ng, ALU.mult
                                    ).then_inc(w_ready, 1)
                elif kind == "PT":
                    n = 2 * P * (k // 8 + 1)
                    dve.wait_ge(pt_full, k + 1)
                    if k >= 1:
                        dve.wait_ge(pv_full, k)
                    v.tensor_copy(PTS[:, 1, 0:n], psum[:, 6, 0:n]).then_inc(pt_dve, 1)

            inv_rms(2, lambda ins: ins.then_inc(lg_ready, 1))
            dve.wait_ge(late_in, 16 * 5)
            for t in range(T):
                v.scalar_tensor_tensor(out=H2[:, t], in0=X[:, t], scalar=ss[:, 4 + t:5 + t], in1=WFF,
                                       op0=ALU.mult, op1=ALU.mult).then_inc(h2_ready, 1)
            for b in (1, 3):
                dve.wait_ge(h2t_full, b + 1)
                v.tensor_copy(H2T[:, 2 * b:2 * b + 2].rearrange("p a b -> p (a b)"), psum[:, 3 + b]
                              ).then_inc(h2t_dve, 1)
            dve.wait_ge(rt_full, 1)
            own.mark(v.tensor_tensor(LG, bank(7, T, EXPERTS), RB[:].unsqueeze(1).to_broadcast([P, T, EXPERTS]),
                                     ALU.add))
            own.settle()
            for t in range(T):
                own.mark(v.max(MX8[:, t], LG[:, t]))
            own.settle()
            for t in range(T):
                own.mark(v.max_index(IX8[:, t], MX8[:, t], LG[:, t]))
                own.mark(v.tensor_scalar(RT[:, 1, t, 0:1], MX8[:, t, 0:1], -1.0, None, ALU.mult))
            own.settle()
            v.tensor_copy(RT[:, 0], IX8[:]).then_inc(mx_ready, 1)
            dve.wait_ge(mx_ready, 1)
            for t in range(T):
                for q in range(TOPK):
                    own.mark(v.tensor_scalar(OH4[:, t, q], EIO[:], RT[:, 0, t, q:q + 1], None, ALU.is_equal))
            own.settle()
            for t in range(T):
                own.mark(v.tensor_reduce(MSK[:, t], OH4[:, t].rearrange("p q e -> p e q"), AX.X, ALU.add))
            dve.wait_ge(te_ready, 1)
            for t in range(T):
                own.mark(v.reciprocal(RT[:, 4, t, 0:1], RT[:, 3, t, 0:1]))
            own.settle()
            for t in range(T):
                own.mark(v.tensor_scalar(RT[:, 5, t, 0:TOPK], RT[:, 2, t, 0:TOPK], RT[:, 4, t, 0:1], None, ALU.mult))
            own.settle()
            for t in range(T):
                own.mark(v.tensor_tensor(OW4[:, t], OH4[:, t], RT[:, 5, t, 0:TOPK].unsqueeze(2)
                                         .to_broadcast([P, TOPK, EXPERTS]), ALU.mult))
            own.settle()
            for t in range(T):
                own.mark(v.tensor_reduce(CW[:, t], OW4[:, t].rearrange("p q e -> p e q"), AX.X, ALU.add))
            own.settle()
            dve.sem_inc(msk_ready, 1)
            dve.wait_ge(rk_full, 1)
            own.mark(v.tensor_scalar(MSK, MSK, -1e4, 1e4, ALU.mult, ALU.add))
            own.mark(v.tensor_reduce(RT[:, 6, 0, 0:1], bank(3, EXPERTS, off=64), AX.X, ALU.max))
            own.settle()
            own.mark(v.tensor_tensor(SLT, bank(3, T, EXPERTS), MSK, ALU.add))
            own.mark(v.tensor_scalar(RT[:, 7, 0, 0:3], TH3[:], RT[:, 6, 0, 0:1], None, ALU.is_lt))
            own.settle()
            own.mark(v.tensor_reduce(RT[:, 8, 0, 0:1], RT[:, 7, 0, 0:3], AX.X, ALU.add))
            own.settle()
            own.mark(v.tensor_scalar(RCI[:], RT[:, 8, 0, 0:1], 1.0, None, ALU.add))
            own.settle()
            dve.sem_inc(round_ready, 1)
            dve.sem_inc(slot_ready, 1)
            dve.wait_ge(cwt_full, 1)
            own.mark(v.tensor_copy(CWT[0:EXPERTS], bank(4, T, P)[0:EXPERTS]))
            own.settle()
            dve.sem_inc(cwt_full, 1)
            for t in range(T):
                dve.wait_ge(bd_full, t + 1)
                xo = X[:, t].rearrange("p (a b) -> p a b", a=2)
                v.tensor_tensor(xo, xo, psum[:, 5:7, :], ALU.add).then_inc(acc_ready, 1)
            dve.wait_ge(acc_ready, T)

            def prepare(e0, settled, base):
                cols = bass.ds(e0, 2)

                def go(k, ins):
                    ins.then_inc(dve_own, 1)
                    return ins

                v.tensor_copy(C2[:, 0], SLT[:, :, cols]).then_inc(dve_own, 1)
                v.tensor_copy(C2[:, 1], CW[:, :, cols]).then_inc(dve_own, 1)
                v.tensor_copy(OHE[0:EXPERTS], IDN[0:EXPERTS, cols].unsqueeze(2)
                              .to_broadcast([EXPERTS, 2, CAP])).then_inc(dve_own, 1)
                dve.wait_ge(dve_own, base + 3)
                v.tensor_scalar(SLT[:, :, cols], SLT[:, :, cols], float(-CAP), None, ALU.add).then_inc(dve_own, 1)
                for t in range(T):
                    for s in range(2):
                        v.tensor_scalar(SPR[:, t, s], IOT[:, 0:CAP], C2[:, 0, t, s:s + 1], None, ALU.is_equal
                                        ).then_inc(dve_own, 1)
                        v.tensor_scalar(CPR[:, t, s], IOT[:], C2[:, 0, t, s:s + 1], C2[:, 1, t, s:s + 1],
                                        ALU.is_equal, ALU.mult).then_inc(dve_own, 1)
                dve.wait_ge(dve_own, base + 12)
                dve.sem_inc(prep_done, 1)

            PREP = 12
            prepare(0, None, own.n)
            base = own.n + PREP
            per = PREP + 2
            dve.sem_inc(gu_read, 1)
            dve.sem_inc(o_read, 1)
            r = rounds(dve)
            with dve.Fori(0, r * EX2) as i:
                for s in range(2):
                    n = i * 2 + s
                    dve.wait_ge(unit_done, n * RING + (NU + 8))
                    gu = psum[:, 0:2, :].rearrange("p q (f two) -> p q f two", two=2)
                    v.tensor_scalar(GBU.rearrange("p (q f) -> p q f", q=2), gu[:, :, :, 0], 7.0, None, ALU.min
                                    ).then_inc(g_ready, 1)
                    v.tensor_scalar(LBU.rearrange("p (q f) -> p q f", q=2), gu[:, :, :, 1], 7.0, -7.0,
                                    ALU.min, ALU.max).then_inc(gu_read, 1)
                    dve.wait_ge(sig_ready, n + 1)
                    v.tensor_tensor(GBU, GBU, SGA, ALU.mult).then_inc(dve_own, 1)
                    dve.wait_ge(dve_own, i * per + (base + (1 if s == 0 else 2)))
                    dve.wait_ge(gu_read, n + 2)
                    v.scalar_tensor_tensor(out=ABU, in0=LBU, scalar=1.0, in1=GBU, op0=ALU.add, op1=ALU.mult
                                           ).then_inc(act_ready, 1)
                    for t in range(T):
                        dve.wait_ge(o_full, n * 2 + (t + 1))
                        xo = X[:, t].rearrange("p (a b) -> p a b", a=2)
                        v.tensor_tensor(xo, xo, psum[:, 3:5, :], ALU.add).then_inc(o_read, 1)
                    if s == 1:
                        dve.wait_ge(ct_full, n + 1)
                        prepare(((i + 1) % EX2) * 2, None, i * per + (base + 2))
            nexp = r * EXPERTS
            for t in range(T):
                dve.wait_ge(o_full, nexp * 2 + (t + 1))
                xo = X[:, t].rearrange("p (a b) -> p a b", a=2)
                v.tensor_tensor(xo, xo, psum[:, 3:5, :], ALU.add).then_inc(o_read, 1)
            dve.wait_ge(o_read, nexp * 2 + 3)
            dve.sem_inc(final_in, 1)
            dve.wait_ge(ss_ready, 6)
            v.tensor_scalar(ss[:, 0:2], ss[:, 0:2], 1.0 / D, EPS, ALU.mult, ALU.add).then_inc(lg_ready, 2)
            dve.wait_ge(sq_root, 3)
            v.reciprocal(ss[:, 4:6], ss[:, 2:4]).then_inc(lg_ready, 1)
            dve.wait_ge(lg_ready, 4)
            for t in range(T):
                v.scalar_tensor_tensor(out=RJ[:, t], in0=X[:, t], scalar=ss[:, 4 + t:5 + t], in1=WFN,
                                       op0=ALU.mult, op1=ALU.mult).then_inc(lg_ready, 1)
            dve.wait_ge(lg_ready, 6)
            dve.sem_inc(norm_ready, 1)


_INS = ['x', 'mix_norm_w', 'w_in', 'conv_w', 'conv_b', 'dt_bias', 'a_log', 'd_skip', 'ssm_norm_w',
        'cmp_pos_k', 'cmp_w1_k', 'cmp_w2_k', 'cmp_pos_v', 'cmp_w1_v', 'cmp_w2_v', 'w_branch_ssm',
        'w_branch_nsa', 'w_out', 'ffn_norm_w', 'router_w', 'router_b', 'w_gate_up', 'b_gate_up', 'w_down',
        'b_down', 'final_norm_w']


def kernel(**inputs):
    import numpy as _np
    import concourse.bacc as _bacc
    from concourse import mybir as _mybir
    from concourse.bass_utils import run_bass_kernel_spmd as _run

    nc = _bacc.Bacc("TRN2", target_bir_lowering=False, num_devices=1)
    arrays, args = {}, []
    for name in _INS:
        a = _np.ascontiguousarray(inputs[name])
        arrays[f"in_{name}_dram"] = a
        args.append(nc.dram_tensor(f"in_{name}_dram", a.shape, _mybir.dt.from_np(a.dtype), kind="ExternalInput").ap())
    args.append(nc.dram_tensor("out_0_dram", (1, 256, 1024), _mybir.dt.float32, kind="ExternalOutput").ap())
    hybrid_block(nc, *args)
    r = _run(nc, [arrays], core_ids=[0])
    return r.results[0]["out_0_dram"]
```

```python
from contextlib import ExitStack

import concourse.bass as bass
from concourse import mybir

F32 = mybir.dt.float32
I32 = mybir.dt.int32
U32 = mybir.dt.uint32
F32R = mybir.dt.float32r
ALU = mybir.AluOpType
ACT = mybir.ActivationFunctionType
AX = mybir.AxisListType

P = 128
D = 1024
SEQ = 256
T = SEQ // P
KT = D // P
HEADS = 16
GROUPS = 4
REP = HEADS // GROUPS
DH = 64
CMP_BLOCK, CMP_STRIDE = 32, 16
NCMP = (SEQ - CMP_BLOCK) // CMP_STRIDE + 1
EXPERTS = 32
TOPK = 4
EPS = 1e-5
NEG = -1e30
CAP = 64
RING = 12
STREAM = 4
EXTRA = 4
SPLITS = 3
SLOT = 2048

OFF_Z, OFF_XBC, OFF_DT, OFF_Q = 0, 1024, 3072, 3088
OFF_KC, OFF_VC, OFF_KS, OFF_VS, OFF_KW, OFF_VW = 4112, 4368, 4624, 4880, 5136, 5392
OFF_NG, OFF_MG = 5648, 5696

UNITS = ([("xbc", m) for m in range(8)] + [("small", 0), ("kc", 0), ("vc", 0), ("ks", 0), ("kw", 0),
         ("w1k", 0), ("w1v", 0), ("vs", 0), ("vw", 0)] + [("q", m) for m in range(4)]
         + [("z", m) for m in range(4)] + [("mg", m) for m in range(8)]
         + [("bs", m) for m in range(4)] + [("bn", m) for m in range(4)] + [("wo", m) for m in range(4)])
NU = len(UNITS)


SPLIT_UNITS = [u for u, (kind, _) in enumerate(UNITS) if kind not in ("w1k", "w1v")]


def token_order():
    u = {x: n for n, x in enumerate(UNITS)}
    out = []

    def unit(kind, m=0):
        out.extend([("H", u[(kind, m)]), ("P", u[(kind, m)])])

    for m in range(8):
        unit("xbc", m)
        if m >= 1:
            out.append(("F", m - 1))
    unit("small")
    out += [("F", 7), ("XD", 0), ("DT", 0)]
    unit("kc")
    out += [("S1", 0)]
    unit("vc")
    out += [("XT", 0)]
    unit("ks")
    out += [("XT", 1)]
    unit("kw")
    out += [("HID", 0), ("BT", 0), ("A", 0)]
    unit("vs")
    out += [("HT", 0), ("A", 1), ("XT", 2)]
    unit("vw")
    out += [("K2", 0), ("Y", 0), ("A", 2), ("ST", 0), ("XT", 3)]
    for m in range(4):
        unit("q", m)
        out += [("Y", m + 1), ("A", m + 3)]
        if m == 0:
            out += [("ST", 1)]
    unit("z", 0)
    out += [("Y", 5), ("A", 7)]
    unit("z", 1)
    out += [("Y", 6)]
    unit("z", 2)
    out += [("Y", 7), ("V2", 0), ("CT", 0), ("GY", 0)]
    unit("z", 3)
    out += [("CS", 0), ("GY", 1)]
    unit("mg", 0)
    out += [("GN", 0), ("CP", 0), ("GY", 2), ("SC", 0)]
    unit("mg", 1)
    out += [("GN", 1), ("GY", 3), ("SC", 1)]
    halves = []
    for x in [("mg", m) for m in range(2, 8)] + [("bs", m) for m in range(4)]:
        halves += [("H", u[x]), ("P", u[x])]
    out += [halves.pop(0), ("GN", 2), halves.pop(0), ("GN", 3), ("YS", 0)]
    for k in range(17):
        if k + 2 < 16:
            out.append(("SC", k + 2))
        if k < 16:
            out.append(("RW", k))
        if k >= 1:
            if k % 4 == 1 and halves:
                out.append(halves.pop(0))
            out.append(("PV", k - 1))
        if halves:
            out.append(halves.pop(0))
        if k < 16:
            out.append(("PT", k))
    out += halves
    for m in range(4):
        unit("bn", m)
        if m >= 1:
            out.append(("MT", m - 1))
    out.append(("MT", 3))
    for m in range(4):
        unit("wo", m)
    order = [("W", SPLIT_UNITS[SPLITS - 1])]
    for token in out:
        order.append(token)
        if token[0] == "H" and token[1] in SPLIT_UNITS[1:]:
            i = SPLIT_UNITS.index(token[1]) - 1 + SPLITS
            if i < len(SPLIT_UNITS):
                order.append(("W", SPLIT_UNITS[i]))
    return order


TOKENS = token_order()


def hybrid_block(nc, x, mix_norm_w, w_in, conv_w, conv_b, dt_bias, a_log, d_skip, ssm_norm_w,
                 cmp_pos_k, cmp_w1_k, cmp_w2_k, cmp_pos_v, cmp_w1_v, cmp_w2_v,
                 w_branch_ssm, w_branch_nsa, w_out, ffn_norm_w, router_w, router_b,
                 w_gate_up, b_gate_up, w_down, b_down, final_norm_w, out):
    with ExitStack() as ctx:
        def sb(name, shape, dt=F32):
            return ctx.enter_context(nc.sbuf_tensor(name, shape, dt))

        def sem(name):
            return ctx.enter_context(nc.semaphore(name))

        def part(t, off, *dims):
            n = 1
            for d in dims:
                n *= d
            names = "abcde"[:len(dims)]
            rank = len(t.shape) - 1
            flat = t[:] if rank == 1 else t[:].rearrange(
                "p " + " ".join("wxyz"[:rank]) + " -> p (" + " ".join("wxyz"[:rank]) + ")")
            v = flat[:, off:off + n]
            if len(dims) == 1:
                return v
            return v.rearrange("p (" + " ".join(names) + ") -> p " + " ".join(names),
                               **{c: d for c, d in zip(names[1:], dims[1:])})

        def at_place(name, shape, place, dt=F32R):
            return nc.alloc_sbuf_tensor_at(name, shape, dt, offset=place)

        ring_at = -(-nc.sbuf_base // 32) * 32
        ring = sb("ring", [P, RING, SLOT])
        X = sb("X", [P, T, D])
        ht_at = -(-nc.sbuf_base // 32) * 32
        HT = sb("HT", [P, KT, SEQ])
        XC = sb("XC", [P, 16, SEQ])
        yv_at = -(-nc.sbuf_base // 32) * 32
        YV = sb("YV", [P, 8, SEQ])
        zs_at = -(-nc.sbuf_base // 32) * 32
        ZS = sb("ZS", [P, 8, SEQ])
        XDT = sb("XDT", [P, 3 * D])
        st_at = -(-nc.sbuf_base // 32) * 32
        ST = sb("ST", [P, D])
        E = sb("E", [P, 2, 512])
        GM = sb("GM", [P, 2, P])
        ec_at = -(-nc.sbuf_base // 32) * 32
        EC = sb("EC", [P, 2, 512])
        CTE = sb("CTE", [P, 2, 512])
        TH = sb("TH", [P, 2, 512])
        QT = sb("QT", [P, 8, SEQ])
        KD = sb("KD", [P, 2, GROUPS, SEQ])
        VT = sb("VT", [P, 2, T, 256])
        PR = sb("PR", [P, P])
        PC = sb("PC", [P, P])
        PH = sb("PH", [P, 96])
        IDN = sb("IDN", [P, P])
        UPP = sb("UPP", [P, P])
        UST = sb("UST", [P, P])
        ONE = sb("ONE", [P, P])
        CM = sb("CM", [P, 256])
        CMC = sb("CMC", [P, T, 16])
        IOI = sb("IOI", [P, P], I32)
        IOT = sb("IOT", [P, P])
        EIO = sb("EIO", [P, EXPERTS])
        TH3 = sb("TH3", [P, 3])
        HM = sb("HM", [P, 8])
        W2K = sb("W2K", [P, 2, DH])
        W2V = sb("W2V", [P, DH])
        DTB = sb("DTB", [P, HEADS])
        ALG = sb("ALG", [P, HEADS])
        DCOL = sb("DCOL", [P, 8])
        RB = sb("RB", [P, EXPERTS])
        SM = sb("SM", [P, T, 64])
        DT = sb("DT", [P, 8, T, HEADS])
        ADT = sb("ADT", [P, T, HEADS])
        CS = sb("CS", [P, T, HEADS])
        DE = sb("DE", [P, HEADS])
        NG = sb("NG", [P, T, 48])
        ss = sb("ss", [P, 8])
        HID = sb("HID", [P, 2, GROUPS, 16])
        BDK = sb("BDK", [P, GROUPS, 2, 16])
        AMX = sb("AMX", [P, 3, 4, 4])

        slot_at = [ring_at + 4 * SLOT * i for i in range(RING)]
        HTL = at_place("HTL", [P, KT, SEQ], slot_at[STREAM])
        OTL = at_place("OTL", [P, KT, SEQ], slot_at[STREAM + 1])
        WH = [at_place(f"WH{i}", [P, SLOT], slot_at[STREAM + 2 + i]) for i in range(SPLITS)]
        WL = [at_place(f"WL{i}", [P, SLOT], slot_at[STREAM + 2 + SPLITS + i]) for i in range(SPLITS)]
        HTH = at_place("HTH", [P, KT, SEQ], ht_at)
        OTH = at_place("OTH", [P, KT, SEQ], zs_at)
        YSH = at_place("YSH", [P, KT, SEQ], ec_at)
        YSL = at_place("YSL", [P, KT, SEQ], yv_at)
        HTHF, HTLF, OTHF, YSHF = [t[:].bitcast(F32) for t in (HTH, HTL, OTH, YSH)]
        WHF = [t[:].bitcast(F32) for t in WH]
        extra = [part(XDT, D, SLOT), at_place("extra1", [P, SLOT], st_at, F32)[:],
                 at_place("extra2", [P, SLOT], ec_at, F32)[:], part(XC, SLOT, SLOT)]

        VBD = part(ST, 0, 2, 8, DH)
        PCS = part(E, 0, T, HEADS, 16)
        PCT = part(E, 512, T, 2, P)
        CSR = part(EC, 512, 512)
        BTK = part(ZS, 0, GROUPS, P)
        HIDT = part(ST, 0, 5, P)
        KCP = EC[:].rearrange("p h (m j) -> p h m j", j=8)
        VCP = CTE[:].rearrange("p h (m j) -> p h m j", j=8)
        CST = part(GM, 0, 6, T, HEADS)
        RW_ = part(GM, 0, KT, EXPERTS)
        HVR = part(CTE, 0, 2, 2, REP, 16)
        KC2 = part(ZS, 0, GROUPS, SEQ)
        VC2 = part(ZS, 1024, GROUPS, SEQ)
        HN = part(ZS, 0, T, D)
        OT = part(ZS, 0, 8, SEQ)
        GA = part(XC, 0, T, 2048)
        SQ = EC
        SP = [part(XDT, 0, 2, 2, 256), part(XDT, 1024, 2, 2, 256), part(TH, 0, 2, 2, 256)]
        PTS = part(XDT, 2048, 2, 512)
        MG = GA[:, :, 0:D]
        H2 = part(XC, 0, T, D)
        H2T = part(XC, 2048, KT, SEQ)
        WFF = part(YV, 0, D)
        WFN = part(YV, 1024, D)
        BGU = part(KD, 0, 2048)
        BDN = part(VT, 0, D)
        XTS = part(ZS, 0, KT, 2, CAP)
        SGA = part(ZS, 1024, 512)
        GBU = part(ZS, 1536, 512)
        LBU = part(HT, 0, 512)
        ABU = part(HT, 512, 512)
        ATS = part(HT, 1024, 4, P)
        YSB = part(HT, 1536, 512)
        CTS = part(QT, 0, 2, T, P)
        SPR = part(QT, 512, T, 2, CAP)
        CPR = part(QT, 768, T, 2, P)
        OHE = part(QT, 1280, 2, CAP)
        C2 = part(QT, 1408, 2, T, 2)
        SLT = part(QT, 1424, T, EXPERTS)
        CW = part(QT, 1488, T, EXPERTS)
        MSK = part(QT, 1552, T, EXPERTS)
        LG = part(QT, 1616, T, EXPERTS)
        MX8 = part(QT, 1680, T, 8)
        CWT = part(QT, 1712, T, P)
        OH4 = part(XDT, 0, T, TOPK, EXPERTS)
        OW4 = part(XDT, 256, T, TOPK, EXPERTS)
        RT = part(XDT, 512, 16, T, 8)
        SQX = part(XC, 2048, T, D)
        RJ = part(ring, 0, T, D)
        IX8 = sb("IX8", [P, T, 8], U32)
        RCI = sb("RCI", [P, 1], I32)

        psum = ctx.enter_context(nc.psum_tensor("psum", [P, 8, 512], F32))

        ring_full = [sem(f"ring_full{i}") for i in range(RING)]
        extra_full = [sem(f"extra_full{i}") for i in range(EXTRA)]
        unit_done = sem("unit_done")
        wh_ready, wl_ready, ys_high, ys_ready, ht_low, mt_low, ot_high = [sem(n) for n in (
            "wh_ready wl_ready ys_high ys_ready ht_low mt_low ot_high").split()]
        proj_free = [sem(f"proj_free{i}") for i in range(3)]
        (x_in, rows_in, small_in, late_in, const_done, dve_own, act_own, pool_own, hn_ready, ht_full,
         ht_act, ht_dve, par_full, par_ready, hv_done, th_ready, th_used, xd_done, sm_ready, dt_e, dt_w,
         dt_l, adt_ready, s1_full, cs_ready, de_ready, xt_full, xdt_ready, bt_ready, xde_ready, a_full,
         csb_read, gm_ready, e_exp, ecs_done, m_done, cte_done, y_full, y_read, st_full, st_ready,
         kv_act, kv_dve, csr_full, csr_ready, kcp_ready, hid_act, hid_full, hid_t3, hid_th, hid_ready, hvr_ready, k2_full, k2_ready, v2_full, v2_ready,
         q_ready, v_ready, z_used, gy_ready, sq_ready, gn_full, rb_ready, yn_ready, ga_ready, cs_full,
         cs_sub, cs_exp, cp_ready, cp_full, cp_read, sc_full, nm_ready, ex_done, w_ready, p_ready,
         pt_full, pt_act, pt_dve, pv_full, pv_read, mg_ready, mt_full, mt_ready, x2_ready, ss_ready,
         sq_root, h2_ready, h2t_full, h2t_act, h2t_dve, rt_full, lg_ready, mx_ready, te_ready, msk_ready,
         rk_full, slot_ready, round_ready, acc_ready, cwt_full, bd_full, final_in, norm_ready, stored,
         prep_done, xte_full, xte_ready, gu_read, ct_full, ct_ready, y_ready, o_full, o_read, g_ready,
         sig_ready, act_ready, at_full, at_ready, zero_ready) = [sem(n) for n in (
            "x_in rows_in small_in late_in const_done dve_own act_own pool_own hn_ready ht_full "
            "ht_act ht_dve par_full par_ready hv_done th_ready th_used xd_done sm_ready dt_e dt_w "
            "dt_l adt_ready s1_full cs_ready de_ready xt_full xdt_ready bt_ready xde_ready a_full "
            "csb_read gm_ready e_exp ecs_done m_done cte_done y_full y_read st_full st_ready "
            "kv_act kv_dve csr_full csr_ready kcp_ready hid_act hid_full hid_t3 hid_th hid_ready hvr_ready k2_full k2_ready v2_full v2_ready "
            "q_ready v_ready z_used gy_ready sq_ready gn_full rb_ready yn_ready ga_ready cs_full "
            "cs_sub cs_exp cp_ready cp_full cp_read sc_full nm_ready ex_done w_ready p_ready "
            "pt_full pt_act pt_dve pv_full pv_read mg_ready mt_full mt_ready x2_ready ss_ready "
            "sq_root h2_ready h2t_full h2t_act h2t_dve rt_full lg_ready mx_ready te_ready msk_ready "
            "rk_full slot_ready round_ready acc_ready cwt_full bd_full final_in norm_ready stored "
            "prep_done xte_full xte_ready gu_read ct_full ct_ready y_ready o_full o_read g_ready "
            "sig_ready act_ready at_full at_ready zero_ready").split()]

        loads = {u: 2 if UNITS[u][0] == "small" else 1 for u in range(NU)}
        full_at, slot_total = {}, [0] * RING
        for u in range(NU):
            slot_total[u % STREAM] += 16 * loads[u]
            full_at[u] = slot_total[u % STREAM]
        bank_of, freed, uses = {}, {}, [0] * 3
        n = 0
        for u, (kind, _) in enumerate(UNITS):
            if kind in ("w1k", "w1v"):
                continue
            bank_of[u], freed[u] = n % 3, uses[n % 3]
            uses[n % 3] += 1
            n += 1

        def slot_view(u, *dims):
            return part(ring, (u % STREAM) * SLOT, *dims)

        def bank(b, *dims, off=0):
            n = 1
            for d in dims:
                n *= d
            v = psum[:, b, off:off + n]
            if len(dims) == 1:
                return v
            names = "abcde"[:len(dims)]
            return v.rearrange("p (" + " ".join(names) + ") -> p " + " ".join(names),
                               **{c: d for c, d in zip(names[1:], dims[1:])})

        at_unit = {x: n for n, x in enumerate(UNITS)}

        def taken(eng, kind, m=0):
            u = at_unit[(kind, m)]
            eng.wait_ge(proj_free[bank_of[u]], freed[u] + 1)

        class Own:

            def __init__(self, eng, s):
                self.eng, self.s, self.n = eng, s, 0

            def mark(self, ins):
                self.n += 1
                ins.then_inc(self.s, 1)

            def settle(self):
                self.eng.wait_ge(self.s, self.n)

        EX2 = EXPERTS // 2

        def rounds(eng):
            eng.wait_ge(round_ready, 1)
            r = eng.value_load(RCI[0:1, 0:1], min_val=1, max_val=4)
            return r

        block = ctx.enter_context(nc.Block())

        @block.sync
        def _(sp):
            sp.dma_start(X[:], x[0].rearrange("(t p) d -> p t d", p=P)).then_inc(x_in, 16)

            def w_cols(w, c0, n):
                return w[0, :, c0:c0 + n].rearrange("(k p) n -> p k n", p=P)

            first = {"z": OFF_Z, "xbc": OFF_XBC, "q": OFF_Q, "kc": OFF_KC, "vc": OFF_VC, "ks": OFF_KS,
                     "vs": OFF_VS, "kw": OFF_KW, "vw": OFF_VW, "mg": OFF_MG}
            for u, (kind, m) in enumerate(UNITS):
                if u >= STREAM:
                    if u - STREAM in SPLIT_UNITS:
                        sp.wait_ge(wl_ready, SPLIT_UNITS.index(u - STREAM) + 1)
                    else:
                        sp.wait_ge(unit_done, u - STREAM + 1)
                full = ring_full[u % STREAM]
                if kind == "small":
                    v = slot_view(u, KT, 64)
                    sp.dma_start(v[:, :, 0:16], w_cols(w_in, OFF_DT, 16)).then_inc(full, 16)
                    sp.dma_start(v[:, :, 16:64], w_cols(w_in, OFF_NG, 48)).then_inc(full, 16)
                elif kind in ("w1k", "w1v"):
                    w1 = cmp_w1_k if kind == "w1k" else cmp_w1_v
                    sp.dma_start(slot_view(u, 16, P), w1[0].rearrange("(k p) n -> p k n", p=P)).then_inc(full, 16)
                else:
                    w = {"bs": w_branch_ssm, "bn": w_branch_nsa, "wo": w_out}.get(kind, w_in)
                    sp.dma_start(slot_view(u, KT, 256), w_cols(w, first.get(kind, 0) + 256 * m, 256)
                                 ).then_inc(full, 16)

            def load(e, s, j):
                own_slot = s == 1 and j < EXTRA
                dst = extra[j] if own_slot else part(ring, j * SLOT, SLOT)
                if j < 8:
                    src = w_gate_up[0, e, P * j:P * j + P, :].rearrange("(k p) n -> p k n", p=P)
                    dst = dst.rearrange("p (k n) -> p k n", k=1)
                else:
                    src = w_down[0, e, 256 * (j - 8):256 * (j - 8) + 256, :].rearrange("(k p) n -> p k n", p=P)
                    dst = dst.rearrange("p (k n) -> p k n", k=2)
                sp.dma_start(dst, src).then_inc(extra_full[j] if own_slot else ring_full[j], 16)

            for j in range(RING):
                if j < STREAM:
                    last = max(u for u in range(NU) if u % STREAM == j)
                    sp.wait_ge(wl_ready, SPLIT_UNITS.index(last) + 1)
                elif j == STREAM + 1:
                    sp.wait_ge(unit_done, at_unit[("bn", 3)] + 1)
                else:
                    sp.wait_ge(unit_done, NU)
                load(0, 0, j)
            for j in range(RING):
                if j < EXTRA:
                    if j in (0, 1):
                        sp.wait_ge(pv_read, 16)
                    elif j == 2:
                        sp.wait_ge(unit_done, at_unit[("bs", 3)] + 1)
                    else:
                        sp.wait_ge(rt_full, 1)
                else:
                    sp.wait_ge(unit_done, NU + j + 1)
                load(1, 1, j)
            r = rounds(sp)
            with sp.Fori(1, r * EX2) as i:
                for s in range(2):
                    for j in range(RING):
                        if j < EXTRA:
                            sp.wait_ge(unit_done, i * (2 * RING) + (NU + (s - 2) * RING + j + 1))
                        else:
                            sp.wait_ge(unit_done, i * (2 * RING) + (NU + (s - 1) * RING + j + 1))
                        load((i % EX2) * 2 + s, s, j)
            sp.wait_ge(norm_ready, 1)
            sp.dma_start(out[0].rearrange("(t p) d -> p t d", p=P), RJ).then_inc(stored, 16)
            sp.wait_ge(stored, 16)

        @block.gpsimd
        def _(pool):
            own = Own(pool, pool_own)
            g = nc.gpsimd
            own.mark(g.memset(IDN[:], 0.0))
            own.mark(g.memset(UPP[:], 1.0))
            own.mark(g.memset(UST[:], 1.0))
            own.mark(g.memset(CM[:], 0.0))
            own.mark(g.memset(CMC[:], 0.0))
            own.mark(g.memset(HM[:], 0.5))
            own.mark(g.memset(ONE[:], 1.0))
            own.settle()
            own.mark(g.affine_select(out=IDN[:], in_=IDN[:], pattern=[[-1, P]], compare_op=ALU.not_equal,
                                     fill=1.0, base=0, channel_multiplier=1))
            own.settle()
            pool.sem_inc(const_done, 1)
            own.mark(g.affine_select(out=UPP[:], in_=UPP[:], pattern=[[1, P]], compare_op=ALU.is_ge,
                                     fill=0.0, base=0, channel_multiplier=-1))
            own.mark(g.affine_select(out=UST[:], in_=UST[:], pattern=[[1, P]], compare_op=ALU.is_gt,
                                     fill=0.0, base=0, channel_multiplier=-1))
            own.mark(g.affine_select(out=CM[:, P:256], in_=CM[:, P:256], pattern=[[-1, P]],
                                     compare_op=ALU.is_ge, fill=NEG, base=0, channel_multiplier=1))
            for t in range(T):
                own.mark(g.affine_select(out=CMC[:, t], in_=CMC[:, t], pattern=[[-CMP_STRIDE, 16]],
                                         compare_op=ALU.is_ge, fill=NEG, base=P * t - CMP_BLOCK + 1,
                                         channel_multiplier=1))
            own.mark(g.affine_select(out=HM[:], in_=HM[:], pattern=[[-16, 8]], compare_op=ALU.is_ge,
                                     fill=0.0, base=0, channel_multiplier=1))
            own.settle()
            own.mark(g.affine_select(out=HM[:], in_=HM[:], pattern=[[16, 8]], compare_op=ALU.is_ge,
                                     fill=0.0, base=15, channel_multiplier=-1))
            own.mark(g.iota(IOI[:], pattern=[[0, 2], [1, CAP]], base=0, channel_multiplier=0))
            own.settle()
            own.mark(g.tensor_copy(IOT[:], IOI[:]))
            own.settle()
            own.mark(g.iota(IOI[:, 0:EXPERTS], pattern=[[1, EXPERTS]], base=0, channel_multiplier=0))
            own.mark(g.iota(IOI[:, 64:67], pattern=[[CAP, 3]], base=CAP, channel_multiplier=0))
            own.settle()
            own.mark(g.tensor_copy(EIO[:], IOI[:, 0:EXPERTS]))
            own.mark(g.tensor_copy(TH3[:], IOI[:, 64:67]))
            for c in (EC, CTE):
                own.mark(g.memset(c[:], 0.0))
            own.mark(g.memset(BDK[:], 0.0))
            own.settle()
            pool.sem_inc(const_done, 1)

            for kind, k in TOKENS:
                if kind == "XD":
                    pool.wait_ge(th_used, 4)
                    pool.wait_ge(small_in, 16 * 8)
                    for j in range(8):
                        ins = g.tensor_scalar(YV[:, j], XC[:, j], DCOL[:, j:j + 1], None, ALU.mult)
                        if j == 7:
                            own.mark(ins)
                    own.settle()
                    pool.sem_inc(xd_done, 1)
                elif kind == "XT" and k < 2:
                    if k == 0:
                        pool.wait_ge(de_ready, 1)
                    pool.wait_ge(xdt_ready, k + 1)
                    g.tensor_tensor(part(XDT, 2048 + 512 * k, 8, DH), part(XDT, 512 * k, 8, DH),
                                    DE[:, 8 * k:8 * k + 8].unsqueeze(2).to_broadcast([P, 8, DH]),
                                    ALU.mult).then_inc(xde_ready, 1)
                elif kind == "A":
                    c, gr, b = k // 4, k % 4, k % 2
                    pool.wait_ge(e_exp, k + 1)
                    pool.wait_ge(gm_ready, k + 1)
                    ev = E[:, b].rearrange("p (r l) -> p r l", r=REP)
                    g.tensor_tensor(ev, ev, GM[:, b].unsqueeze(1).to_broadcast([P, REP, P]),
                                    ALU.mult).then_inc(m_done, 1)
                    if c == 1:
                        pool.wait_ge(ecs_done, k - 3)
                        if k >= 6:
                            pool.wait_ge(y_full, k - 1)
                        g.tensor_tensor(CTE[:, b].rearrange("p (r l) -> p r l", r=REP),
                                        EC[:, b].rearrange("p (r l) -> p r l", r=REP),
                                        XC[:, 12 + gr, P:2 * P].unsqueeze(1).to_broadcast([P, REP, P]),
                                        ALU.mult).then_inc(cte_done, 1)
                elif kind == "RW":
                    b, nk = k % 3, P * (k // 8 + 1)
                    pool.wait_ge(w_ready, k + 1)
                    v = SP[b][:, :, :, 0:nk]
                    g.tensor_tensor(v, v, AMX[:, b, 3].rearrange("p (h y) -> p h y", h=2).unsqueeze(3)
                                    .to_broadcast([P, 2, 2, nk]), ALU.mult).then_inc(p_ready, 1)
            pool.wait_ge(slot_ready, 1)
            own.mark(g.memset(YSB, 0.0))
            own.mark(g.memset(CTS[:, 1], 0.0))
            own.settle()
            pool.sem_inc(zero_ready, 1)

        @block.tensor
        def _(pe):
            mm = nc.tensor.matmul

            def tr(o, i):
                return nc.tensor.transpose(o, i, IDN[:, :])

            pe.wait_ge(const_done, 1)
            pe.wait_ge(rows_in, 16 * 6)
            tr(bank(4, P), PR[:]).then_inc(par_full, 1)
            for b in range(4):
                for kk in range(2):
                    for t in range(T):
                        if b == 0 and kk == 0:
                            pe.wait_ge(hn_ready, t + 1)
                        ins = tr(bank(b, 2, T, P)[:, kk, t], HN[:, t, P * (2 * b + kk):P * (2 * b + kk + 1)])
                ins.then_inc(ht_full, 1)
            pe.wait_ge(const_done, 2)

            def half_unit(u, half):
                kind, m = UNITS[u]
                b = bank_of[u]
                if half == 0:
                    if freed[u]:
                        pe.wait_ge(proj_free[b], freed[u])
                    if u == 0:
                        pe.wait_ge(ht_low, 1)
                    if kind == "bs" and m == 0:
                        pe.wait_ge(ys_ready, 1)
                    if kind == "bn" and m == 0:
                        pe.wait_ge(pv_read, 16)
                feature_major = kind in ("xbc", "kc", "vc", "ks", "kw", "q", "z")
                high, low = {"bs": (YSH, YSL), "bn": (OTH, OTL)}.get(kind, (HTH, HTL))
                rows = slice(P * half, P * half + P)
                nco = 64 if kind == "small" else 256
                i = SPLIT_UNITS.index(u)
                wh, wl = part(WH[i % SPLITS], 0, KT, nco), part(WL[i % SPLITS], 0, KT, nco)
                if half == 0:
                    pe.wait_ge(wh_ready, i + 1)
                for n, (w, src) in enumerate(((wh, high), (wh, low), (wl, high))):
                    if n == 2 and half == 0:
                        pe.wait_ge(wl_ready, i + 1)
                    for k in range(KT):
                        if half == 0 and n < 2 and k % 2 == 0 and u == 0:
                            pe.wait_ge((ht_act, ht_low)[n], k // 2 + 1)
                        if half == 0 and n < 2 and k % 2 == 0 and u == at_unit[("wo", 0)]:
                            pe.wait_ge((mt_ready, mt_low)[n], k // 2 + 1)
                        if feature_major:
                            ins = mm(bank(b, 2, SEQ)[:, half], w[:, k, rows], src[:, k, :],
                                     start=(n == 0 and k == 0), stop=(n == 2 and k == KT - 1))
                        else:
                            ins = mm(bank(b, 2, nco)[:, half], src[:, k, rows], w[:, k, :],
                                     start=(n == 0 and k == 0), stop=(n == 2 and k == KT - 1))
                if half == 1:
                    ins.then_inc(unit_done, 1)

            for kind, k in TOKENS:
                if kind == "H":
                    half_unit(k, 0)
                elif kind == "P":
                    half_unit(k, 1)
                elif kind == "S1":
                    pe.wait_ge(adt_ready, 1)
                    pe.wait_ge(par_ready, 1)
                    mm(bank(4, 16), UPP[:], ADT[:, 0], start=True, stop=True)
                    mm(bank(4, 16, off=16), UPP[:], ADT[:, 1], start=True, stop=True)
                    mm(bank(4, 16, off=32), ONE[:], ADT[:, 0], start=True, stop=True).then_inc(s1_full, 1)
                elif kind == "XT":
                    c, half = k // 2, k % 2
                    if k in (1, 3):
                        pe.wait_ge(xdt_ready, k)
                    if k == 2:
                        pe.wait_ge(bt_ready, 1)
                    for j in range(4):
                        ins = tr(bank(5, 4, P)[:, j], XC[:, 4 * half + j, P * c:P * c + P])
                    ins.then_inc(xt_full, 1)
                elif kind == "BT":
                    pe.wait_ge(xdt_ready, 2)
                    for j in range(4):
                        ins = tr(bank(5, 4, P)[:, j], XC[:, 8 + j, 0:P])
                    ins.then_inc(xt_full, 1)
                elif kind == "HID":
                    pe.wait_ge(kcp_ready, 4)
                    for kv in ("w1k", "w1v"):
                        pe.wait_ge(ring_full[at_unit[(kv, 0)] % STREAM], full_at[at_unit[(kv, 0)]])
                    for j in range(16):
                        for kv, src in ((0, KCP), (1, VCP)):
                            w1 = slot_view(at_unit[("w1v" if kv else "w1k", 0)], 16, P)
                            ins = mm(psum[64 * kv:64 * kv + 64, 7, 0:P], src[:, j // 8, :, j % 8], w1[:, j],
                                     start=(j == 0), stop=(j == 15))
                            if j == 15:
                                ins.then_inc(unit_done, 1)
                elif kind == "HT":
                    pe.wait_ge(hid_act, 1)
                    tr(bank(7, P, off=P), HIDT[:, 4]).then_inc(hid_full, 1)
                elif kind == "K2":
                    pe.wait_ge(hid_ready, 1)
                    mm(bank(7, 64, off=256), W2K[:].rearrange("p a b -> p (a b)"),
                       HID[:, 0].rearrange("p a b -> p (a b)"), start=True, stop=True).then_inc(k2_full, 1)
                elif kind == "V2":
                    pe.wait_ge(hvr_ready, 1)
                    pe.wait_ge(y_read, 8)
                    for hb in range(2):
                        lhs = HVR[:, hb].rearrange("p g r c -> p (g r c)")
                        ins = mm(bank(6, 64, off=128 + 64 * hb), lhs, W2V[:], start=True, stop=True)
                    ins.then_inc(v2_full, 1)
                elif kind == "A":
                    c, gr = k // 4, k % 4
                    if k == 0:
                        pe.wait_ge(cs_ready, 1)
                    else:
                        pe.wait_ge(csb_read, k)
                        pe.wait_ge(gm_ready, k)
                    if k >= 5:
                        pe.wait_ge(ecs_done, k - 4)
                    for r in range(REP):
                        mm(bank(3, REP, P)[:, r], ADT[:, c, REP * gr + r:REP * gr + r + 1].to_broadcast([P, P]),
                           UPP[:], start=True, stop=True)
                    mm(bank(4, P), XC[:, 8 + gr, P * c:P * c + P], XC[:, 12 + gr, P * c:P * c + P],
                       start=True, stop=True).then_inc(a_full, 1)
                elif kind == "ST":
                    pe.wait_ge(xde_ready, k + 1)
                    if k == 0:
                        pe.wait_ge(bt_ready, 1)
                        pe.wait_ge(k2_ready, 1)
                    else:
                        pe.wait_ge(st_ready, 1)
                    for j in range(2):
                        gr = 2 * k + j
                        ins = mm(bank(7, 2, 256)[:, j], BTK[:, gr], part(XDT, 2048 + 256 * gr, 256),
                                 start=True, stop=True)
                    ins.then_inc(st_full, 1)
                elif kind == "Y":
                    c, gr, b = k // 4, k % 4, k % 2
                    pe.wait_ge(m_done, k + 1)
                    if c == 0:
                        pe.wait_ge(xdt_ready, 2)
                    else:
                        pe.wait_ge(xdt_ready, 4)
                        pe.wait_ge(cte_done, k - 3)
                        pe.wait_ge(st_ready, 2)
                    if k:
                        pe.wait_ge(y_read, k)
                    for jj in range(2):
                        for hh in range(2):
                            r = 2 * jj + hh
                            h = REP * gr + r
                            o = psum[64 * hh:64 * hh + 64, 6, P * jj:P * jj + P]
                            ins = mm(o, part(XDT, D * c + DH * h, DH), E[:, b, P * r:P * r + P],
                                     start=True, stop=(c == 0))
                            if c == 1:
                                ins = mm(o, ST[:, DH * h:DH * h + DH], CTE[:, b, P * r:P * r + P],
                                         start=False, stop=True)
                    ins.then_inc(y_full, 1)
                elif kind == "GN":
                    pe.wait_ge(sq_ready, k + 1)
                    if k == 0:
                        pe.wait_ge(v2_ready, 1)
                    else:
                        pe.wait_ge(rb_ready, k)
                    mm(bank(6, SEQ), ONE[:], SQ[:, k % 2, 0:SEQ], start=True, stop=False)
                    mm(bank(6, SEQ), ONE[:], SQ[:, k % 2, SEQ:2 * SEQ], start=False, stop=True
                       ).then_inc(gn_full, 1)
                elif kind == "CS":
                    pe.wait_ge(csr_ready, 1)
                    for t in range(T):
                        for q in range(2):
                            ins = tr(bank(5, P, off=256 * t + P * q), CSR[:, 256 * q + P * t:256 * q + P * t + P])
                    ins.then_inc(cs_full, 1)
                elif kind == "CT":
                    for m in range(4):
                        taken(pe, "q", m)
                    pe.wait_ge(k2_ready, 1)
                    pe.wait_ge(xdt_ready, 4)
                    for q in range(2):
                        for j4 in range(4):
                            j = 4 * q + j4
                            ins = mm(psum[32 * j4:32 * j4 + 32, 5, 256 * q:256 * q + 256],
                                     BDK[:, j // 2].rearrange("p a b -> p (a b)"), QT[:, j, :],
                                     start=True, stop=True, tile_position=(0, 32 * j4))
                    ins.then_inc(csr_full, 1)
                elif kind == "CP":
                    pe.wait_ge(cp_ready, 1)
                    for t in range(T):
                        for hb in range(2):
                            ins = tr(bank(5, T, 2, P)[:, t, hb], PCS[:, t, 8 * hb:8 * hb + 8]
                                     .rearrange("p a b -> p (a b)"))
                    ins.then_inc(cp_full, 1)
                elif kind == "SC":
                    t, j = k // 8, k % 8
                    if k == 0:
                        pe.wait_ge(gm_ready, 8)
                        pe.wait_ge(ecs_done, 4)
                        pe.wait_ge(csb_read, 8)
                        taken(pe, "ks")
                        taken(pe, "kw")
                    else:
                        pe.wait_ge(nm_ready, k)
                    nk = P * (t + 1)
                    for y in range(2):
                        for hh in range(2):
                            s = slice(64 * hh, 64 * hh + 64)
                            ins = mm(psum[:, 3 + hh, 256 * y:256 * y + nk], QT[s, j, P * t:P * t + P],
                                     KD[s, y, j // 2, 0:nk], start=True, stop=True)
                    ins.then_inc(sc_full, 1)
                elif kind == "PT":
                    t = k // 8
                    pe.wait_ge(p_ready, k + 1)
                    if k == 0:
                        pe.wait_ge(cp_read, 1)
                        pe.wait_ge(rb_ready, 4)
                    else:
                        pe.wait_ge(pt_act, k)
                        pe.wait_ge(pt_dve, k)
                    for hh in range(2):
                        for y in range(2):
                            for bl in range(t + 1):
                                ins = tr(bank(5 + hh, P, off=P * (y * (t + 1) + bl)),
                                         SP[k % 3][:, hh, y, P * bl:P * bl + P])
                    ins.then_inc(pt_full, 1)
                elif kind == "PV":
                    t, j = k // 8, k % 8
                    if k == 0:
                        taken(pe, "vs")
                        taken(pe, "vw")
                        pe.wait_ge(v2_ready, 1)
                        pe.wait_ge(st_ready, 2)
                        pe.wait_ge(gy_ready, 4)
                    else:
                        pe.wait_ge(pv_read, k)
                    pe.wait_ge(pt_act, k + 1)
                    pe.wait_ge(pt_dve, k + 1)
                    mm(bank(7, P), VBD[:, j // 4, 2 * (j % 4):2 * (j % 4) + 2].rearrange("p a b -> p (a b)"),
                       PCT[:, t, j // 4], start=True, stop=False, skip_group_check=True)
                    for y in range(2):
                        for bl in range(t + 1):
                            for hh in range(2):
                                last = y == 1 and bl == t
                                ins = mm(psum[64 * hh:64 * hh + 64, 7, 0:P],
                                         VT[:, y, bl, DH * (j // 2):DH * (j // 2) + DH],
                                         PTS[:, hh, P * (y * (t + 1) + bl):P * (y * (t + 1) + bl) + P],
                                         start=False, stop=last, skip_group_check=True)
                    ins.then_inc(pv_full, 1)
                elif kind == "MT":
                    pe.wait_ge(mg_ready, k + 1)
                    if k >= 2:
                        pe.wait_ge(mt_low, k - 1)
                    for kk in range(2):
                        for t in range(T):
                            ins = tr(bank(3 + k % 2, 2, T, P)[:, kk, t],
                                     MG[:, t, P * (2 * k + kk):P * (2 * k + kk) + P])
                    ins.then_inc(mt_full, 1)

            pe.wait_ge(h2_ready, 2)
            for b in range(4):
                for kk in range(2):
                    for t in range(T):
                        ins = tr(bank(3 + b, 2, T, P)[:, kk, t], H2[:, t, P * (2 * b + kk):P * (2 * b + kk + 1)])
                ins.then_inc(h2t_full, 1)
            pe.wait_ge(h2t_act, 2)
            pe.wait_ge(h2t_dve, 2)
            pe.wait_ge(late_in, 16 * 5)
            for t in range(T):
                for k in range(KT):
                    ins = mm(bank(7, EXPERTS, off=EXPERTS * t), H2T[:, k, P * t:P * t + P], RW_[:, k, :],
                             start=(k == 0), stop=(k == KT - 1))
            ins.then_inc(rt_full, 1)
            pe.wait_ge(msk_ready, 1)
            mm(bank(3, EXPERTS), UST[:], MSK[:, 0], start=True, stop=True)
            mm(bank(3, EXPERTS, off=32), ONE[:], MSK[:, 0], start=True, stop=False)
            mm(bank(3, EXPERTS, off=32), UST[:], MSK[:, 1], start=False, stop=True)
            mm(bank(3, EXPERTS, off=64), ONE[:], MSK[:, 0], start=True, stop=False)
            mm(bank(3, EXPERTS, off=64), ONE[:], MSK[:, 1], start=False, stop=True).then_inc(rk_full, 1)
            for t in range(T):
                ins = tr(bank(4, T, P)[0:EXPERTS, t], CW[:, t])
            ins.then_inc(cwt_full, 1)
            def gather():
                for k in range(KT):
                    for t in range(T):
                        ins = mm(bank(5 + k // 4, P, off=P * (k % 4)), H2[:, t, P * k:P * k + P],
                                 SPR[:, t].rearrange("p a b -> p (a b)"), start=(t == 0), stop=(t == T - 1))
                ins.then_inc(xte_full, 1)

            def combine(n, s):
                pe.wait_ge(o_read, n * 2 + 1)
                for t in range(T):
                    for h in range(2):
                        r = slice(64 * h, 64 * h + 64)
                        ins = mm(psum[:, 3 + 2 * t + h, :], CTS[r, 1 - s, t], YSB[r, :], start=True, stop=True)
                    ins.then_inc(o_full, 1)

            pe.wait_ge(prep_done, 1)
            gather()
            pe.wait_ge(cwt_full, 2)
            for t in range(T):
                if t:
                    pe.wait_ge(acc_ready, t)
                for h in range(2):
                    ins = mm(psum[:, 3 + h, :], CWT[0:EXPERTS, t], BDN[0:EXPERTS, 512 * h:512 * h + 512],
                             start=True, stop=True)
                ins.then_inc(bd_full, 1)
            pe.wait_ge(zero_ready, 1)
            r = rounds(pe)
            with pe.Fori(0, r * EX2) as i:
                for s in range(2):
                    n = i * 2 + s
                    if s == 0:
                        pe.wait_ge(xte_ready, i + 1)
                        pe.wait_ge(prep_done, i + 1)
                    pe.wait_ge(gu_read, n + 1)
                    for c in range(4):
                        mm(psum[64 * (c % 2):64 * (c % 2) + 64, c // 2, :], OHE[0:EXPERTS, s],
                           BGU[0:EXPERTS, 512 * c:512 * c + 512], start=True, stop=False)
                    for k in range(KT):
                        if k >= EXTRA:
                            w = part(ring, k * SLOT, SLOT)
                            pe.wait_ge(ring_full[k], n * 16 + (slot_total[k] + 16))
                        elif s == 0:
                            w = part(ring, k * SLOT, SLOT)
                            pe.wait_ge(ring_full[k], i * 16 + (slot_total[k] + 16))
                        else:
                            w = extra[k]
                            pe.wait_ge(extra_full[k], i * 16 + 16)
                        for c in range(4):
                            ins = mm(psum[64 * (c % 2):64 * (c % 2) + 64, c // 2, :], XTS[:, k, s],
                                     w[:, 512 * c:512 * c + 512], start=False, stop=(k == KT - 1))
                        ins.then_inc(unit_done, 1)
                    pe.wait_ge(at_ready, n + 1)
                    for t in range(T):
                        ins = tr(bank(7, T, P)[:, t], CPR[:, t, s])
                    ins.then_inc(ct_full, 1)
                    pe.wait_ge(y_ready, n + 1)
                    combine(n, s)
                    pe.wait_ge(act_ready, n + 1)
                    pe.wait_ge(ct_ready, n + 1)
                    for jb in range(4):
                        ins = tr(bank(7, 4, P)[:, jb], ABU[:, P * jb:P * jb + P])
                    ins.then_inc(at_full, 1)
                    pe.wait_ge(at_ready, n + 2)
                    for k in range(KT):
                        slot = 8 + k // 2
                        if s == 1 and k == 4:
                            pe.wait_ge(prep_done, i + 2)
                            pe.wait_ge(o_read, n * 2 + 3)
                            gather()
                        if k % 2 == 0:
                            pe.wait_ge(ring_full[slot], n * 16 + (slot_total[slot] + 16))
                        q, hf = k // 4, (k // 2) % 2
                        lhs = ATS[:, 2 * q + k % 2, 64 * hf:64 * hf + 64]
                        for h in range(2):
                            ins = mm(psum[64 * h:64 * h + 64, 2, :], lhs,
                                     ring[:, slot, 1024 * (k % 2) + 512 * h:1024 * (k % 2) + 512 * h + 512],
                                     start=(k == 0), stop=(k == KT - 1))
                        if k % 2:
                            ins.then_inc(unit_done, 1)
            pe.wait_ge(y_ready, r * EXPERTS + 1)
            pe.wait_ge(ct_ready, r * EXPERTS)
            combine(r * EXPERTS, 0)

        @block.scalar
        def _(act):
            own = Own(act, act_own)
            a = nc.scalar.activation
            rows = [(mix_norm_w, 8), (ssm_norm_w, 8), (conv_b, 16), (conv_w, 64), (cmp_pos_k, 16),
                    (cmp_pos_v, 16)]
            at = 0
            for w, nrow in rows:
                flat = w[0] if len(w.shape) == 2 else w[0].rearrange("a b -> (a b)")
                act.dma_start(PR[at:at + nrow, :], flat.rearrange("(a b) -> a b", b=P)).then_inc(rows_in, 16)
                at += nrow
            act.dma_start(DTB[:], dt_bias[0].partition_broadcast(P)).then_inc(small_in, 16)
            act.dma_start(ALG[:], a_log[0].partition_broadcast(P)).then_inc(small_in, 16)
            dcol = d_skip[0].rearrange("(j two) -> two j", two=2)
            for hh in range(2):
                act.dma_start(DCOL[64 * hh:64 * hh + 64, :], dcol[hh].partition_broadcast(64),
                              allow_slow_non_contiguous=True).then_inc(small_in, 16)
            act.dma_start(W2K[:, 0], cmp_w2_k[0]).then_inc(small_in, 16)
            act.dma_start(W2K[:, 1], cmp_w2_k[0]).then_inc(small_in, 16)
            act.dma_start(W2V[:], cmp_w2_v[0]).then_inc(small_in, 16)
            act.dma_start(RB[:], router_b[0].partition_broadcast(P)).then_inc(small_in, 16)

            act.wait_ge(x_in, 16)
            for t in range(T):
                a(part(YV, D * t, D), X[:, t], ACT.Square, accum_out=ss[:, t:t + 1]).then_inc(ss_ready, 1)
            act.wait_ge(dve_own, 1)
            a(ss[:, 2:4], ss[:, 0:2], ACT.Sqrt).then_inc(sq_root, 1)

            def split(u):
                i = SPLIT_UNITS.index(u)
                act.wait_ge(ring_full[u % STREAM], full_at[u])
                if i >= SPLITS:
                    act.wait_ge(unit_done, SPLIT_UNITS[i - SPLITS] + 1)
                n = KT * (64 if UNITS[u][0] == "small" else 256)
                a(WH[i % SPLITS][:, 0:n], slot_view(u, n), ACT.Copy).then_inc(wh_ready, 1)

            split(0)
            act.wait_ge(par_ready, 1)
            for b in range(4):
                act.wait_ge(ht_full, b + 1)
                for kk in range(2):
                    ins = a(HTH[:, 2 * b + kk], bank(b, 2, SEQ)[:, kk], ACT.Copy,
                            scale=PC[:, 2 * b + kk:2 * b + kk + 1])
                ins.then_inc(ht_act, 1)
            split(1)

            n_th = 0
            for kind, k in TOKENS:
                if kind == "W":
                    split(k)
                elif kind == "YS":
                    act.wait_ge(yn_ready, 4)
                    a(YSH[:], YV[:], ACT.Copy).then_inc(ys_high, 1)
                elif kind == "P":
                    what, m = UNITS[k]
                    if what in ("w1k", "w1v", "small", "vs", "bs", "bn", "wo"):
                        continue
                    b = bank_of[k]
                    pv = bank(b, 2, SEQ)
                    act.wait_ge(unit_done, k + 1)
                    if what == "xbc":
                        for f in range(2):
                            ch = 2 * m + f
                            ins = a(XC[:, ch], pv[:, f], ACT.Identity, scale=PH[:, 16 + 48 + ch:16 + 49 + ch],
                                    bias=PH[:, ch:ch + 1])
                        ins.then_inc(hv_done, 1)
                    elif what in ("kc", "ks", "vc", "kw"):
                        if what in ("ks", "kw"):
                            y = 0 if what == "ks" else 1
                            for f in range(2):
                                for src in range(2):
                                    s = slice(64 * src, 64 * src + 64)
                                    a(KD[64 * src:64 * src + 64, y, 2 * f + src], pv[s, f], ACT.Copy)
                                    ins = a(KD[64 * (1 - src):64 * (1 - src) + 64, y, 2 * f + src], pv[s, f],
                                             ACT.Copy)
                            ins.then_inc(proj_free[b], 1)
                        else:
                            dst = KC2 if what == "kc" else VC2
                            for f in range(2):
                                for src in range(2):
                                    s = slice(64 * src, 64 * src + 64)
                                    a(dst[0:64, 2 * f + src, :], pv[s, f], ACT.Copy)
                                    ins = a(dst[64:128, 2 * f + src, 0:SEQ - 1], pv[s, f, 1:SEQ], ACT.Copy)
                            ins.then_inc(proj_free[b], 1)
                    elif what == "vw":
                        a(VT[:, 1], pv, ACT.Copy).then_inc(proj_free[b], 1)
                    elif what == "q":
                        a(QT[:, 2 * m:2 * m + 2], pv, ACT.Copy).then_inc(proj_free[b], 1)
                    elif what == "z":
                        if n_th >= 2:
                            act.wait_ge(th_used, n_th - 1)
                        a(TH[:, n_th % 2], psum[:, b], ACT.Tanh, scale=0.5).then_inc(th_ready, 1)
                        n_th += 1
                    elif what == "mg":
                        if m == 0:
                            act.wait_ge(y_full, 8)
                            act.wait_ge(cte_done, 4)
                        a(GA[:, :, 256 * m:256 * m + 256], pv, ACT.Tanh, scale=0.5).then_inc(proj_free[b], 1)
                elif kind == "F":
                    if n_th >= 2:
                        act.wait_ge(th_used, n_th - 1)
                    b = bank_of[k]
                    act.wait_ge(proj_free[b], freed[k] + 1)
                    a(TH[:, n_th % 2], XC[:, 2 * k:2 * k + 2].rearrange("p a b -> p (a b)"), ACT.Tanh
                      ).then_inc(th_ready, 1)
                    n_th += 1
                elif kind == "DT":
                    taken(act, "small")
                    own.mark(a(NG[:], SM[:, :, 16:64], ACT.Tanh, scale=0.5))
                    act.wait_ge(small_in, 16 * 8)
                    own.mark(a(ALG[:], ALG[:], ACT.Exp))
                    act.wait_ge(dt_e, 1)
                    a(DT[:, 2], DT[:, 1], ACT.Exp, scale=-1.0).then_inc(dt_w, 1)
                    act.wait_ge(dt_e, 2)
                    a(DT[:, 4], DT[:, 3], ACT.Ln).then_inc(dt_l, 1)
                    act.wait_ge(dt_l, 1)
                elif kind == "S1":
                    act.wait_ge(cs_ready, 1)
                    a(DE[:], DE[:], ACT.Exp).then_inc(de_ready, 1)
                elif kind == "HID":
                    act.wait_ge(hid_t3, 1)
                    a(HIDT[:, 3], HIDT[:, 2], ACT.Tanh, scale=0.7978845608028654).then_inc(hid_th, 1)
                elif kind == "A":
                    act.wait_ge(csb_read, k + 1)
                    a(E[:, k % 2], E[:, k % 2], ACT.Exp).then_inc(e_exp, 1)
                    if k >= 4:
                        if k >= 6:
                            act.wait_ge(cte_done, k - 5)
                        a(EC[:, k % 2], psum[:, 3], ACT.Exp).then_inc(ecs_done, 1)
                elif kind == "GY":
                    act.wait_ge(gy_ready, k + 1)
                    if k == 0:
                        act.wait_ge(cte_done, 4)
                    if k == 1:
                        act.wait_ge(cs_full, 1)
                    if k >= 2:
                        act.wait_ge(gn_full, k - 1)
                    a(SQ[:, k % 2], YV[:, 2 * k:2 * k + 2].rearrange("p a b -> p (a b)"), ACT.Square
                      ).then_inc(sq_ready, 1)
                elif kind == "GN":
                    act.wait_ge(gn_full, k + 1)
                    own.mark(a(CTE[:, k % 2, 0:SEQ], bank(6, SEQ), ACT.Ln, scale=0.25 / 256, bias=ss[:, 6:7]))
                    own.settle()
                    a(CTE[:, k % 2, SEQ:2 * SEQ], CTE[:, k % 2, 0:SEQ], ACT.Exp, scale=-0.5).then_inc(rb_ready, 1)
                elif kind == "CT":
                    act.wait_ge(csr_full, 1)
                    act.wait_ge(cte_done, 4)
                    act.wait_ge(y_full, 8)
                    a(CSR, psum[:, 5], ACT.Copy).then_inc(csr_ready, 1)
                elif kind == "CS":
                    act.wait_ge(cs_sub, 1)
                    a(PCS[:], PCS[:], ACT.Exp).then_inc(cs_exp, 1)
                elif kind == "CP":
                    act.wait_ge(cp_full, 1)
                    a(PCT[:], bank(5, T, 2, P), ACT.Copy).then_inc(cp_read, 1)
                elif kind == "SC":
                    b, nk = k % 3, P * (k // 8 + 1)
                    act.wait_ge(nm_ready, k + 1)
                    for hh in range(2):
                        for y in range(2):
                            q = 2 * hh + y
                            ins = a(SP[b][:, hh, y, 0:nk], SP[b][:, hh, y, 0:nk], ACT.Exp,
                                    bias=AMX[:, b, 1, q:q + 1], accum_out=AMX[:, b, 2, q:q + 1])
                    ins.then_inc(ex_done, 1)
                elif kind == "PT":
                    n = 2 * P * (k // 8 + 1)
                    act.wait_ge(pt_full, k + 1)
                    if k >= 1:
                        act.wait_ge(pv_full, k)
                    a(PTS[:, 0, 0:n], psum[:, 5, 0:n], ACT.Copy).then_inc(pt_act, 1)
                elif kind == "PV":
                    t, j = k // 8, k % 8
                    act.wait_ge(pv_full, k + 1)
                    a(OTH[:, j, P * t:P * t + P], bank(7, P), ACT.Copy).then_inc(ot_high, 1)
                elif kind == "MT":
                    act.wait_ge(mt_full, k + 1)
                    a(HTH[:, 2 * k:2 * k + 2].rearrange("p a b -> p (a b)"), psum[:, 3 + k % 2], ACT.Copy,
                      scale=0.5).then_inc(mt_ready, 1)

            act.wait_ge(mg_ready, 4)
            act.wait_ge(unit_done, NU - 4)
            act.dma_start(RW_, router_w[0].rearrange("(k p) e -> p k e", p=P)).then_inc(late_in, 16)
            act.dma_start(WFF, ffn_norm_w[0].partition_broadcast(P)).then_inc(late_in, 16)
            act.dma_start(WFN, final_norm_w.partition_broadcast(P)).then_inc(late_in, 16)
            act.dma_start(BGU[0:EXPERTS, :], b_gate_up[0]).then_inc(late_in, 16)
            act.dma_start(BDN[0:EXPERTS, :], b_down[0]).then_inc(late_in, 16)

            act.wait_ge(x2_ready, 4)
            for t in range(T):
                a(SQX[:, t], X[:, t], ACT.Square, accum_out=ss[:, t:t + 1]).then_inc(ss_ready, 1)
            act.wait_ge(lg_ready, 1)
            a(ss[:, 2:4], ss[:, 0:2], ACT.Sqrt).then_inc(sq_root, 1)
            for b in (0, 2):
                act.wait_ge(h2t_full, b + 1)
                a(H2T[:, 2 * b:2 * b + 2].rearrange("p a b -> p (a b)"), psum[:, 3 + b], ACT.Copy
                  ).then_inc(h2t_act, 1)
            act.wait_ge(mx_ready, 1)
            for t in range(T):
                ins = a(RT[:, 2, t, 0:TOPK], MX8[:, t, 0:TOPK], ACT.Exp, bias=RT[:, 1, t, 0:1],
                        accum_out=RT[:, 3, t, 0:1])
            ins.then_inc(te_ready, 1)

            def tokens_in():
                for b in range(2):
                    ins = a(XTS[:, 4 * b:4 * b + 4].rearrange("p a b c -> p (a b c)"), psum[:, 5 + b], ACT.Copy)
                ins.then_inc(xte_ready, 1)

            act.wait_ge(xte_full, 1)
            tokens_in()
            act.wait_ge(zero_ready, 1)
            act.sem_inc(y_ready, 1)
            act.sem_inc(at_ready, 1)
            r = rounds(act)
            with act.Fori(0, r * EX2) as i:
                for s in range(2):
                    n = i * 2 + s
                    act.wait_ge(ct_full, n + 1)
                    a(CTS[:, s], bank(7, T, P), ACT.Copy).then_inc(ct_ready, 1)
                    act.wait_ge(g_ready, n + 1)
                    a(SGA, GBU, ACT.Sigmoid, scale=1.702).then_inc(sig_ready, 1)
                    act.wait_ge(at_full, n + 1)
                    a(ATS.rearrange("p a b -> p (a b)"), psum[:, 7], ACT.Copy).then_inc(at_ready, 1)
                    if s == 1:
                        act.wait_ge(xte_full, i + 2)
                        tokens_in()
                    act.wait_ge(unit_done, n * RING + (NU + RING))
                    a(YSB, psum[:, 2], ACT.Copy).then_inc(y_ready, 1)
            act.wait_ge(final_in, 1)
            for t in range(T):
                a(SQX[:, t], X[:, t], ACT.Square, accum_out=ss[:, t:t + 1]).then_inc(ss_ready, 1)
            act.wait_ge(lg_ready, 3)
            a(ss[:, 2:4], ss[:, 0:2], ACT.Sqrt).then_inc(sq_root, 1)

        @block.vector
        def _(dve):
            own = Own(dve, dve_own)
            v = nc.vector

            def inv_rms(n, done):
                dve.wait_ge(ss_ready, 2 * n)
                done(v.tensor_scalar(ss[:, 0:2], ss[:, 0:2], 1.0 / D, EPS, ALU.mult, ALU.add))
                dve.wait_ge(sq_root, n)
                own.mark(v.reciprocal(ss[:, 4:6], ss[:, 2:4]))
                own.settle()

            inv_rms(1, own.mark)
            for t in range(T):
                v.tensor_scalar(HN[:, t], X[:, t], ss[:, 4 + t:5 + t], None, ALU.mult).then_inc(hn_ready, 1)
            own.mark(v.memset(ss[:, 6:7], EPS))
            dve.wait_ge(par_full, 1)
            own.mark(v.tensor_copy(PC[:], bank(4, P)))
            own.settle()
            own.mark(v.tensor_scalar(PH[:, 0:80], PC[:, 16:96], 0.5, None, ALU.mult))
            own.mark(v.tensor_scalar(PH[:, 80:88], PC[:, 8:16], 0.5, None, ALU.mult))
            own.settle()
            dve.sem_inc(par_ready, 1)

            def split(u):
                i = SPLIT_UNITS.index(u)
                dve.wait_ge(wh_ready, i + 1)
                n = KT * (64 if UNITS[u][0] == "small" else 256)
                v.tensor_tensor(WL[i % SPLITS][:, 0:n], slot_view(u, n), WHF[i % SPLITS][:, 0:n], ALU.subtract
                                ).then_inc(wl_ready, 1)

            for b in range(4):
                dve.wait_ge(ht_act, b + 1)
                for kk in range(2):
                    j = 2 * b + kk
                    ins = v.scalar_tensor_tensor(out=HTL[:, j], in0=bank(b, 2, SEQ)[:, kk],
                                                 scalar=PC[:, j:j + 1], in1=HTHF[:, j], op0=ALU.mult,
                                                 op1=ALU.subtract)
                ins.then_inc(ht_low, 1)
            split(0)
            split(1)

            n_th = 0
            for kind, k in TOKENS:
                if kind == "W":
                    split(k)
                elif kind == "YS":
                    dve.wait_ge(ys_high, 1)
                    v.tensor_tensor(YSL[:], YV[:], YSHF, ALU.subtract).then_inc(ys_ready, 1)
                elif kind == "PV":
                    t, j = k // 8, k % 8
                    dve.wait_ge(ot_high, k + 1)
                    v.tensor_tensor(OTL[:, j, P * t:P * t + P], bank(7, P), OTHF[:, j, P * t:P * t + P],
                                    ALU.subtract).then_inc(pv_read, 1)
                elif kind == "MT":
                    dve.wait_ge(mt_ready, k + 1)
                    v.scalar_tensor_tensor(out=HTL[:, 2 * k:2 * k + 2].rearrange("p a b -> p (a b)"),
                                           in0=psum[:, 3 + k % 2], scalar=0.5,
                                           in1=HTHF[:, 2 * k:2 * k + 2].rearrange("p a b -> p (a b)"),
                                           op0=ALU.mult, op1=ALU.subtract).then_inc(mt_low, 1)
                elif kind == "P":
                    what, m = UNITS[k]
                    if what in ("w1k", "w1v", "kc", "vc", "ks", "kw", "vw", "q", "mg"):
                        continue
                    b = bank_of[k]
                    pv = bank(b, 2, SEQ)
                    dve.wait_ge(unit_done, k + 1)
                    if what == "xbc":
                        dve.wait_ge(hv_done, m + 1)
                        for tap in (2, 1, 0):
                            back = 3 - tap
                            for f in range(2):
                                ch = 2 * m + f
                                w = PH[:, 16 + 16 * tap + ch:17 + 16 * tap + ch]
                                o = XC[:, ch, back:SEQ]
                                ins = v.scalar_tensor_tensor(out=o, in0=pv[:, f, 0:SEQ - back], scalar=w,
                                                             in1=o, op0=ALU.mult, op1=ALU.add)
                                if not (tap == 0 and f == 1):
                                    own.mark(ins)
                                else:
                                    ins.then_inc(proj_free[b], 1)
                                if f == 1 and tap:
                                    own.settle()
                    elif what == "small":
                        v.tensor_copy(SM[:], bank(b, T, 64)).then_inc(proj_free[b], 1)
                    elif what == "vs":
                        v.tensor_copy(VT[:, 0], pv).then_inc(proj_free[b], 1)
                    elif what == "z":
                        dve.wait_ge(th_ready, n_th + 1)
                        zs = ZS[:, 2 * m:2 * m + 2].rearrange("p a b -> p (a b)")
                        own.mark(v.scalar_tensor_tensor(out=zs, in0=TH[:, n_th % 2], scalar=1.0,
                                                        in1=psum[:, b], op0=ALU.add, op1=ALU.mult))
                        own.settle()
                        dve.sem_inc(proj_free[b], 1)
                        dve.sem_inc(th_used, 1)
                        n_th += 1
                    elif what == "bs":
                        v.scalar_tensor_tensor(out=GA[:, :, 256 * m:256 * m + 256],
                                               in0=GA[:, :, 256 * m:256 * m + 256], scalar=1.0, in1=pv,
                                               op0=ALU.add, op1=ALU.mult).then_inc(proj_free[b], 1)
                    elif what == "bn":
                        ga = GA[:, :, D + 256 * m:D + 256 * m + 256]
                        v.scalar_tensor_tensor(out=ga, in0=ga, scalar=1.0, in1=pv,
                                               op0=ALU.add, op1=ALU.mult).then_inc(proj_free[b], 1)
                        dve.wait_ge(proj_free[b], freed[k] + 1)
                        mg = MG[:, :, 256 * m:256 * m + 256]
                        v.tensor_tensor(mg, mg, ga, ALU.add).then_inc(mg_ready, 1)
                    elif what == "wo":
                        xo = X[:, :, 256 * m:256 * m + 256]
                        v.tensor_tensor(xo, xo, pv, ALU.add).then_inc(x2_ready, 1)
                        dve.wait_ge(x2_ready, m + 1)
                        dve.sem_inc(proj_free[b], 1)
                elif kind == "F":
                    dve.wait_ge(th_ready, n_th + 1)
                    dve.wait_ge(proj_free[bank_of[k]], freed[k] + 1)
                    xc = XC[:, 2 * k:2 * k + 2].rearrange("p a b -> p (a b)")
                    v.scalar_tensor_tensor(out=xc, in0=TH[:, n_th % 2], scalar=1.0, in1=xc, op0=ALU.add,
                                           op1=ALU.mult).then_inc(th_used, 1)
                    n_th += 1
                elif kind == "DT":
                    taken(dve, "small")
                    dve.wait_ge(small_in, 16 * 8)
                    b16 = [P, T, HEADS]
                    own.mark(v.tensor_tensor(DT[:, 0], SM[:, :, 0:16], DTB[:].unsqueeze(1).to_broadcast(b16), ALU.add))
                    own.settle()
                    own.mark(v.tensor_scalar(DT[:, 5], DT[:, 0], -1.0, None, ALU.mult))
                    own.settle()
                    v.tensor_tensor(DT[:, 1], DT[:, 0], DT[:, 5], ALU.max).then_inc(dt_e, 1)
                    dve.wait_ge(dt_w, 1)
                    v.tensor_scalar(DT[:, 3], DT[:, 2], 1.0, None, ALU.add).then_inc(dt_e, 1)
                    dve.wait_ge(dt_e, 2)
                    own.mark(v.scalar_tensor_tensor(out=DT[:, 6], in0=DT[:, 3], scalar=-1.0, in1=DT[:, 2],
                                                    op0=ALU.add, op1=ALU.subtract))
                    own.mark(v.reciprocal(DT[:, 7], DT[:, 3]))
                    own.settle()
                    own.mark(v.tensor_tensor(DT[:, 6], DT[:, 6], DT[:, 7], ALU.mult))
                    dve.wait_ge(dt_l, 1)
                    own.settle()
                    own.mark(v.tensor_tensor(DT[:, 4], DT[:, 4], DT[:, 6], ALU.subtract))
                    own.settle()
                    own.mark(v.scalar_tensor_tensor(out=DT[:, 0], in0=DT[:, 0], scalar=0.0, in1=DT[:, 4],
                                                    op0=ALU.max, op1=ALU.add))
                    own.settle()
                    dve.wait_ge(act_own, 2)
                    v.scalar_tensor_tensor(out=ADT[:], in0=DT[:, 0], scalar=-1.0,
                                           in1=ALG[:].unsqueeze(1).to_broadcast(b16), op0=ALU.mult,
                                           op1=ALU.mult).then_inc(adt_ready, 1)
                    own.mark(v.tensor_scalar(NG[:], NG[:], 0.5, 0.5, ALU.mult, ALU.add))
                elif kind == "S1":
                    dve.wait_ge(s1_full, 1)
                    own.mark(v.tensor_copy(CS[:], bank(4, T, 16)))
                    own.settle()
                    own.mark(v.tensor_tensor(DE[:], bank(4, 16, off=32), CS[:, 0], ALU.subtract))
                    own.settle()
                    dve.sem_inc(cs_ready, 1)
                elif kind == "XT":
                    c, half = k // 2, k % 2
                    dve.wait_ge(xt_full, k + 1 + (k >= 2))
                    v.tensor_tensor(part(XDT, D * c + 512 * half, 8, DH), bank(5, 8, DH),
                                    DT[:, 0, c, 8 * half:8 * half + 8].unsqueeze(2).to_broadcast([P, 8, DH]),
                                    ALU.mult).then_inc(xdt_ready, 1)
                    if k == 0:
                        for i, (src, dst, kind_) in enumerate(((KC2, KCP, "kc"), (VC2, VCP, "vc"))):
                            taken(dve, kind_)
                            for half in range(2):
                                nb = 16 - half
                                d4 = dst[:, half].rearrange("p (g c) j -> p g c j", g=GROUPS)[:, :, 0:nb]
                                s4 = src.rearrange("p g (c j two) -> p g c j two", c=16, two=2
                                                   )[:, :, half:16, :, 0]
                                p0 = 96 + 16 * i + 8 * half
                                for g4 in range(GROUPS):
                                    ins = v.tensor_tensor(d4[:, g4], s4[:, g4], PC[:, p0:p0 + 8].unsqueeze(1)
                                                          .to_broadcast([P, nb, 8]), ALU.add)
                                ins.then_inc(kcp_ready, 1)
                elif kind == "BT":
                    dve.wait_ge(xt_full, 3)
                    v.tensor_copy(BTK, bank(5, 4, P)).then_inc(bt_ready, 1)
                elif kind == "HID":
                    dve.wait_ge(unit_done, at_unit[("w1v", 0)] + 1)
                    h = HIDT
                    own.mark(v.tensor_copy(h[:, 0], bank(7, P)))
                    own.settle()
                    own.mark(v.tensor_tensor(h[:, 1], h[:, 0], h[:, 0], ALU.mult))
                    own.settle()
                    own.mark(v.tensor_scalar(h[:, 1], h[:, 1], 0.044715, 1.0, ALU.mult, ALU.add))
                    own.settle()
                    v.tensor_tensor(h[:, 2], h[:, 1], h[:, 0], ALU.mult).then_inc(hid_t3, 1)
                    dve.wait_ge(hid_th, 1)
                    v.scalar_tensor_tensor(out=h[:, 4], in0=h[:, 3], scalar=1.0, in1=h[:, 0], op0=ALU.add,
                                           op1=ALU.mult).then_inc(hid_act, 1)
                elif kind == "HT":
                    dve.wait_ge(hid_full, 1)
                    v.tensor_copy(HID[:].rearrange("p a b c -> p (a b c)"), bank(7, P, off=P)
                                  ).then_inc(hid_ready, 1)
                elif kind == "K2":
                    dve.wait_ge(k2_full, 1)
                    dve.wait_ge(const_done, 2)
                    for hh in range(2):
                        s = slice(64 * hh, 64 * hh + 64)
                        own.mark(v.tensor_scalar(BDK[s, :, hh, :], psum[s, 7, 256:320].rearrange(
                            "p (g c) -> p g c", g=GROUPS), 0.5, None, ALU.mult))
                    own.settle()
                    dve.sem_inc(k2_ready, 1)
                elif kind == "V2":
                    dve.wait_ge(y_full, 8)
                    for hb in range(2):
                        for g2 in range(2):
                            own.mark(v.tensor_copy(HVR[:, hb, g2], HID[:, 1, 2 * hb + g2].unsqueeze(1)
                                                   .to_broadcast([P, REP, 16])))
                    own.settle()
                    dve.sem_inc(hvr_ready, 1)
                    dve.wait_ge(v2_full, 1)
                    for hb in range(2):
                        own.mark(v.tensor_tensor(VBD[:, hb], bank(6, DH, off=128 + 64 * hb).unsqueeze(1)
                                                 .to_broadcast([P, 8, DH]),
                                                 HM[:].unsqueeze(2).to_broadcast([P, 8, DH]), ALU.mult))
                    own.settle()
                    dve.sem_inc(v2_ready, 1)
                elif kind == "A":
                    c, gr, b = k // 4, k % 4, k % 2
                    dve.wait_ge(a_full, k + 1)
                    if k >= 2:
                        dve.wait_ge(y_full, k - 1)
                    for r in range(REP):
                        ins = v.tensor_scalar(E[:, b, P * r:P * r + P], bank(3, REP, P)[:, r],
                                              CS[:, c, REP * gr + r:REP * gr + r + 1], 0.0,
                                              ALU.subtract, ALU.min)
                    ins.then_inc(csb_read, 1)
                    if k >= 2:
                        dve.wait_ge(m_done, k - 1)
                    v.tensor_tensor(GM[:, b], bank(4, P), UPP[:], ALU.mult).then_inc(gm_ready, 1)
                elif kind == "ST":
                    dve.wait_ge(st_full, k + 1)
                    v.tensor_copy(ST[:, 512 * k:512 * k + 512], psum[:, 7]).then_inc(st_ready, 1)
                elif kind == "Y":
                    c, gr = k // 4, k % 4
                    dve.wait_ge(y_full, k + 1)
                    if k == 0:
                        dve.wait_ge(xd_done, 1)
                    yv = YV[:, 2 * gr:2 * gr + 2, P * c:P * c + P]
                    v.tensor_tensor(yv, yv, bank(6, 2, P), ALU.add).then_inc(y_read, 1)
                elif kind == "GY":
                    if k == 0:
                        dve.wait_ge(y_read, 8)
                    yv = YV[:, 2 * k:2 * k + 2]
                    v.tensor_tensor(yv, yv, ZS[:, 2 * k:2 * k + 2], ALU.mult).then_inc(gy_ready, 1)
                elif kind == "GN":
                    dve.wait_ge(rb_ready, k + 1)
                    dve.wait_ge(sq_ready, k + 1)
                    for f in range(2):
                        j = 2 * k + f
                        ins = v.scalar_tensor_tensor(out=YV[:, j], in0=YV[:, j], scalar=PH[:, 80 + j:81 + j],
                                                     in1=CTE[:, k % 2, SEQ:2 * SEQ], op0=ALU.mult, op1=ALU.mult)
                        if f == 0:
                            own.mark(ins)
                        else:
                            own.mark(ins)
                    own.settle()
                    dve.sem_inc(yn_ready, 1)
                elif kind == "CS":
                    dve.wait_ge(cs_full, 1)
                    for t in range(T):
                        own.mark(v.scalar_tensor_tensor(
                            out=PCS[:, t], in0=bank(5, HEADS, 16, off=256 * t), scalar=DH ** -0.5,
                            in1=CMC[:, t].unsqueeze(1).to_broadcast([P, HEADS, 16]), op0=ALU.mult, op1=ALU.add))
                    own.settle()
                    own.mark(v.tensor_reduce(CST[:, 0], PCS[:], AX.X, ALU.max))
                    own.settle()
                    own.mark(v.tensor_scalar(CST[:, 0], CST[:, 0], -1e25, None, ALU.max))
                    own.settle()
                    v.tensor_tensor(PCS[:], PCS[:], CST[:, 0].unsqueeze(3).to_broadcast([P, T, HEADS, 16]),
                                    ALU.subtract).then_inc(cs_sub, 1)
                    dve.wait_ge(cs_exp, 1)
                    own.mark(v.tensor_reduce(CST[:, 1], PCS[:], AX.X, ALU.add))
                    own.settle()
                    own.mark(v.tensor_scalar(CST[:, 1], CST[:, 1], 1e-30, None, ALU.max))
                    own.settle()
                    own.mark(v.reciprocal(CST[:, 2], CST[:, 1]))
                    own.settle()
                    own.mark(v.tensor_tensor(CST[:, 3], CST[:, 2],
                                             NG[:].rearrange("p t (h y) -> p t h y", y=3)[:, :, :, 0], ALU.mult))
                    own.settle()
                    v.tensor_tensor(PCS[:], PCS[:], CST[:, 3].unsqueeze(3).to_broadcast([P, T, HEADS, 16]),
                                    ALU.mult).then_inc(cp_ready, 1)
                elif kind == "SC":
                    t, j, b = k // 8, k % 8, k % 3
                    nk = P * (t + 1)
                    dve.wait_ge(sc_full, k + 1)
                    if k == 0:
                        dve.wait_ge(y_full, 8)
                        dve.wait_ge(st_full, 2)
                    if k >= 3:
                        dve.wait_ge(pt_full, k - 2)
                    for hh in range(2):
                        for y in range(2):
                            q = 2 * hh + y
                            own.mark(v.tensor_tensor_reduce(
                                SP[b][:, hh, y, 0:nk], psum[:, 3 + hh, 256 * y:256 * y + nk],
                                CM[:, 256 - nk:256], DH ** -0.5, -3e38, ALU.add, ALU.max,
                                AMX[:, b, 0, q:q + 1]))
                    own.settle()
                    v.tensor_scalar(AMX[:, b, 1], AMX[:, b, 0], -1.0, None, ALU.mult).then_inc(nm_ready, 1)
                elif kind == "RW":
                    t, j, b = k // 8, k % 8, k % 3
                    dve.wait_ge(ex_done, k + 1)
                    own.mark(v.tensor_scalar(AMX[:, b, 2], AMX[:, b, 2], 1e-30, None, ALU.max))
                    own.settle()
                    own.mark(v.reciprocal(AMX[:, b, 2], AMX[:, b, 2]))
                    own.settle()
                    ng = NG[:, t].rearrange("p (h y) -> p h y", y=3)[:, 2 * j:2 * j + 2, 1:3]
                    v.tensor_tensor(AMX[:, b, 3].rearrange("p (h y) -> p h y", h=2),
                                    AMX[:, b, 2].rearrange("p (h y) -> p h y", h=2), ng, ALU.mult
                                    ).then_inc(w_ready, 1)
                elif kind == "PT":
                    n = 2 * P * (k // 8 + 1)
                    dve.wait_ge(pt_full, k + 1)
                    if k >= 1:
                        dve.wait_ge(pv_full, k)
                    v.tensor_copy(PTS[:, 1, 0:n], psum[:, 6, 0:n]).then_inc(pt_dve, 1)

            inv_rms(2, lambda ins: ins.then_inc(lg_ready, 1))
            dve.wait_ge(late_in, 16 * 5)
            for t in range(T):
                v.scalar_tensor_tensor(out=H2[:, t], in0=X[:, t], scalar=ss[:, 4 + t:5 + t], in1=WFF,
                                       op0=ALU.mult, op1=ALU.mult).then_inc(h2_ready, 1)
            for b in (1, 3):
                dve.wait_ge(h2t_full, b + 1)
                v.tensor_copy(H2T[:, 2 * b:2 * b + 2].rearrange("p a b -> p (a b)"), psum[:, 3 + b]
                              ).then_inc(h2t_dve, 1)
            dve.wait_ge(rt_full, 1)
            own.mark(v.tensor_tensor(LG, bank(7, T, EXPERTS), RB[:].unsqueeze(1).to_broadcast([P, T, EXPERTS]),
                                     ALU.add))
            own.settle()
            for t in range(T):
                own.mark(v.max(MX8[:, t], LG[:, t]))
            own.settle()
            for t in range(T):
                own.mark(v.max_index(IX8[:, t], MX8[:, t], LG[:, t]))
                own.mark(v.tensor_scalar(RT[:, 1, t, 0:1], MX8[:, t, 0:1], -1.0, None, ALU.mult))
            own.settle()
            v.tensor_copy(RT[:, 0], IX8[:]).then_inc(mx_ready, 1)
            dve.wait_ge(mx_ready, 1)
            for t in range(T):
                for q in range(TOPK):
                    own.mark(v.tensor_scalar(OH4[:, t, q], EIO[:], RT[:, 0, t, q:q + 1], None, ALU.is_equal))
            own.settle()
            for t in range(T):
                own.mark(v.tensor_reduce(MSK[:, t], OH4[:, t].rearrange("p q e -> p e q"), AX.X, ALU.add))
            dve.wait_ge(te_ready, 1)
            for t in range(T):
                own.mark(v.reciprocal(RT[:, 4, t, 0:1], RT[:, 3, t, 0:1]))
            own.settle()
            for t in range(T):
                own.mark(v.tensor_scalar(RT[:, 5, t, 0:TOPK], RT[:, 2, t, 0:TOPK], RT[:, 4, t, 0:1], None, ALU.mult))
            own.settle()
            for t in range(T):
                own.mark(v.tensor_tensor(OW4[:, t], OH4[:, t], RT[:, 5, t, 0:TOPK].unsqueeze(2)
                                         .to_broadcast([P, TOPK, EXPERTS]), ALU.mult))
            own.settle()
            for t in range(T):
                own.mark(v.tensor_reduce(CW[:, t], OW4[:, t].rearrange("p q e -> p e q"), AX.X, ALU.add))
            own.settle()
            dve.sem_inc(msk_ready, 1)
            dve.wait_ge(rk_full, 1)
            own.mark(v.tensor_scalar(MSK, MSK, -1e4, 1e4, ALU.mult, ALU.add))
            own.mark(v.tensor_reduce(RT[:, 6, 0, 0:1], bank(3, EXPERTS, off=64), AX.X, ALU.max))
            own.settle()
            own.mark(v.tensor_tensor(SLT, bank(3, T, EXPERTS), MSK, ALU.add))
            own.mark(v.tensor_scalar(RT[:, 7, 0, 0:3], TH3[:], RT[:, 6, 0, 0:1], None, ALU.is_lt))
            own.settle()
            own.mark(v.tensor_reduce(RT[:, 8, 0, 0:1], RT[:, 7, 0, 0:3], AX.X, ALU.add))
            own.settle()
            own.mark(v.tensor_scalar(RCI[:], RT[:, 8, 0, 0:1], 1.0, None, ALU.add))
            own.settle()
            dve.sem_inc(round_ready, 1)
            dve.sem_inc(slot_ready, 1)
            dve.wait_ge(cwt_full, 1)
            own.mark(v.tensor_copy(CWT[0:EXPERTS], bank(4, T, P)[0:EXPERTS]))
            own.settle()
            dve.sem_inc(cwt_full, 1)
            def prepare(e0, settled, base):
                cols = bass.ds(e0, 2)

                def go(k, ins):
                    ins.then_inc(dve_own, 1)
                    return ins

                v.tensor_copy(C2[:, 0], SLT[:, :, cols]).then_inc(dve_own, 1)
                v.tensor_copy(C2[:, 1], CW[:, :, cols]).then_inc(dve_own, 1)
                v.tensor_copy(OHE[0:EXPERTS], IDN[0:EXPERTS, cols].unsqueeze(2)
                              .to_broadcast([EXPERTS, 2, CAP])).then_inc(dve_own, 1)
                dve.wait_ge(dve_own, base + 3)
                v.tensor_scalar(SLT[:, :, cols], SLT[:, :, cols], float(-CAP), None, ALU.add).then_inc(dve_own, 1)
                for t in range(T):
                    for s in range(2):
                        v.tensor_scalar(SPR[:, t, s], IOT[:, 0:CAP], C2[:, 0, t, s:s + 1], None, ALU.is_equal
                                        ).then_inc(dve_own, 1)
                        v.tensor_scalar(CPR[:, t, s], IOT[:], C2[:, 0, t, s:s + 1], C2[:, 1, t, s:s + 1],
                                        ALU.is_equal, ALU.mult).then_inc(dve_own, 1)
                dve.wait_ge(dve_own, base + 12)
                dve.sem_inc(prep_done, 1)

            PREP = 12
            prepare(0, None, own.n)
            for t in range(T):
                dve.wait_ge(bd_full, t + 1)
                xo = X[:, t].rearrange("p (a b) -> p a b", a=2)
                v.tensor_tensor(xo, xo, psum[:, 3:5, :], ALU.add).then_inc(acc_ready, 1)
            dve.wait_ge(acc_ready, T)
            base = own.n + PREP
            per = PREP + 2
            dve.sem_inc(gu_read, 1)
            dve.sem_inc(o_read, 1)
            r = rounds(dve)
            with dve.Fori(0, r * EX2) as i:
                for s in range(2):
                    n = i * 2 + s
                    dve.wait_ge(unit_done, n * RING + (NU + 8))
                    gu = psum[:, 0:2, :].rearrange("p q (f two) -> p q f two", two=2)
                    v.tensor_scalar(GBU.rearrange("p (q f) -> p q f", q=2), gu[:, :, :, 0], 7.0, None, ALU.min
                                    ).then_inc(g_ready, 1)
                    v.tensor_scalar(LBU.rearrange("p (q f) -> p q f", q=2), gu[:, :, :, 1], 7.0, -7.0,
                                    ALU.min, ALU.max).then_inc(gu_read, 1)
                    dve.wait_ge(sig_ready, n + 1)
                    v.tensor_tensor(GBU, GBU, SGA, ALU.mult).then_inc(dve_own, 1)
                    dve.wait_ge(dve_own, i * per + (base + (1 if s == 0 else 2)))
                    dve.wait_ge(gu_read, n + 2)
                    v.scalar_tensor_tensor(out=ABU, in0=LBU, scalar=1.0, in1=GBU, op0=ALU.add, op1=ALU.mult
                                           ).then_inc(act_ready, 1)
                    for t in range(T):
                        dve.wait_ge(o_full, n * 2 + (t + 1))
                        xo = X[:, t].rearrange("p (a b) -> p a b", a=2)
                        v.tensor_tensor(xo, xo, psum[:, 3 + 2 * t:5 + 2 * t, :], ALU.add).then_inc(o_read, 1)
                    if s == 1:
                        dve.wait_ge(ct_full, n + 1)
                        prepare(((i + 1) % EX2) * 2, None, i * per + (base + 2))
            nexp = r * EXPERTS
            for t in range(T):
                dve.wait_ge(o_full, nexp * 2 + (t + 1))
                xo = X[:, t].rearrange("p (a b) -> p a b", a=2)
                v.tensor_tensor(xo, xo, psum[:, 3 + 2 * t:5 + 2 * t, :], ALU.add).then_inc(o_read, 1)
            dve.wait_ge(o_read, nexp * 2 + 3)
            dve.sem_inc(final_in, 1)
            dve.wait_ge(ss_ready, 6)
            v.tensor_scalar(ss[:, 0:2], ss[:, 0:2], 1.0 / D, EPS, ALU.mult, ALU.add).then_inc(lg_ready, 2)
            dve.wait_ge(sq_root, 3)
            v.reciprocal(ss[:, 4:6], ss[:, 2:4]).then_inc(lg_ready, 1)
            dve.wait_ge(lg_ready, 4)
            for t in range(T):
                v.scalar_tensor_tensor(out=RJ[:, t], in0=X[:, t], scalar=ss[:, 4 + t:5 + t], in1=WFN,
                                       op0=ALU.mult, op1=ALU.mult).then_inc(lg_ready, 1)
            dve.wait_ge(lg_ready, 6)
            dve.sem_inc(norm_ready, 1)


_INS = ['x', 'mix_norm_w', 'w_in', 'conv_w', 'conv_b', 'dt_bias', 'a_log', 'd_skip', 'ssm_norm_w',
        'cmp_pos_k', 'cmp_w1_k', 'cmp_w2_k', 'cmp_pos_v', 'cmp_w1_v', 'cmp_w2_v', 'w_branch_ssm',
        'w_branch_nsa', 'w_out', 'ffn_norm_w', 'router_w', 'router_b', 'w_gate_up', 'b_gate_up', 'w_down',
        'b_down', 'final_norm_w']


def kernel(**inputs):
    import numpy as _np
    import concourse.bacc as _bacc
    from concourse import mybir as _mybir
    from concourse.bass_utils import run_bass_kernel_spmd as _run

    nc = _bacc.Bacc("TRN2", target_bir_lowering=False, num_devices=1)
    arrays, args = {}, []
    for name in _INS:
        a = _np.ascontiguousarray(inputs[name])
        arrays[f"in_{name}_dram"] = a
        args.append(nc.dram_tensor(f"in_{name}_dram", a.shape, _mybir.dt.from_np(a.dtype), kind="ExternalInput").ap())
    args.append(nc.dram_tensor("out_0_dram", (1, 256, 1024), _mybir.dt.float32, kind="ExternalOutput").ap())
    hybrid_block(nc, *args)
    r = _run(nc, [arrays], core_ids=[0])
    return r.results[0]["out_0_dram"]
```

```python
from contextlib import ExitStack

import concourse.bass as bass
from concourse import mybir

F32 = mybir.dt.float32
I32 = mybir.dt.int32
U32 = mybir.dt.uint32
F32R = mybir.dt.float32r
ALU = mybir.AluOpType
ACT = mybir.ActivationFunctionType
AX = mybir.AxisListType

P = 128
D = 1024
SEQ = 256
T = SEQ // P
KT = D // P
HEADS = 16
GROUPS = 4
REP = HEADS // GROUPS
DH = 64
CMP_BLOCK, CMP_STRIDE = 32, 16
NCMP = (SEQ - CMP_BLOCK) // CMP_STRIDE + 1
EXPERTS = 32
TOPK = 4
EPS = 1e-5
NEG = -1e30
CAP = 64
RING = 12
UNITS_E = 12
SLOTS = 17
SHARED = 2 * UNITS_E - SLOTS
STREAM = 4
SPLITS = 3
SLOT = 2048

OFF_Z, OFF_XBC, OFF_DT, OFF_Q = 0, 1024, 3072, 3088
OFF_KC, OFF_VC, OFF_KS, OFF_VS, OFF_KW, OFF_VW = 4112, 4368, 4624, 4880, 5136, 5392
OFF_NG, OFF_MG = 5648, 5696

UNITS = ([("xbc", m) for m in range(8)] + [("small", 0), ("kc", 0), ("vc", 0), ("ks", 0), ("kw", 0),
         ("w1k", 0), ("w1v", 0), ("vs", 0), ("vw", 0)] + [("q", m) for m in range(4)]
         + [("z", m) for m in range(4)] + [("mg", m) for m in range(8)]
         + [("bs", m) for m in range(4)] + [("bn", m) for m in range(4)] + [("wo", m) for m in range(4)])
NU = len(UNITS)


SPLIT_UNITS = [u for u, (kind, _) in enumerate(UNITS) if kind not in ("w1k", "w1v")]

POOL_UNITS = [u for n, u in enumerate(SPLIT_UNITS) if UNITS[u][0] in ("mg", "bs")]


def token_order():
    u = {x: n for n, x in enumerate(UNITS)}
    out = []

    def unit(kind, m=0):
        out.extend([("H", u[(kind, m)]), ("P", u[(kind, m)])])

    for m in range(8):
        unit("xbc", m)
        if m >= 1:
            out.append(("F", m - 1))
    unit("small")
    out += [("F", 7), ("XD", 0), ("DT", 0)]
    unit("kc")
    out += [("S1", 0)]
    unit("vc")
    out += [("XT", 0)]
    unit("ks")
    out += [("XT", 1)]
    unit("kw")
    out += [("HID", 0), ("BT", 0), ("A", 0)]
    unit("vs")
    out += [("HT", 0), ("A", 1), ("XT", 2)]
    unit("vw")
    out += [("K2", 0), ("Y", 0), ("A", 2), ("ST", 0), ("XT", 3)]
    for m in range(4):
        unit("q", m)
        out += [("Y", m + 1), ("A", m + 3)]
        if m == 0:
            out += [("ST", 1)]
    unit("z", 0)
    out += [("Y", 5), ("A", 7)]
    unit("z", 1)
    out += [("Y", 6)]
    unit("z", 2)
    out += [("Y", 7), ("V2", 0), ("CT", 0), ("GY", 0)]
    unit("z", 3)
    out += [("CS", 0), ("GY", 1)]
    unit("mg", 0)
    out += [("GN", 0), ("CP", 0), ("GY", 2), ("SC", 0)]
    unit("mg", 1)
    out += [("GN", 1), ("GY", 3), ("SC", 1)]
    halves = []
    for x in [("mg", m) for m in range(2, 8)] + [("bs", m) for m in range(4)]:
        halves += [("H", u[x]), ("P", u[x])]
    out += [halves.pop(0), ("GN", 2), halves.pop(0), ("GN", 3)]
    for k in range(17):
        if k + 2 < 16:
            out.append(("SC", k + 2))
        if k < 16:
            out.append(("RW", k))
        out += {0: [("GR", 0)], 1: [("GX", 0)], 4: [("YS", 0)]}.get(k, [])
        if halves and k in (1, 8):
            out.append(halves.pop(0))
        if k >= 1:
            out.append(("PV", k - 1))
        if halves:
            out.append(halves.pop(0))
        if k < 16:
            out.append(("PT", k))
    out += halves + [("LD", 0)]
    for m in range(4):
        unit("bn", m)
        if m >= 1:
            out.append(("MT", m - 1))
    out.append(("MT", 3))
    for m in range(4):
        unit("wo", m)
    order, due = [("W", SPLIT_UNITS[SPLITS - 1])], []
    first, last = out.index(("GR", 0)), out.index(("PT", 15))
    for n, token in enumerate(out):
        order.append(token)
        if token[0] == "H" and token[1] in SPLIT_UNITS[1:]:
            i = SPLIT_UNITS.index(token[1]) - 1 + SPLITS
            if i < len(SPLIT_UNITS):
                due.append(("W", SPLIT_UNITS[i]))
        if not first <= n < last or token[0] in ("H",):
            order += due
            due = []
    return order


TOKENS = token_order()


def hybrid_block(nc, x, mix_norm_w, w_in, conv_w, conv_b, dt_bias, a_log, d_skip, ssm_norm_w,
                 cmp_pos_k, cmp_w1_k, cmp_w2_k, cmp_pos_v, cmp_w1_v, cmp_w2_v,
                 w_branch_ssm, w_branch_nsa, w_out, ffn_norm_w, router_w, router_b,
                 w_gate_up, b_gate_up, w_down, b_down, final_norm_w, out):
    with ExitStack() as ctx:
        def sb(name, shape, dt=F32):
            return ctx.enter_context(nc.sbuf_tensor(name, shape, dt))

        def sem(name):
            return ctx.enter_context(nc.semaphore(name))

        def part(t, off, *dims):
            n = 1
            for d in dims:
                n *= d
            names = "abcde"[:len(dims)]
            rank = len(t.shape) - 1
            flat = t[:] if rank == 1 else t[:].rearrange(
                "p " + " ".join("wxyz"[:rank]) + " -> p (" + " ".join("wxyz"[:rank]) + ")")
            v = flat[:, off:off + n]
            if len(dims) == 1:
                return v
            return v.rearrange("p (" + " ".join(names) + ") -> p " + " ".join(names),
                               **{c: d for c, d in zip(names[1:], dims[1:])})

        def at_place(name, shape, place, dt=F32R):
            return nc.alloc_sbuf_tensor_at(name, shape, dt, offset=place)

        ring_at = -(-nc.sbuf_base // 32) * 32
        ring = sb("ring", [P, RING, SLOT])
        X = sb("X", [P, T, D])
        ht_at = -(-nc.sbuf_base // 32) * 32
        HT = sb("HT", [P, KT, SEQ])
        XC = sb("XC", [P, 16, SEQ])
        yv_at = -(-nc.sbuf_base // 32) * 32
        YV = sb("YV", [P, 8, SEQ])
        zs_at = -(-nc.sbuf_base // 32) * 32
        ZS = sb("ZS", [P, 8, SEQ])
        XDT = sb("XDT", [P, 3 * D])
        st_at = -(-nc.sbuf_base // 32) * 32
        ST = sb("ST", [P, D])
        E = sb("E", [P, 2, 512])
        GM = sb("GM", [P, 2, P])
        ec_at = -(-nc.sbuf_base // 32) * 32
        EC = sb("EC", [P, 2, 512])
        CTE = sb("CTE", [P, 2, 512])
        QT = sb("QT", [P, 8, SEQ])
        KD = sb("KD", [P, 2, GROUPS, SEQ])
        th_at = -(-nc.sbuf_base // 32) * 32
        TH = sb("TH", [P, 2, 512])
        VT = sb("VT", [P, 2, T, 256])
        PR = sb("PR", [P, P])
        PC = sb("PC", [P, P])
        PH = sb("PH", [P, 96])
        IDN = sb("IDN", [P, P])
        UPP = sb("UPP", [P, P])
        UST = sb("UST", [P, P])
        ONE = sb("ONE", [P, P])
        CM = sb("CM", [P, 256])
        CMC = sb("CMC", [P, T, 16])
        IOI = sb("IOI", [P, P], I32)
        IOT = sb("IOT", [P, P])
        EIO = sb("EIO", [P, EXPERTS])
        TH3 = sb("TH3", [P, 3])
        HM = sb("HM", [P, 8])
        W2K = sb("W2K", [P, 2, DH])
        W2V = sb("W2V", [P, DH])
        DTB = sb("DTB", [P, HEADS])
        ALG = sb("ALG", [P, HEADS])
        DCOL = sb("DCOL", [P, 8])
        RB = sb("RB", [P, EXPERTS])
        SM = sb("SM", [P, T, 64])
        DT = sb("DT", [P, 8, T, HEADS])
        ADT = sb("ADT", [P, T, HEADS])
        CS = sb("CS", [P, T, HEADS])
        DE = sb("DE", [P, HEADS])
        NG = sb("NG", [P, T, 48])
        ss = sb("ss", [P, 8])
        HID = sb("HID", [P, 2, GROUPS, 16])
        BDK = sb("BDK", [P, GROUPS, 2, 16])
        AMX = sb("AMX", [P, 3, 4, 4])

        slot_at = [ring_at + 4 * SLOT * i for i in range(RING)]
        HTL = at_place("HTL", [P, KT, SEQ], slot_at[STREAM])
        OTL = at_place("OTL", [P, KT, SEQ], slot_at[STREAM + 1])
        WH = [at_place(f"WH{i}", [P, SLOT], slot_at[STREAM + 2 + i]) for i in range(SPLITS)]
        WL = [at_place(f"WL{i}", [P, SLOT], slot_at[STREAM + 2 + SPLITS + i]) for i in range(SPLITS)]
        HTH = at_place("HTH", [P, KT, SEQ], ht_at)
        OTH = at_place("OTH", [P, KT, SEQ], zs_at)
        YSH = at_place("YSH", [P, KT, SEQ], ec_at)
        YSL = at_place("YSL", [P, KT, SEQ], yv_at)
        HTHF, HTLF, OTHF, YSHF = [t[:].bitcast(F32) for t in (HTH, HTL, OTH, YSH)]
        WHF = [t[:].bitcast(F32) for t in WH]
        rslot = [part(ring, i * SLOT, SLOT) for i in range(RING)]
        last_split = [(len(SPLIT_UNITS) - 1 - i) % SPLITS for i in range(SPLITS)]
        places = [part(XDT, D, SLOT),
                  at_place("slot1", [P, SLOT], st_at, F32)[:],
                  at_place("slot2", [P, SLOT], th_at, F32)[:],
                  at_place("slot3", [P, SLOT], ec_at, F32)[:],
                  rslot[(NU - 4) % STREAM], rslot[(NU - 3) % STREAM],
                  rslot[STREAM + 1],
                  rslot[(NU - 2) % STREAM], rslot[(NU - 1) % STREAM]]
        for i in (2, 1, 0):
            places += [rslot[STREAM + 2 + last_split[i]], rslot[STREAM + 2 + SPLITS + last_split[i]]]
        places += [rslot[STREAM], part(XC, SLOT, SLOT)]

        def slot_of(s, j):
            return j if s == 0 or j < SHARED else UNITS_E + j - SHARED

        VBD = part(ST, 0, 2, 8, DH)
        PCS = part(E, 0, T, HEADS, 16)
        PCT = part(E, 512, T, 2, P)
        CSR = part(EC, 512, 512)
        BTK = part(ZS, 0, GROUPS, P)
        HIDT = part(ST, 0, 5, P)
        KCP = EC[:].rearrange("p h (m j) -> p h m j", j=8)
        VCP = CTE[:].rearrange("p h (m j) -> p h m j", j=8)
        CST = part(GM, 0, 6, T, HEADS)
        RW_ = part(GM, 0, KT, EXPERTS)
        HVR = part(CTE, 0, 2, 2, REP, 16)
        KC2 = part(ZS, 0, GROUPS, SEQ)
        VC2 = part(ZS, 1024, GROUPS, SEQ)
        HN = part(ZS, 0, T, D)
        OT = part(ZS, 0, 8, SEQ)
        GA = part(XC, 0, T, 2048)
        SQ = EC
        SP = [part(XDT, 0, 2, 2, 256), part(XDT, 1024, 2, 2, 256), part(TH, 0, 2, 2, 256)]
        PTS = part(XDT, 2048, 2, 512)
        MG = GA[:, :, 0:D]
        H2 = part(XC, 0, T, D)
        H2T = part(XC, 2048, KT, SEQ)
        WFF = part(YV, 0, D)
        WFN = part(YV, 1024, D)
        BGU = part(KD, 0, 2048)
        XTS = part(ZS, 0, KT, 2, CAP)
        SGA = part(ZS, 1024, 512)
        GBU = part(ZS, 1536, 512)
        LBU = part(HT, 0, 512)
        ABU = part(HT, 512, 512)
        ATS = part(HT, 1024, 4, P)
        YSB = part(HT, 1536, 512)
        CTS = part(QT, 0, 2, T, P)
        SPR = part(QT, 512, T, 2, CAP)
        CPR = part(QT, 768, T, 2, P)
        OHE = part(QT, 1280, 2, CAP)
        C2 = part(QT, 1408, 2, T, 2)
        SLT = part(QT, 1424, T, EXPERTS)
        CWP = part(QT, 1488, T, 2, CAP)
        CW = CWP[:, :, 0, 0:EXPERTS]
        MSK = part(QT, 1744, T, EXPERTS)
        MFAR = part(XDT, 768, T, EXPERTS)
        junk = part(XDT, 832, 4)
        LG = part(QT, 1808, T, EXPERTS)
        MX8 = part(QT, 1872, T, 8)
        OH4 = part(XDT, 0, T, TOPK, EXPERTS)
        OW4 = part(XDT, 256, T, TOPK, EXPERTS)
        RT = part(XDT, 512, 16, T, 8)
        SQX = part(XC, 2048, T, D)
        RJ = part(ring, 0, T, D)
        IX8 = sb("IX8", [P, T, 8], U32)
        RCI = sb("RCI", [P, 1], I32)

        psum = ctx.enter_context(nc.psum_tensor("psum", [P, 8, 512], F32))

        ring_full = [sem(f"ring_full{i}") for i in range(STREAM)]
        slot_full = [sem(f"slot_full{i}") for i in range(SLOTS)]
        unit_done = sem("unit_done")
        x_in = [sem(f"x_in{t}") for t in range(T)]
        wl_pool = sem("wl_pool")
        proj_free = [sem(f"proj_free{i}") for i in range(3)]
        (rows_in, small_in, late_in, const_done, dve_own, act_own, pool_own, hn_ready, ht_full,
         ht_act, par_full, par_ready, hv_done, th_ready, th_used, xd_done, dt_e, dt_w, dt_l, adt_ready,
         s1_full, cs_ready, de_ready, xt_full, xdt_ready, bt_ready, xde_ready, a_full, csb_read,
         gm_ready, e_exp, ecs_done, m_done, cte_done, y_full, y_read, st_full, st_ready, csr_full,
         csr_ready, kcp_ready, hid_act, hid_full, hid_t3, hid_th, hid_ready, hvr_ready, k2_full,
         k2_ready, v2_full, v2_ready, gy_ready, sq_ready, gn_full, rb_ready, yn_ready, cs_full, cs_sub,
         cs_exp, cp_ready, cp_full, cp_read, sc_full, nm_ready, ex_done, w_ready, p_ready, pt_full,
         pt_act, pt_dve, pv_full, pv_read, mg_ready, mt_full, mt_ready, x2_ready, ss_ready, sq_root,
         h2_ready, h2t_full, h2t_act, h2t_dve, rt_full, lg_ready, mx_ready, te_ready, msk_ready,
         rk_full, round_ready, cwt_full, final_in, norm_ready, stored, prep_done, xte_full,
         xte_ready, gu_read, ct_full, ct_ready, y_ready, o_full, o_read, g_ready, sig_ready, act_ready,
         at_full, at_ready, zero_ready, cw_ready, gn_read, sq2_ready, bd_in, spr_ready, wh_ready,
         wl_ready, ys_high, ys_ready, ht_low, mt_low, ot_high) = [sem(n) for n in (
            "rows_in small_in late_in const_done dve_own act_own pool_own hn_ready ht_full ht_act "
            "par_full par_ready hv_done th_ready th_used xd_done dt_e dt_w dt_l adt_ready s1_full "
            "cs_ready de_ready xt_full xdt_ready bt_ready xde_ready a_full csb_read gm_ready e_exp "
            "ecs_done m_done cte_done y_full y_read st_full st_ready csr_full csr_ready kcp_ready "
            "hid_act hid_full hid_t3 hid_th hid_ready hvr_ready k2_full k2_ready v2_full v2_ready "
            "gy_ready sq_ready gn_full rb_ready yn_ready cs_full cs_sub cs_exp cp_ready cp_full cp_read "
            "sc_full nm_ready ex_done w_ready p_ready pt_full pt_act pt_dve pv_full pv_read mg_ready "
            "mt_full mt_ready x2_ready ss_ready sq_root h2_ready h2t_full h2t_act h2t_dve rt_full "
            "lg_ready mx_ready te_ready msk_ready rk_full round_ready cwt_full final_in "
            "norm_ready stored prep_done xte_full xte_ready gu_read ct_full ct_ready y_ready o_full "
            "o_read g_ready sig_ready act_ready at_full at_ready zero_ready cw_ready gn_read sq2_ready "
            "bd_in spr_ready wh_ready wl_ready ys_high ys_ready ht_low mt_low ot_high").split()]

        loads = {u: 2 if UNITS[u][0] == "small" else 1 for u in range(NU)}
        full_at, slot_total = {}, [0] * STREAM
        for u in range(NU):
            slot_total[u % STREAM] += 16 * loads[u]
            full_at[u] = slot_total[u % STREAM]
        bank_of, freed, uses = {}, {}, [0] * 3
        n = 0
        for u, (kind, _) in enumerate(UNITS):
            if kind in ("w1k", "w1v"):
                continue
            bank_of[u], freed[u] = n % 3, uses[n % 3]
            uses[n % 3] += 1
            n += 1

        def slot_view(u, *dims):
            return part(ring, (u % STREAM) * SLOT, *dims)

        def bank(b, *dims, off=0):
            n = 1
            for d in dims:
                n *= d
            v = psum[:, b, off:off + n]
            if len(dims) == 1:
                return v
            names = "abcde"[:len(dims)]
            return v.rearrange("p (" + " ".join(names) + ") -> p " + " ".join(names),
                               **{c: d for c, d in zip(names[1:], dims[1:])})

        NORM_BANKS = (3, 5, 6, 7)
        at_unit = {x: n for n, x in enumerate(UNITS)}

        def taken(eng, kind, m=0):
            u = at_unit[(kind, m)]
            eng.wait_ge(proj_free[bank_of[u]], freed[u] + 1)

        def low_ready(eng, i):
            u = SPLIT_UNITS[i]
            done = [w for w in SPLIT_UNITS[:i + 1] if (w in POOL_UNITS) == (u in POOL_UNITS)]
            eng.wait_ge(wl_pool if u in POOL_UNITS else wl_ready, len(done))

        class Own:

            def __init__(self, eng, s):
                self.eng, self.s, self.n = eng, s, 0

            def mark(self, ins):
                self.n += 1
                ins.then_inc(self.s, 1)

            def settle(self):
                self.eng.wait_ge(self.s, self.n)

        EX2 = EXPERTS // 2
        PAIR = 2 * UNITS_E

        def slot_loads(i, s, j):
            return i * 32 + 16 * (s + 1) if j < SHARED else i * 16 + 16

        def rounds(eng):
            eng.wait_ge(round_ready, 1)
            r = eng.value_load(RCI[0:1, 0:1], min_val=1, max_val=4)
            return r

        block = ctx.enter_context(nc.Block())

        @block.sync
        def _(sp):
            for t in range(T):
                sp.dma_start(X[:, t], x[0, P * t:P * t + P]).then_inc(x_in[t], 16)
            sp.wait_ge(rows_in, 16 * 6)

            def w_cols(w, c0, n):
                return w[0, :, c0:c0 + n].rearrange("(k p) n -> p k n", p=P)

            first = {"z": OFF_Z, "xbc": OFF_XBC, "q": OFF_Q, "kc": OFF_KC, "vc": OFF_VC, "ks": OFF_KS,
                     "vs": OFF_VS, "kw": OFF_KW, "vw": OFF_VW, "mg": OFF_MG}
            for u, (kind, m) in enumerate(UNITS):
                if u == 2:
                    sp.dma_start(DTB[:], dt_bias[0].partition_broadcast(P)).then_inc(small_in, 16)
                    sp.dma_start(ALG[:], a_log[0].partition_broadcast(P)).then_inc(small_in, 16)
                    dcol = d_skip[0].rearrange("(j two) -> two j", two=2)
                    for hh in range(2):
                        sp.dma_start(DCOL[64 * hh:64 * hh + 64, :], dcol[hh].partition_broadcast(64),
                                     allow_slow_non_contiguous=True).then_inc(small_in, 16)
                    sp.dma_start(W2K[:, 0], cmp_w2_k[0]).then_inc(small_in, 16)
                    sp.dma_start(W2K[:, 1], cmp_w2_k[0]).then_inc(small_in, 16)
                    sp.dma_start(W2V[:], cmp_w2_v[0]).then_inc(small_in, 16)
                    sp.dma_start(RB[:], router_b[0].partition_broadcast(P)).then_inc(small_in, 16)
                if u >= STREAM:
                    if u - STREAM in SPLIT_UNITS:
                        low_ready(sp, SPLIT_UNITS.index(u - STREAM))
                    else:
                        sp.wait_ge(unit_done, u - STREAM + 1)
                full = ring_full[u % STREAM]
                if kind == "small":
                    v = slot_view(u, KT, 64)
                    sp.dma_start(v[:, :, 0:16], w_cols(w_in, OFF_DT, 16)).then_inc(full, 16)
                    sp.dma_start(v[:, :, 16:64], w_cols(w_in, OFF_NG, 48)).then_inc(full, 16)
                elif kind in ("w1k", "w1v"):
                    w1 = cmp_w1_k if kind == "w1k" else cmp_w1_v
                    sp.dma_start(slot_view(u, 16, P), w1[0].rearrange("(k p) n -> p k n", p=P)).then_inc(full, 16)
                else:
                    w = {"bs": w_branch_ssm, "bn": w_branch_nsa, "wo": w_out}.get(kind, w_in)
                    sp.dma_start(slot_view(u, KT, 256), w_cols(w, first.get(kind, 0) + 256 * m, 256)
                                 ).then_inc(full, 16)

            def load(e, s, j):
                dst = places[slot_of(s, j)]
                if j < 8:
                    src = w_gate_up[0, e, P * j:P * j + P, :].rearrange("(k p) n -> p k n", p=P)
                    dst = dst.rearrange("p (k n) -> p k n", k=1)
                else:
                    src = w_down[0, e, 256 * (j - 8):256 * (j - 8) + 256, :].rearrange("(k p) n -> p k n", p=P)
                    dst = dst.rearrange("p (k n) -> p k n", k=2)
                sp.dma_start(dst, src).then_inc(slot_full[slot_of(s, j)], 16)

            for u in range(SLOTS):
                if u < 3:
                    sp.wait_ge(pv_read, 16)
                elif u == 3:
                    sp.wait_ge(unit_done, at_unit[("bs", 3)] + 1)
                elif u == 6:
                    sp.wait_ge(unit_done, at_unit[("bn", 3)] + 1)
                elif u < 9:
                    low_ready(sp, len(SPLIT_UNITS) - {4: 4, 5: 3, 7: 2, 8: 1}[u])
                elif u < 15:
                    sp.wait_ge(unit_done, NU - (14 - u) // 2)
                elif u == 15:
                    sp.wait_ge(unit_done, NU)
                else:
                    sp.wait_ge(rt_full, 1)
                s = u // UNITS_E
                load(s, s, u - s * (UNITS_E - SHARED))
            for j in range(SHARED):
                sp.wait_ge(unit_done, NU + j + 1)
                load(1, 1, j)
            for s, order in ((0, [*range(SHARED, UNITS_E), *range(SHARED)]), (1, range(UNITS_E))):
                for j in order:
                    back = UNITS_E if j < SHARED else PAIR
                    sp.wait_ge(unit_done, NU + PAIR + UNITS_E * s + j - back + 1)
                    load(2 + s, s, j)
            r = rounds(sp)
            with sp.Fori(2, r * EX2) as i:
                for u in range(PAIR):
                    back = UNITS_E if u % UNITS_E < SHARED else PAIR
                    sp.wait_ge(unit_done, i * PAIR + (NU + u - back + 1))
                    load((i % EX2) * 2 + u // UNITS_E, u // UNITS_E, u % UNITS_E)
            for t in range(T):
                sp.wait_ge(norm_ready, t + 1)
                sp.dma_start(out[0, P * t:P * t + P], RJ[:, t]).then_inc(stored, 16)
            sp.wait_ge(stored, 16 * T)

        @block.gpsimd
        def _(pool):
            own = Own(pool, pool_own)
            g = nc.gpsimd
            own.mark(g.memset(IDN[:], 0.0))
            own.mark(g.memset(UPP[:], 1.0))
            own.mark(g.memset(UST[:], 1.0))
            own.mark(g.memset(CM[:], 0.0))
            own.mark(g.memset(CMC[:], 0.0))
            own.mark(g.memset(HM[:], 0.5))
            own.mark(g.memset(ONE[:], 1.0))
            own.settle()
            own.mark(g.affine_select(out=IDN[:], in_=IDN[:], pattern=[[-1, P]], compare_op=ALU.not_equal,
                                     fill=1.0, base=0, channel_multiplier=1))
            own.settle()
            pool.sem_inc(const_done, 1)
            own.mark(g.affine_select(out=UPP[:], in_=UPP[:], pattern=[[1, P]], compare_op=ALU.is_ge,
                                     fill=0.0, base=0, channel_multiplier=-1))
            own.mark(g.affine_select(out=UST[:], in_=UST[:], pattern=[[1, P]], compare_op=ALU.is_gt,
                                     fill=0.0, base=0, channel_multiplier=-1))
            own.mark(g.affine_select(out=CM[:, P:256], in_=CM[:, P:256], pattern=[[-1, P]],
                                     compare_op=ALU.is_ge, fill=NEG, base=0, channel_multiplier=1))
            for t in range(T):
                own.mark(g.affine_select(out=CMC[:, t], in_=CMC[:, t], pattern=[[-CMP_STRIDE, 16]],
                                         compare_op=ALU.is_ge, fill=NEG, base=P * t - CMP_BLOCK + 1,
                                         channel_multiplier=1))
            own.mark(g.affine_select(out=HM[:], in_=HM[:], pattern=[[-16, 8]], compare_op=ALU.is_ge,
                                     fill=0.0, base=0, channel_multiplier=1))
            own.settle()
            own.mark(g.affine_select(out=HM[:], in_=HM[:], pattern=[[16, 8]], compare_op=ALU.is_ge,
                                     fill=0.0, base=15, channel_multiplier=-1))
            own.mark(g.iota(IOI[:], pattern=[[0, 2], [1, CAP]], base=0, channel_multiplier=0))
            own.settle()
            own.mark(g.tensor_copy(IOT[:], IOI[:]))
            own.settle()
            own.mark(g.iota(IOI[:, 0:EXPERTS], pattern=[[1, EXPERTS]], base=0, channel_multiplier=0))
            own.mark(g.iota(IOI[:, 64:67], pattern=[[CAP, 3]], base=CAP, channel_multiplier=0))
            own.settle()
            own.mark(g.tensor_copy(EIO[:], IOI[:, 0:EXPERTS]))
            own.mark(g.tensor_copy(TH3[:], IOI[:, 64:67]))
            for c in (EC, CTE):
                own.mark(g.memset(c[:], 0.0))
            own.mark(g.memset(BDK[:], 0.0))
            own.settle()
            pool.sem_inc(const_done, 1)

            for kind, k in TOKENS:
                if kind == "W" and k in POOL_UNITS:
                    i = SPLIT_UNITS.index(k)
                    pool.wait_ge(wh_ready, i + 1)
                    g.tensor_tensor(WL[i % SPLITS][:], slot_view(k, SLOT), WHF[i % SPLITS], ALU.subtract
                                    ).then_inc(wl_pool, 1)
                elif kind == "XD":
                    pool.wait_ge(th_used, 4)
                    pool.wait_ge(small_in, 16 * 8)
                    for j in range(8):
                        ins = g.tensor_scalar(YV[:, j], XC[:, j], DCOL[:, j:j + 1], None, ALU.mult)
                        if j == 7:
                            own.mark(ins)
                    own.settle()
                    pool.sem_inc(xd_done, 1)
                elif kind == "XT" and k < 2:
                    if k == 0:
                        pool.wait_ge(de_ready, 1)
                    pool.wait_ge(xdt_ready, k + 1)
                    g.tensor_tensor(part(XDT, 2048 + 512 * k, 8, DH), part(XDT, 512 * k, 8, DH),
                                    DE[:, 8 * k:8 * k + 8].unsqueeze(2).to_broadcast([P, 8, DH]),
                                    ALU.mult).then_inc(xde_ready, 1)
                elif kind == "A":
                    c, gr, b = k // 4, k % 4, k % 2
                    pool.wait_ge(e_exp, k + 1)
                    pool.wait_ge(gm_ready, k + 1)
                    ev = E[:, b].rearrange("p (r l) -> p r l", r=REP)
                    g.tensor_tensor(ev, ev, GM[:, b].unsqueeze(1).to_broadcast([P, REP, P]),
                                    ALU.mult).then_inc(m_done, 1)
                    if c == 1:
                        pool.wait_ge(ecs_done, k - 3)
                        if k >= 6:
                            pool.wait_ge(y_full, k - 1)
                        g.tensor_tensor(CTE[:, b].rearrange("p (r l) -> p r l", r=REP),
                                        EC[:, b].rearrange("p (r l) -> p r l", r=REP),
                                        XC[:, 12 + gr, P:2 * P].unsqueeze(1).to_broadcast([P, REP, P]),
                                        ALU.mult).then_inc(cte_done, 1)
                elif kind == "RW":
                    b, nk = k % 3, P * (k // 8 + 1)
                    pool.wait_ge(w_ready, k + 1)
                    v = SP[b][:, :, :, 0:nk]
                    g.tensor_tensor(v, v, AMX[:, b, 3].rearrange("p (h y) -> p h y", h=2).unsqueeze(3)
                                    .to_broadcast([P, 2, 2, nk]), ALU.mult).then_inc(p_ready, 1)
            pool.wait_ge(unit_done, NU)
            for r in (32, 96):
                own.mark(g.memset(YSB[r:r + 32], 0.0))
                own.settle()
            own.mark(g.memset(CWP, 0.0))
            own.settle()
            pool.sem_inc(zero_ready, 1)

        @block.tensor
        def _(pe):
            mm = nc.tensor.matmul

            def tr(o, i):
                return nc.tensor.transpose(o, i, IDN[:, :])

            pe.wait_ge(const_done, 1)
            pe.wait_ge(rows_in, 16 * 6)
            tr(bank(4, P), PR[:]).then_inc(par_full, 1)
            for b in range(4):
                for kk in range(2):
                    for t in range(T):
                        if b == 0 and kk == 0:
                            pe.wait_ge(hn_ready, t + 1)
                        ins = tr(bank(NORM_BANKS[b], 2, T, P)[:, kk, t], HN[:, t, P * (2 * b + kk):P * (2 * b + kk + 1)])
                ins.then_inc(ht_full, 1)
            pe.wait_ge(const_done, 2)

            def half_unit(u, half):
                kind, m = UNITS[u]
                b = bank_of[u]
                if half == 0:
                    if freed[u]:
                        pe.wait_ge(proj_free[b], freed[u])
                    if kind == "bs" and m == 0:
                        pe.wait_ge(ys_ready, 1)
                    if kind == "bn" and m == 0:
                        pe.wait_ge(pv_read, 16)
                feature_major = kind in ("xbc", "kc", "vc", "ks", "kw", "q", "z")
                high, low = {"bs": (YSH, YSL), "bn": (OTH, OTL)}.get(kind, (HTH, HTL))
                rows = slice(P * half, P * half + P)
                nco = 64 if kind == "small" else 256
                i = SPLIT_UNITS.index(u)
                wh, wl = part(WH[i % SPLITS], 0, KT, nco), part(WL[i % SPLITS], 0, KT, nco)
                if half == 0:
                    pe.wait_ge(wh_ready, i + 1)
                passes = [(wh, high), (wh, low), (wl, high)]
                if u == 0:
                    passes = [(wh, high), (wl, high), (wh, low)]
                for n, (w, src) in enumerate(passes):
                    if w is wl and half == 0:
                        low_ready(pe, i)
                    for k in range(KT):
                        if half == 0 and u == 0 and k % 2 == 0 and n != 1:
                            pe.wait_ge(ht_act if n == 0 else ht_low, k // 2 + 1)
                        if half == 0 and n < 2 and k % 2 == 0 and u == at_unit[("wo", 0)]:
                            pe.wait_ge((mt_ready, mt_low)[n], k // 2 + 1)
                        if feature_major:
                            ins = mm(bank(b, 2, SEQ)[:, half], w[:, k, rows], src[:, k, :],
                                     start=(n == 0 and k == 0), stop=(n == 2 and k == KT - 1))
                        else:
                            ins = mm(bank(b, 2, nco)[:, half], src[:, k, rows], w[:, k, :],
                                     start=(n == 0 and k == 0), stop=(n == 2 and k == KT - 1))
                if half == 1:
                    ins.then_inc(unit_done, 1)

            for kind, k in TOKENS:
                if kind == "H":
                    half_unit(k, 0)
                elif kind == "P":
                    half_unit(k, 1)
                elif kind == "S1":
                    pe.wait_ge(adt_ready, 1)
                    pe.wait_ge(par_ready, 1)
                    mm(bank(4, 16), UPP[:], ADT[:, 0], start=True, stop=True)
                    mm(bank(4, 16, off=16), UPP[:], ADT[:, 1], start=True, stop=True)
                    mm(bank(4, 16, off=32), ONE[:], ADT[:, 0], start=True, stop=True).then_inc(s1_full, 1)
                elif kind == "XT":
                    c, half = k // 2, k % 2
                    if k in (1, 3):
                        pe.wait_ge(xdt_ready, k)
                    if k == 2:
                        pe.wait_ge(bt_ready, 1)
                    for j in range(4):
                        ins = tr(bank(5, 4, P)[:, j], XC[:, 4 * half + j, P * c:P * c + P])
                    ins.then_inc(xt_full, 1)
                elif kind == "BT":
                    pe.wait_ge(xdt_ready, 2)
                    for j in range(4):
                        ins = tr(bank(5, 4, P)[:, j], XC[:, 8 + j, 0:P])
                    ins.then_inc(xt_full, 1)
                elif kind == "HID":
                    pe.wait_ge(kcp_ready, 4)
                    for kv in ("w1k", "w1v"):
                        pe.wait_ge(ring_full[at_unit[(kv, 0)] % STREAM], full_at[at_unit[(kv, 0)]])
                    for j in range(16):
                        for kv, src in ((0, KCP), (1, VCP)):
                            w1 = slot_view(at_unit[("w1v" if kv else "w1k", 0)], 16, P)
                            ins = mm(psum[64 * kv:64 * kv + 64, 7, 0:P], src[:, j // 8, :, j % 8], w1[:, j],
                                     start=(j == 0), stop=(j == 15))
                            if j == 15:
                                ins.then_inc(unit_done, 1)
                elif kind == "HT":
                    pe.wait_ge(hid_act, 1)
                    tr(bank(7, P, off=P), HIDT[:, 4]).then_inc(hid_full, 1)
                elif kind == "K2":
                    pe.wait_ge(hid_ready, 1)
                    mm(bank(7, 64, off=256), W2K[:].rearrange("p a b -> p (a b)"),
                       HID[:, 0].rearrange("p a b -> p (a b)"), start=True, stop=True).then_inc(k2_full, 1)
                elif kind == "V2":
                    pe.wait_ge(hvr_ready, 1)
                    pe.wait_ge(y_read, 8)
                    for hb in range(2):
                        lhs = HVR[:, hb].rearrange("p g r c -> p (g r c)")
                        ins = mm(bank(6, 64, off=128 + 64 * hb), lhs, W2V[:], start=True, stop=True)
                    ins.then_inc(v2_full, 1)
                elif kind == "A":
                    c, gr = k // 4, k % 4
                    if k == 0:
                        pe.wait_ge(cs_ready, 1)
                    else:
                        pe.wait_ge(csb_read, k)
                        pe.wait_ge(gm_ready, k)
                    if k >= 5:
                        pe.wait_ge(ecs_done, k - 4)
                    for r in range(REP):
                        mm(bank(3, REP, P)[:, r], ADT[:, c, REP * gr + r:REP * gr + r + 1].to_broadcast([P, P]),
                           UPP[:], start=True, stop=True)
                    mm(bank(4, P), XC[:, 8 + gr, P * c:P * c + P], XC[:, 12 + gr, P * c:P * c + P],
                       start=True, stop=True).then_inc(a_full, 1)
                elif kind == "ST":
                    pe.wait_ge(xde_ready, k + 1)
                    if k == 0:
                        pe.wait_ge(bt_ready, 1)
                        pe.wait_ge(k2_ready, 1)
                    else:
                        pe.wait_ge(st_ready, 1)
                    for j in range(2):
                        gr = 2 * k + j
                        ins = mm(bank(7, 2, 256)[:, j], BTK[:, gr], part(XDT, 2048 + 256 * gr, 256),
                                 start=True, stop=True)
                    ins.then_inc(st_full, 1)
                elif kind == "Y":
                    c, gr, b = k // 4, k % 4, k % 2
                    pe.wait_ge(m_done, k + 1)
                    if c == 0:
                        pe.wait_ge(xdt_ready, 2)
                    else:
                        pe.wait_ge(xdt_ready, 4)
                        pe.wait_ge(cte_done, k - 3)
                        pe.wait_ge(st_ready, 2)
                    if k:
                        pe.wait_ge(y_read, k)
                    for jj in range(2):
                        for hh in range(2):
                            r = 2 * jj + hh
                            h = REP * gr + r
                            o = psum[64 * hh:64 * hh + 64, 6, P * jj:P * jj + P]
                            ins = mm(o, part(XDT, D * c + DH * h, DH), E[:, b, P * r:P * r + P],
                                     start=True, stop=(c == 0))
                            if c == 1:
                                ins = mm(o, ST[:, DH * h:DH * h + DH], CTE[:, b, P * r:P * r + P],
                                         start=False, stop=True)
                    ins.then_inc(y_full, 1)
                elif kind == "GN":
                    pe.wait_ge(sq_ready, k + 1)
                    if k == 0:
                        pe.wait_ge(v2_ready, 1)
                    if k == 2:
                        pe.wait_ge(st_ready, 2)
                    o = bank(6 + k // 2, SEQ, off=SEQ * (k % 2))
                    mm(o, ONE[:], SQ[:, k % 2, 0:SEQ], start=True, stop=False)
                    mm(o, ONE[:], SQ[:, k % 2, SEQ:2 * SEQ], start=False, stop=True).then_inc(gn_full, 1)
                elif kind == "CS":
                    pe.wait_ge(csr_ready, 1)
                    for t in range(T):
                        for q in range(2):
                            ins = tr(bank(5, P, off=256 * t + P * q), CSR[:, 256 * q + P * t:256 * q + P * t + P])
                    ins.then_inc(cs_full, 1)
                elif kind == "CT":
                    for m in range(4):
                        taken(pe, "q", m)
                    pe.wait_ge(k2_ready, 1)
                    pe.wait_ge(xdt_ready, 4)
                    for q in range(2):
                        for j4 in range(4):
                            j = 4 * q + j4
                            ins = mm(psum[32 * j4:32 * j4 + 32, 5, 256 * q:256 * q + 256],
                                     BDK[:, j // 2].rearrange("p a b -> p (a b)"), QT[:, j, :],
                                     start=True, stop=True, tile_position=(0, 32 * j4))
                    ins.then_inc(csr_full, 1)
                elif kind == "CP":
                    pe.wait_ge(cp_ready, 1)
                    for t in range(T):
                        for hb in range(2):
                            ins = tr(bank(5, T, 2, P)[:, t, hb], PCS[:, t, 8 * hb:8 * hb + 8]
                                     .rearrange("p a b -> p (a b)"))
                    ins.then_inc(cp_full, 1)
                elif kind == "SC":
                    t, j = k // 8, k % 8
                    if k == 0:
                        pe.wait_ge(gm_ready, 8)
                        pe.wait_ge(ecs_done, 4)
                        pe.wait_ge(csb_read, 8)
                        taken(pe, "ks")
                        taken(pe, "kw")
                    else:
                        pe.wait_ge(nm_ready, k)
                    nk = P * (t + 1)
                    for y in range(2):
                        for hh in range(2):
                            s = slice(64 * hh, 64 * hh + 64)
                            ins = mm(psum[:, 3 + hh, 256 * y:256 * y + nk], QT[s, j, P * t:P * t + P],
                                     KD[s, y, j // 2, 0:nk], start=True, stop=True)
                    ins.then_inc(sc_full, 1)
                elif kind == "PT":
                    t = k // 8
                    pe.wait_ge(p_ready, k + 1)
                    if k == 0:
                        pe.wait_ge(cp_read, 1)
                        pe.wait_ge(gn_read, 2)
                    else:
                        pe.wait_ge(pt_act, k)
                        pe.wait_ge(pt_dve, k)
                    for hh in range(2):
                        for y in range(2):
                            for bl in range(t + 1):
                                ins = tr(bank(5 + hh, P, off=P * (y * (t + 1) + bl)),
                                         SP[k % 3][:, hh, y, P * bl:P * bl + P])
                    ins.then_inc(pt_full, 1)
                elif kind == "PV":
                    t, j = k // 8, k % 8
                    if k == 0:
                        taken(pe, "vs")
                        taken(pe, "vw")
                        pe.wait_ge(v2_ready, 1)
                        pe.wait_ge(st_ready, 2)
                        pe.wait_ge(gy_ready, 4)
                    else:
                        pe.wait_ge(pv_read, k)
                    pe.wait_ge(pt_act, k + 1)
                    pe.wait_ge(pt_dve, k + 1)
                    mm(bank(7, P), VBD[:, j // 4, 2 * (j % 4):2 * (j % 4) + 2].rearrange("p a b -> p (a b)"),
                       PCT[:, t, j // 4], start=True, stop=False, skip_group_check=True)
                    for y in range(2):
                        for bl in range(t + 1):
                            for hh in range(2):
                                last = y == 1 and bl == t
                                ins = mm(psum[64 * hh:64 * hh + 64, 7, 0:P],
                                         VT[:, y, bl, DH * (j // 2):DH * (j // 2) + DH],
                                         PTS[:, hh, P * (y * (t + 1) + bl):P * (y * (t + 1) + bl) + P],
                                         start=False, stop=last, skip_group_check=True)
                    ins.then_inc(pv_full, 1)
                elif kind == "MT":
                    pe.wait_ge(mg_ready, k + 1)
                    if k >= 2:
                        pe.wait_ge(mt_low, k - 1)
                    for kk in range(2):
                        for t in range(T):
                            ins = tr(bank(3 + k % 2, 2, T, P)[:, kk, t],
                                     MG[:, t, P * (2 * k + kk):P * (2 * k + kk) + P])
                    ins.then_inc(mt_full, 1)

            for b in range(4):
                pe.wait_ge(h2_ready, 2 if b < 2 else 4)
                for kk in range(2):
                    for t in range(T):
                        ins = tr(bank(3 + b, 2, T, P)[:, kk, t], H2[:, t, P * (2 * b + kk):P * (2 * b + kk + 1)])
                ins.then_inc(h2t_full, 1)
            pe.wait_ge(late_in, 16 * 4)
            for t in range(T):
                for k in range(KT):
                    if t == 0 and k % 2 == 0:
                        pe.wait_ge(h2t_dve if k == 4 else h2t_act, (1, 2, 1, 3)[k // 2])
                    ins = mm(bank(7, EXPERTS, off=EXPERTS * t), H2T[:, k, P * t:P * t + P], RW_[:, k, :],
                             start=(k == 0), stop=(k == KT - 1))
            ins.then_inc(rt_full, 1)
            pe.wait_ge(msk_ready, 1)
            mm(bank(3, EXPERTS), UST[:], MSK[:, 0], start=True, stop=True)
            mm(bank(3, EXPERTS, off=32), ONE[:], MSK[:, 0], start=True, stop=False)
            mm(bank(3, EXPERTS, off=32), UST[:], MSK[:, 1], start=False, stop=True)
            mm(bank(3, EXPERTS, off=64), ONE[:], MSK[:, 0], start=True, stop=False)
            mm(bank(3, EXPERTS, off=64), ONE[:], MSK[:, 1], start=False, stop=True).then_inc(rk_full, 1)
            pe.wait_ge(cw_ready, 1)
            for t in range(T):
                ins = tr(bank(4, T, P)[:, t], CWP[:, t].rearrange("p a b -> p (a b)"))
            ins.then_inc(cwt_full, 1)
            def gather():
                for k in range(KT):
                    for t in range(T):
                        ins = mm(bank(5 + k // 4, P, off=P * (k % 4)), H2[:, t, P * k:P * k + P],
                                 SPR[:, t].rearrange("p a b -> p (a b)"), start=(t == 0), stop=(t == T - 1))
                ins.then_inc(xte_full, 1)

            def combine(n, s):
                pe.wait_ge(o_read, n * 2 + 1)
                for t in range(T):
                    for h in range(2):
                        r = slice(64 * h, 64 * h + 64)
                        ins = mm(psum[:, 3 + 2 * t + h, :], CTS[r, 1 - s, t], YSB[r, :], start=True, stop=True)
                    ins.then_inc(o_full, 1)

            r = rounds(pe)
            with pe.Fori(0, r * EX2) as i:
                for s in range(2):
                    n = i * 2 + s
                    if s == 0:
                        pe.wait_ge(spr_ready, i + 1)
                        pe.wait_ge(o_read, n * 2 + 1)
                        gather()
                        pe.wait_ge(prep_done, i + 1)
                    pe.wait_ge(gu_read, n + 1)
                    for c in range(4):
                        mm(psum[64 * (c % 2):64 * (c % 2) + 64, c // 2, :], OHE[0:EXPERTS, s],
                           BGU[0:EXPERTS, 512 * c:512 * c + 512], start=True, stop=False)
                    if s == 0:
                        pe.wait_ge(xte_ready, i + 1)
                    for k in range(KT):
                        w = places[slot_of(s, k)]
                        pe.wait_ge(slot_full[slot_of(s, k)], slot_loads(i, s, k))
                        for c in range(4):
                            ins = mm(psum[64 * (c % 2):64 * (c % 2) + 64, c // 2, :], XTS[:, k, s],
                                     w[:, 512 * c:512 * c + 512], start=False, stop=(k == KT - 1))
                        ins.then_inc(unit_done, 1)
                    pe.wait_ge(at_ready, n + 1)
                    for t in range(T):
                        ins = tr(bank(7, T, P)[:, t], CPR[:, t, s])
                    ins.then_inc(ct_full, 1)
                    pe.wait_ge(y_ready, n + 1)
                    combine(n, s)
                    pe.wait_ge(act_ready, n + 1)
                    pe.wait_ge(ct_ready, n + 1)
                    for jb in range(4):
                        ins = tr(bank(7, 4, P)[:, jb], ABU[:, P * jb:P * jb + P])
                    ins.then_inc(at_full, 1)
                    pe.wait_ge(at_ready, n + 2)
                    for k in range(KT):
                        w = places[slot_of(s, 8 + k // 2)]
                        if k % 2 == 0:
                            pe.wait_ge(slot_full[slot_of(s, 8 + k // 2)], slot_loads(i, s, 8 + k // 2))
                        q, hf = k // 4, (k // 2) % 2
                        lhs = ATS[:, 2 * q + k % 2, 64 * hf:64 * hf + 64]
                        for h in range(2):
                            ins = mm(psum[64 * h:64 * h + 64, 2, :], lhs,
                                     w[:, 1024 * (k % 2) + 512 * h:1024 * (k % 2) + 512 * h + 512],
                                     start=(k == 0), stop=(k == KT - 1))
                        if k % 2:
                            ins.then_inc(unit_done, 1)
            pe.wait_ge(y_ready, r * EXPERTS + 1)
            pe.wait_ge(ct_ready, r * EXPERTS)
            combine(r * EXPERTS, 0)

        @block.scalar
        def _(act):
            own = Own(act, act_own)
            a = nc.scalar.activation
            rows = [(mix_norm_w, 8), (ssm_norm_w, 8), (conv_b, 16), (conv_w, 64), (cmp_pos_k, 16),
                    (cmp_pos_v, 16)]
            at = 0
            for w, nrow in rows:
                flat = w[0] if len(w.shape) == 2 else w[0].rearrange("a b -> (a b)")
                act.dma_start(PR[at:at + nrow, :], flat.rearrange("(a b) -> a b", b=P)).then_inc(rows_in, 16)
                at += nrow
            act.wait_ge(x_in[0], 16)
            a(part(YV, 0, D), X[:, 0], ACT.Square, accum_out=ss[:, 0:1]).then_inc(ss_ready, 1)
            act.wait_ge(dve_own, 1)
            a(ss[:, 2:4], ss[:, 0:2], ACT.Sqrt).then_inc(sq_root, 1)

            def split(u):
                i = SPLIT_UNITS.index(u)
                act.wait_ge(ring_full[u % STREAM], full_at[u])
                if i >= SPLITS:
                    act.wait_ge(unit_done, SPLIT_UNITS[i - SPLITS] + 1)
                n = KT * (64 if UNITS[u][0] == "small" else 256)
                a(WH[i % SPLITS][:, 0:n], slot_view(u, n), ACT.Copy).then_inc(wh_ready, 1)

            act.wait_ge(par_ready, 1)
            for b in range(4):
                act.wait_ge(ht_full, b + 1)
                for kk in range(2):
                    ins = a(HTH[:, 2 * b + kk], bank(NORM_BANKS[b], 2, SEQ)[:, kk], ACT.Copy,
                            scale=PC[:, 2 * b + kk:2 * b + kk + 1])
                ins.then_inc(ht_act, 1)
            act.wait_ge(wh_ready, 1)
            split(1)

            n_th = 0
            for kind, k in TOKENS:
                if kind == "W":
                    split(k)
                elif kind == "LD":
                    act.wait_ge(pv_read, 16)
                    act.wait_ge(unit_done, at_unit[("bs", 3)] + 1)
                    act.dma_start(RW_, router_w[0].rearrange("(k p) e -> p k e", p=P)).then_inc(late_in, 16)
                    act.dma_start(WFF, ffn_norm_w[0].partition_broadcast(P)).then_inc(late_in, 16)
                    act.dma_start(WFN, final_norm_w.partition_broadcast(P)).then_inc(late_in, 16)
                    act.dma_start(BGU[0:EXPERTS, :], b_gate_up[0]).then_inc(late_in, 16)
                elif kind == "YS":
                    act.wait_ge(yn_ready, 1)
                    a(YSH[:], YV[:], ACT.Copy).then_inc(ys_high, 1)
                elif kind == "P":
                    what, m = UNITS[k]
                    if what == "wo":
                        act.wait_ge(x2_ready, m + 1)
                        for t in range(T):
                            ins = a(SQX[:, t, 256 * m:256 * m + 256], X[:, t, 256 * m:256 * m + 256], ACT.Square,
                                    accum_out=RT[:, 9, t, m:m + 1])
                        ins.then_inc(sq2_ready, 1)
                        if m == 0:
                            a(junk[:, 0:1], ss[:, 6:7], ACT.Sqrt)
                    if what in ("w1k", "w1v", "small", "vs", "bs", "bn", "wo"):
                        continue
                    b = bank_of[k]
                    pv = bank(b, 2, SEQ)
                    act.wait_ge(unit_done, k + 1)
                    if what == "xbc":
                        for f in range(2):
                            ch = 2 * m + f
                            ins = a(XC[:, ch], pv[:, f], ACT.Identity, scale=PH[:, 16 + 48 + ch:16 + 49 + ch],
                                    bias=PH[:, ch:ch + 1])
                        ins.then_inc(hv_done, 1)
                    elif what in ("kc", "ks", "vc", "kw"):
                        if what in ("ks", "kw"):
                            y = 0 if what == "ks" else 1
                            for f in range(2):
                                for src in range(2):
                                    s = slice(64 * src, 64 * src + 64)
                                    a(KD[64 * src:64 * src + 64, y, 2 * f + src], pv[s, f], ACT.Copy)
                                    ins = a(KD[64 * (1 - src):64 * (1 - src) + 64, y, 2 * f + src], pv[s, f],
                                             ACT.Copy)
                            ins.then_inc(proj_free[b], 1)
                        else:
                            dst = KC2 if what == "kc" else VC2
                            for f in range(2):
                                for src in range(2):
                                    s = slice(64 * src, 64 * src + 64)
                                    a(dst[0:64, 2 * f + src, :], pv[s, f], ACT.Copy)
                                    ins = a(dst[64:128, 2 * f + src, 0:SEQ - 1], pv[s, f, 1:SEQ], ACT.Copy)
                            ins.then_inc(proj_free[b], 1)
                    elif what == "vw":
                        a(VT[:, 1], pv, ACT.Copy).then_inc(proj_free[b], 1)
                    elif what == "q":
                        a(QT[:, 2 * m:2 * m + 2], pv, ACT.Copy).then_inc(proj_free[b], 1)
                    elif what == "z":
                        if n_th >= 2:
                            act.wait_ge(th_used, n_th - 1)
                        a(TH[:, n_th % 2], psum[:, b], ACT.Tanh, scale=0.5).then_inc(th_ready, 1)
                        n_th += 1
                    elif what == "mg":
                        if m == 0:
                            act.wait_ge(y_full, 8)
                            act.wait_ge(cte_done, 4)
                        a(GA[:, :, 256 * m:256 * m + 256], pv, ACT.Tanh, scale=0.5).then_inc(proj_free[b], 1)
                elif kind == "F":
                    if n_th >= 2:
                        act.wait_ge(th_used, n_th - 1)
                    b = bank_of[k]
                    act.wait_ge(proj_free[b], freed[k] + 1)
                    a(TH[:, n_th % 2], XC[:, 2 * k:2 * k + 2].rearrange("p a b -> p (a b)"), ACT.Tanh
                      ).then_inc(th_ready, 1)
                    n_th += 1
                elif kind == "DT":
                    taken(act, "small")
                    own.mark(a(NG[:], SM[:, :, 16:64], ACT.Tanh, scale=0.5))
                    act.wait_ge(small_in, 16 * 8)
                    own.mark(a(ALG[:], ALG[:], ACT.Exp))
                    act.wait_ge(dt_e, 1)
                    a(DT[:, 2], DT[:, 1], ACT.Exp, scale=-1.0).then_inc(dt_w, 1)
                    act.wait_ge(dt_e, 2)
                    a(DT[:, 4], DT[:, 3], ACT.Ln).then_inc(dt_l, 1)
                    act.wait_ge(dt_l, 1)
                elif kind == "S1":
                    act.wait_ge(cs_ready, 1)
                    a(DE[:], DE[:], ACT.Exp).then_inc(de_ready, 1)
                elif kind == "HID":
                    act.wait_ge(hid_t3, 1)
                    a(HIDT[:, 3], HIDT[:, 2], ACT.Tanh, scale=0.7978845608028654).then_inc(hid_th, 1)
                elif kind == "A":
                    act.wait_ge(csb_read, k + 1)
                    a(E[:, k % 2], E[:, k % 2], ACT.Exp).then_inc(e_exp, 1)
                    if k >= 4:
                        if k >= 6:
                            act.wait_ge(cte_done, k - 5)
                        a(EC[:, k % 2], psum[:, 3], ACT.Exp).then_inc(ecs_done, 1)
                elif kind == "GY":
                    act.wait_ge(gy_ready, k + 1)
                    if k == 0:
                        act.wait_ge(cte_done, 4)
                    if k == 1:
                        act.wait_ge(cs_full, 1)
                    if k >= 2:
                        act.wait_ge(gn_full, k - 1)
                    a(SQ[:, k % 2], YV[:, 2 * k:2 * k + 2].rearrange("p a b -> p (a b)"), ACT.Square
                      ).then_inc(sq_ready, 1)
                elif kind == "GR":
                    act.wait_ge(gn_full, 4)
                    for b in range(2):
                        a(CTE[:, b], psum[:, 6 + b], ACT.Ln, scale=0.25 / 256, bias=ss[:, 6:7]).then_inc(gn_read, 1)
                    act.wait_ge(gn_read, 2)
                    a(CTE[:], CTE[:], ACT.Exp, scale=-0.5).then_inc(rb_ready, 1)
                elif kind == "CT":
                    act.wait_ge(csr_full, 1)
                    act.wait_ge(cte_done, 4)
                    act.wait_ge(y_full, 8)
                    a(CSR, psum[:, 5], ACT.Copy).then_inc(csr_ready, 1)
                elif kind == "CS":
                    act.wait_ge(cs_sub, 1)
                    a(PCS[:], PCS[:], ACT.Exp).then_inc(cs_exp, 1)
                elif kind == "CP":
                    act.wait_ge(cp_full, 1)
                    a(PCT[:], bank(5, T, 2, P), ACT.Copy).then_inc(cp_read, 1)
                elif kind == "SC":
                    b, nk = k % 3, P * (k // 8 + 1)
                    act.wait_ge(nm_ready, k + 1)
                    for hh in range(2):
                        for y in range(2):
                            q = 2 * hh + y
                            ins = a(SP[b][:, hh, y, 0:nk], SP[b][:, hh, y, 0:nk], ACT.Exp,
                                    bias=AMX[:, b, 1, q:q + 1], accum_out=AMX[:, b, 2, q:q + 1])
                    ins.then_inc(ex_done, 1)
                elif kind == "PT":
                    n = 2 * P * (k // 8 + 1)
                    act.wait_ge(pt_full, k + 1)
                    if k >= 1:
                        act.wait_ge(pv_full, k)
                    a(PTS[:, 0, 0:n], psum[:, 5, 0:n], ACT.Copy).then_inc(pt_act, 1)
                elif kind == "PV":
                    t, j = k // 8, k % 8
                    act.wait_ge(pv_full, k + 1)
                    a(OTH[:, j, P * t:P * t + P], bank(7, P), ACT.Copy).then_inc(ot_high, 1)
                elif kind == "MT":
                    act.wait_ge(mt_full, k + 1)
                    a(HTH[:, 2 * k:2 * k + 2].rearrange("p a b -> p (a b)"), psum[:, 3 + k % 2], ACT.Copy,
                      scale=0.5).then_inc(mt_ready, 1)

            act.wait_ge(unit_done, NU)
            for h in range(2):
                act.dma_start(YSB[64 * h:64 * h + EXPERTS], b_down[0][:, 512 * h:512 * h + 512]
                              ).then_inc(bd_in, 16)

            act.wait_ge(lg_ready, 1)
            a(ss[:, 2:4], ss[:, 0:2], ACT.Sqrt).then_inc(sq_root, 1)
            a(junk[:, 0:1], ss[:, 6:7], ACT.Exp)
            for b in (0, 1, 3):
                act.wait_ge(h2t_full, b + 1)
                a(H2T[:, 2 * b:2 * b + 2].rearrange("p a b -> p (a b)"), psum[:, 3 + b], ACT.Copy
                  ).then_inc(h2t_act, 1)
            act.wait_ge(mx_ready, 1)
            for t in range(T):
                ins = a(RT[:, 2, t, 0:TOPK], MX8[:, t, 0:TOPK], ACT.Exp, bias=RT[:, 1, t, 0:1],
                        accum_out=RT[:, 3, t, 0:1])
            ins.then_inc(te_ready, 1)

            def tokens_in():
                for b in range(2):
                    ins = a(XTS[:, 4 * b:4 * b + 4].rearrange("p a b c -> p (a b c)"), psum[:, 5 + b], ACT.Copy)
                ins.then_inc(xte_ready, 1)

            act.wait_ge(cwt_full, 1)
            own.mark(a(CTS[:, 1], bank(4, T, P), ACT.Copy))
            own.settle()
            act.wait_ge(zero_ready, 1)
            act.wait_ge(bd_in, 16 * 2)
            act.sem_inc(y_ready, 1)
            act.sem_inc(at_ready, 1)
            r = rounds(act)
            with act.Fori(0, r * EX2) as i:
                for s in range(2):
                    n = i * 2 + s
                    if s == 0:
                        act.wait_ge(xte_full, i + 1)
                        tokens_in()
                    act.wait_ge(ct_full, n + 1)
                    a(CTS[:, s], bank(7, T, P), ACT.Copy).then_inc(ct_ready, 1)
                    act.wait_ge(g_ready, n + 1)
                    a(SGA, GBU, ACT.Sigmoid, scale=1.702).then_inc(sig_ready, 1)
                    act.wait_ge(at_full, n + 1)
                    a(ATS.rearrange("p a b -> p (a b)"), psum[:, 7], ACT.Copy).then_inc(at_ready, 1)
                    act.wait_ge(unit_done, n * UNITS_E + (NU + UNITS_E))
                    a(YSB, psum[:, 2], ACT.Copy).then_inc(y_ready, 1)
            a(junk[:, 0:1], ss[:, 6:7], ACT.Sqrt)
            for t in range(T):
                act.wait_ge(final_in, t + 1)
                a(SQX[:, t], X[:, t], ACT.Square, accum_out=ss[:, t:t + 1]).then_inc(ss_ready, 1)
            act.wait_ge(lg_ready, 3)
            a(ss[:, 2:4], ss[:, 0:2], ACT.Sqrt).then_inc(sq_root, 1)

        @block.vector
        def _(dve):
            own = Own(dve, dve_own)
            v = nc.vector

            dve.wait_ge(x_in[1], 16)
            v.tensor_tensor_reduce(part(YV, D, D), X[:, 1], X[:, 1], 1.0, 0.0, ALU.mult, ALU.add, ss[:, 1:2]
                                   ).then_inc(ss_ready, 1)
            dve.wait_ge(ss_ready, 2)
            own.mark(v.tensor_scalar(ss[:, 0:2], ss[:, 0:2], 1.0 / D, EPS, ALU.mult, ALU.add))
            dve.wait_ge(sq_root, 1)
            own.mark(v.reciprocal(ss[:, 4:6], ss[:, 2:4]))
            own.settle()
            for t in range(T):
                v.tensor_scalar(HN[:, t], X[:, t], ss[:, 4 + t:5 + t], None, ALU.mult).then_inc(hn_ready, 1)
            own.mark(v.memset(ss[:, 6:7], EPS))
            dve.wait_ge(par_full, 1)
            own.mark(v.tensor_copy(PC[:], bank(4, P)))
            own.settle()
            own.mark(v.tensor_scalar(PH[:, 0:80], PC[:, 16:96], 0.5, None, ALU.mult))
            own.mark(v.tensor_scalar(PH[:, 80:88], PC[:, 8:16], 0.5, None, ALU.mult))
            own.settle()
            dve.sem_inc(par_ready, 1)

            def split(u):
                i = SPLIT_UNITS.index(u)
                dve.wait_ge(wh_ready, i + 1)
                n = KT * (64 if UNITS[u][0] == "small" else 256)
                v.tensor_tensor(WL[i % SPLITS][:, 0:n], slot_view(u, n), WHF[i % SPLITS][:, 0:n], ALU.subtract
                                ).then_inc(wl_ready, 1)

            dve.wait_ge(ring_full[0], full_at[0])
            own.mark(v.tensor_copy(WH[0][:], slot_view(0, SLOT)))
            own.settle()
            dve.sem_inc(wh_ready, 1)
            v.tensor_tensor(WL[0][:], slot_view(0, SLOT), WHF[0], ALU.subtract).then_inc(wl_ready, 1)
            for b in range(4):
                dve.wait_ge(ht_act, b + 1)
                for kk in range(2):
                    j = 2 * b + kk
                    ins = v.scalar_tensor_tensor(out=HTL[:, j], in0=bank(NORM_BANKS[b], 2, SEQ)[:, kk],
                                                 scalar=PC[:, j:j + 1], in1=HTHF[:, j], op0=ALU.mult,
                                                 op1=ALU.subtract)
                ins.then_inc(ht_low, 1)
            split(1)

            n_th = 0
            for kind, k in TOKENS:
                if kind == "W":
                    if k not in POOL_UNITS:
                        split(k)
                elif kind == "YS":
                    dve.wait_ge(ys_high, 1)
                    v.tensor_tensor(YSL[:], YV[:], YSHF, ALU.subtract).then_inc(ys_ready, 1)
                elif kind == "PV":
                    t, j = k // 8, k % 8
                    dve.wait_ge(ot_high, k + 1)
                    v.tensor_tensor(OTL[:, j, P * t:P * t + P], bank(7, P), OTHF[:, j, P * t:P * t + P],
                                    ALU.subtract).then_inc(pv_read, 1)
                elif kind == "MT":
                    dve.wait_ge(mt_ready, k + 1)
                    v.scalar_tensor_tensor(out=HTL[:, 2 * k:2 * k + 2].rearrange("p a b -> p (a b)"),
                                           in0=psum[:, 3 + k % 2], scalar=0.5,
                                           in1=HTHF[:, 2 * k:2 * k + 2].rearrange("p a b -> p (a b)"),
                                           op0=ALU.mult, op1=ALU.subtract).then_inc(mt_low, 1)
                elif kind == "P":
                    what, m = UNITS[k]
                    if what in ("w1k", "w1v", "kc", "vc", "ks", "kw", "vw", "q", "mg"):
                        continue
                    b = bank_of[k]
                    pv = bank(b, 2, SEQ)
                    dve.wait_ge(unit_done, k + 1)
                    if what == "xbc":
                        dve.wait_ge(hv_done, m + 1)
                        for tap in (2, 1, 0):
                            back = 3 - tap
                            for f in range(2):
                                ch = 2 * m + f
                                w = PH[:, 16 + 16 * tap + ch:17 + 16 * tap + ch]
                                o = XC[:, ch, back:SEQ]
                                ins = v.scalar_tensor_tensor(out=o, in0=pv[:, f, 0:SEQ - back], scalar=w,
                                                             in1=o, op0=ALU.mult, op1=ALU.add)
                                if not (tap == 0 and f == 1):
                                    own.mark(ins)
                                else:
                                    ins.then_inc(proj_free[b], 1)
                                if f == 1 and tap:
                                    own.settle()
                    elif what == "small":
                        v.tensor_copy(SM[:], bank(b, T, 64)).then_inc(proj_free[b], 1)
                    elif what == "vs":
                        v.tensor_copy(VT[:, 0], pv).then_inc(proj_free[b], 1)
                    elif what == "z":
                        dve.wait_ge(th_ready, n_th + 1)
                        zs = ZS[:, 2 * m:2 * m + 2].rearrange("p a b -> p (a b)")
                        own.mark(v.scalar_tensor_tensor(out=zs, in0=TH[:, n_th % 2], scalar=1.0,
                                                        in1=psum[:, b], op0=ALU.add, op1=ALU.mult))
                        own.settle()
                        dve.sem_inc(proj_free[b], 1)
                        dve.sem_inc(th_used, 1)
                        n_th += 1
                    elif what == "bs":
                        v.scalar_tensor_tensor(out=GA[:, :, 256 * m:256 * m + 256],
                                               in0=GA[:, :, 256 * m:256 * m + 256], scalar=1.0, in1=pv,
                                               op0=ALU.add, op1=ALU.mult).then_inc(proj_free[b], 1)
                    elif what == "bn":
                        ga = GA[:, :, D + 256 * m:D + 256 * m + 256]
                        v.scalar_tensor_tensor(out=ga, in0=ga, scalar=1.0, in1=pv,
                                               op0=ALU.add, op1=ALU.mult).then_inc(proj_free[b], 1)
                        dve.wait_ge(proj_free[b], freed[k] + 1)
                        mg = MG[:, :, 256 * m:256 * m + 256]
                        v.tensor_tensor(mg, mg, ga, ALU.add).then_inc(mg_ready, 1)
                    elif what == "wo":
                        xo = X[:, :, 256 * m:256 * m + 256]
                        v.tensor_tensor(xo, xo, pv, ALU.add).then_inc(x2_ready, 1)
                        dve.wait_ge(x2_ready, m + 1)
                        dve.sem_inc(proj_free[b], 1)
                elif kind == "F":
                    dve.wait_ge(th_ready, n_th + 1)
                    dve.wait_ge(proj_free[bank_of[k]], freed[k] + 1)
                    xc = XC[:, 2 * k:2 * k + 2].rearrange("p a b -> p (a b)")
                    v.scalar_tensor_tensor(out=xc, in0=TH[:, n_th % 2], scalar=1.0, in1=xc, op0=ALU.add,
                                           op1=ALU.mult).then_inc(th_used, 1)
                    n_th += 1
                elif kind == "DT":
                    taken(dve, "small")
                    dve.wait_ge(small_in, 16 * 8)
                    b16 = [P, T, HEADS]
                    own.mark(v.tensor_tensor(DT[:, 0], SM[:, :, 0:16], DTB[:].unsqueeze(1).to_broadcast(b16), ALU.add))
                    own.settle()
                    own.mark(v.tensor_scalar(DT[:, 5], DT[:, 0], -1.0, None, ALU.mult))
                    own.settle()
                    v.tensor_tensor(DT[:, 1], DT[:, 0], DT[:, 5], ALU.max).then_inc(dt_e, 1)
                    dve.wait_ge(dt_w, 1)
                    v.tensor_scalar(DT[:, 3], DT[:, 2], 1.0, None, ALU.add).then_inc(dt_e, 1)
                    dve.wait_ge(dt_e, 2)
                    own.mark(v.scalar_tensor_tensor(out=DT[:, 6], in0=DT[:, 3], scalar=-1.0, in1=DT[:, 2],
                                                    op0=ALU.add, op1=ALU.subtract))
                    own.mark(v.reciprocal(DT[:, 7], DT[:, 3]))
                    own.settle()
                    own.mark(v.tensor_tensor(DT[:, 6], DT[:, 6], DT[:, 7], ALU.mult))
                    dve.wait_ge(dt_l, 1)
                    own.settle()
                    own.mark(v.tensor_tensor(DT[:, 4], DT[:, 4], DT[:, 6], ALU.subtract))
                    own.settle()
                    own.mark(v.scalar_tensor_tensor(out=DT[:, 0], in0=DT[:, 0], scalar=0.0, in1=DT[:, 4],
                                                    op0=ALU.max, op1=ALU.add))
                    own.settle()
                    dve.wait_ge(act_own, 2)
                    v.scalar_tensor_tensor(out=ADT[:], in0=DT[:, 0], scalar=-1.0,
                                           in1=ALG[:].unsqueeze(1).to_broadcast(b16), op0=ALU.mult,
                                           op1=ALU.mult).then_inc(adt_ready, 1)
                    own.mark(v.tensor_scalar(NG[:], NG[:], 0.5, 0.5, ALU.mult, ALU.add))
                elif kind == "S1":
                    dve.wait_ge(s1_full, 1)
                    own.mark(v.tensor_copy(CS[:], bank(4, T, 16)))
                    own.settle()
                    own.mark(v.tensor_tensor(DE[:], bank(4, 16, off=32), CS[:, 0], ALU.subtract))
                    own.settle()
                    dve.sem_inc(cs_ready, 1)
                elif kind == "XT":
                    c, half = k // 2, k % 2
                    dve.wait_ge(xt_full, k + 1 + (k >= 2))
                    v.tensor_tensor(part(XDT, D * c + 512 * half, 8, DH), bank(5, 8, DH),
                                    DT[:, 0, c, 8 * half:8 * half + 8].unsqueeze(2).to_broadcast([P, 8, DH]),
                                    ALU.mult).then_inc(xdt_ready, 1)
                    if k == 0:
                        for i, (src, dst, kind_) in enumerate(((KC2, KCP, "kc"), (VC2, VCP, "vc"))):
                            taken(dve, kind_)
                            for half in range(2):
                                nb = 16 - half
                                d4 = dst[:, half].rearrange("p (g c) j -> p g c j", g=GROUPS)[:, :, 0:nb]
                                s4 = src.rearrange("p g (c j two) -> p g c j two", c=16, two=2
                                                   )[:, :, half:16, :, 0]
                                p0 = 96 + 16 * i + 8 * half
                                for g4 in range(GROUPS):
                                    ins = v.tensor_tensor(d4[:, g4], s4[:, g4], PC[:, p0:p0 + 8].unsqueeze(1)
                                                          .to_broadcast([P, nb, 8]), ALU.add)
                                ins.then_inc(kcp_ready, 1)
                elif kind == "BT":
                    dve.wait_ge(xt_full, 3)
                    v.tensor_copy(BTK, bank(5, 4, P)).then_inc(bt_ready, 1)
                elif kind == "HID":
                    dve.wait_ge(unit_done, at_unit[("w1v", 0)] + 1)
                    h = HIDT
                    own.mark(v.tensor_copy(h[:, 0], bank(7, P)))
                    own.settle()
                    own.mark(v.tensor_tensor(h[:, 1], h[:, 0], h[:, 0], ALU.mult))
                    own.settle()
                    own.mark(v.tensor_scalar(h[:, 1], h[:, 1], 0.044715, 1.0, ALU.mult, ALU.add))
                    own.settle()
                    v.tensor_tensor(h[:, 2], h[:, 1], h[:, 0], ALU.mult).then_inc(hid_t3, 1)
                    dve.wait_ge(hid_th, 1)
                    v.scalar_tensor_tensor(out=h[:, 4], in0=h[:, 3], scalar=1.0, in1=h[:, 0], op0=ALU.add,
                                           op1=ALU.mult).then_inc(hid_act, 1)
                elif kind == "HT":
                    dve.wait_ge(hid_full, 1)
                    v.tensor_copy(HID[:].rearrange("p a b c -> p (a b c)"), bank(7, P, off=P)
                                  ).then_inc(hid_ready, 1)
                elif kind == "K2":
                    dve.wait_ge(k2_full, 1)
                    dve.wait_ge(const_done, 2)
                    for hh in range(2):
                        s = slice(64 * hh, 64 * hh + 64)
                        own.mark(v.tensor_scalar(BDK[s, :, hh, :], psum[s, 7, 256:320].rearrange(
                            "p (g c) -> p g c", g=GROUPS), 0.5, None, ALU.mult))
                    own.settle()
                    dve.sem_inc(k2_ready, 1)
                elif kind == "V2":
                    dve.wait_ge(y_full, 8)
                    for hb in range(2):
                        for g2 in range(2):
                            own.mark(v.tensor_copy(HVR[:, hb, g2], HID[:, 1, 2 * hb + g2].unsqueeze(1)
                                                   .to_broadcast([P, REP, 16])))
                    own.settle()
                    dve.sem_inc(hvr_ready, 1)
                    dve.wait_ge(v2_full, 1)
                    for hb in range(2):
                        own.mark(v.tensor_tensor(VBD[:, hb], bank(6, DH, off=128 + 64 * hb).unsqueeze(1)
                                                 .to_broadcast([P, 8, DH]),
                                                 HM[:].unsqueeze(2).to_broadcast([P, 8, DH]), ALU.mult))
                    own.settle()
                    dve.sem_inc(v2_ready, 1)
                elif kind == "A":
                    c, gr, b = k // 4, k % 4, k % 2
                    dve.wait_ge(a_full, k + 1)
                    if k >= 2:
                        dve.wait_ge(y_full, k - 1)
                    for r in range(REP):
                        ins = v.tensor_scalar(E[:, b, P * r:P * r + P], bank(3, REP, P)[:, r],
                                              CS[:, c, REP * gr + r:REP * gr + r + 1], 0.0,
                                              ALU.subtract, ALU.min)
                    ins.then_inc(csb_read, 1)
                    if k >= 2:
                        dve.wait_ge(m_done, k - 1)
                    v.tensor_tensor(GM[:, b], bank(4, P), UPP[:], ALU.mult).then_inc(gm_ready, 1)
                elif kind == "ST":
                    dve.wait_ge(st_full, k + 1)
                    v.tensor_copy(ST[:, 512 * k:512 * k + 512], psum[:, 7]).then_inc(st_ready, 1)
                elif kind == "Y":
                    c, gr = k // 4, k % 4
                    dve.wait_ge(y_full, k + 1)
                    if k == 0:
                        dve.wait_ge(xd_done, 1)
                    yv = YV[:, 2 * gr:2 * gr + 2, P * c:P * c + P]
                    v.tensor_tensor(yv, yv, bank(6, 2, P), ALU.add).then_inc(y_read, 1)
                elif kind == "GY":
                    if k == 0:
                        dve.wait_ge(y_read, 8)
                    yv = YV[:, 2 * k:2 * k + 2]
                    v.tensor_tensor(yv, yv, ZS[:, 2 * k:2 * k + 2], ALU.mult).then_inc(gy_ready, 1)
                elif kind == "GX":
                    dve.wait_ge(rb_ready, 1)
                    for j in range(KT):
                        own.mark(v.scalar_tensor_tensor(
                            out=YV[:, j], in0=YV[:, j], scalar=PH[:, 80 + j:81 + j],
                            in1=part(CTE, SEQ * (j // 2), SEQ), op0=ALU.mult, op1=ALU.mult))
                    own.settle()
                    dve.sem_inc(yn_ready, 1)
                elif kind == "CS":
                    dve.wait_ge(cs_full, 1)
                    for t in range(T):
                        own.mark(v.scalar_tensor_tensor(
                            out=PCS[:, t], in0=bank(5, HEADS, 16, off=256 * t), scalar=DH ** -0.5,
                            in1=CMC[:, t].unsqueeze(1).to_broadcast([P, HEADS, 16]), op0=ALU.mult, op1=ALU.add))
                    own.settle()
                    own.mark(v.tensor_reduce(CST[:, 0], PCS[:], AX.X, ALU.max))
                    own.settle()
                    own.mark(v.tensor_scalar(CST[:, 0], CST[:, 0], -1e25, None, ALU.max))
                    own.settle()
                    v.tensor_tensor(PCS[:], PCS[:], CST[:, 0].unsqueeze(3).to_broadcast([P, T, HEADS, 16]),
                                    ALU.subtract).then_inc(cs_sub, 1)
                    dve.wait_ge(cs_exp, 1)
                    own.mark(v.tensor_reduce(CST[:, 1], PCS[:], AX.X, ALU.add))
                    own.settle()
                    own.mark(v.tensor_scalar(CST[:, 1], CST[:, 1], 1e-30, None, ALU.max))
                    own.settle()
                    own.mark(v.reciprocal(CST[:, 2], CST[:, 1]))
                    own.settle()
                    own.mark(v.tensor_tensor(CST[:, 3], CST[:, 2],
                                             NG[:].rearrange("p t (h y) -> p t h y", y=3)[:, :, :, 0], ALU.mult))
                    own.settle()
                    v.tensor_tensor(PCS[:], PCS[:], CST[:, 3].unsqueeze(3).to_broadcast([P, T, HEADS, 16]),
                                    ALU.mult).then_inc(cp_ready, 1)
                elif kind == "SC":
                    t, j, b = k // 8, k % 8, k % 3
                    nk = P * (t + 1)
                    dve.wait_ge(sc_full, k + 1)
                    if k == 0:
                        dve.wait_ge(y_full, 8)
                        dve.wait_ge(st_full, 2)
                    if k >= 3:
                        dve.wait_ge(pt_full, k - 2)
                    for hh in range(2):
                        for y in range(2):
                            q = 2 * hh + y
                            own.mark(v.tensor_tensor_reduce(
                                SP[b][:, hh, y, 0:nk], psum[:, 3 + hh, 256 * y:256 * y + nk],
                                CM[:, 256 - nk:256], DH ** -0.5, -3e38, ALU.add, ALU.max,
                                AMX[:, b, 0, q:q + 1]))
                    own.settle()
                    v.tensor_scalar(AMX[:, b, 1], AMX[:, b, 0], -1.0, None, ALU.mult).then_inc(nm_ready, 1)
                elif kind == "RW":
                    t, j, b = k // 8, k % 8, k % 3
                    dve.wait_ge(ex_done, k + 1)
                    own.mark(v.tensor_scalar(AMX[:, b, 2], AMX[:, b, 2], 1e-30, None, ALU.max))
                    own.settle()
                    own.mark(v.reciprocal(AMX[:, b, 2], AMX[:, b, 2]))
                    own.settle()
                    ng = NG[:, t].rearrange("p (h y) -> p h y", y=3)[:, 2 * j:2 * j + 2, 1:3]
                    v.tensor_tensor(AMX[:, b, 3].rearrange("p (h y) -> p h y", h=2),
                                    AMX[:, b, 2].rearrange("p (h y) -> p h y", h=2), ng, ALU.mult
                                    ).then_inc(w_ready, 1)
                elif kind == "PT":
                    n = 2 * P * (k // 8 + 1)
                    dve.wait_ge(pt_full, k + 1)
                    if k >= 1:
                        dve.wait_ge(pv_full, k)
                    v.tensor_copy(PTS[:, 1, 0:n], psum[:, 6, 0:n]).then_inc(pt_dve, 1)

            dve.wait_ge(sq2_ready, 4)
            own.mark(v.tensor_reduce(ss[:, 0:2], RT[:, 9, :, 0:4], AX.X, ALU.add))
            own.settle()
            v.tensor_scalar(ss[:, 0:2], ss[:, 0:2], 1.0 / D, EPS, ALU.mult, ALU.add).then_inc(lg_ready, 1)
            dve.wait_ge(sq_root, 2)
            own.mark(v.reciprocal(ss[:, 4:6], ss[:, 2:4]))
            own.settle()
            dve.wait_ge(late_in, 16 * 4)
            for h in range(2):
                cols = slice(512 * h, 512 * h + 512)
                for t in range(T):
                    v.scalar_tensor_tensor(out=H2[:, t, cols], in0=X[:, t, cols], scalar=ss[:, 4 + t:5 + t],
                                           in1=WFF[:, cols], op0=ALU.mult, op1=ALU.mult).then_inc(h2_ready, 1)
            dve.wait_ge(h2t_full, 3)
            v.tensor_copy(H2T[:, 4:6].rearrange("p a b -> p (a b)"), psum[:, 5]).then_inc(h2t_dve, 1)
            dve.wait_ge(rt_full, 1)
            own.mark(v.tensor_tensor(LG, bank(7, T, EXPERTS), RB[:].unsqueeze(1).to_broadcast([P, T, EXPERTS]),
                                     ALU.add))
            own.settle()
            for t in range(T):
                own.mark(v.max(MX8[:, t], LG[:, t]))
            own.settle()
            for t in range(T):
                own.mark(v.max_index(IX8[:, t], MX8[:, t], LG[:, t]))
                own.mark(v.tensor_scalar(RT[:, 1, t, 0:1], MX8[:, t, 0:1], -1.0, None, ALU.mult))
            own.settle()
            v.tensor_copy(RT[:, 0], IX8[:]).then_inc(mx_ready, 1)
            dve.wait_ge(mx_ready, 1)
            for t in range(T):
                own.mark(v.tensor_tensor(OH4[:, t], EIO[:].unsqueeze(1).to_broadcast([P, TOPK, EXPERTS]),
                                         RT[:, 0, t, 0:TOPK].unsqueeze(2).to_broadcast([P, TOPK, EXPERTS]),
                                         ALU.is_equal))
            own.settle()
            for t in range(T):
                own.mark(v.tensor_reduce(MSK[:, t], OH4[:, t].rearrange("p q e -> p e q"), AX.X, ALU.add))
            own.settle()
            dve.sem_inc(msk_ready, 1)
            own.mark(v.tensor_scalar(MFAR, MSK, -1e4, 1e4, ALU.mult, ALU.add))
            dve.wait_ge(te_ready, 1)
            for t in range(T):
                own.mark(v.reciprocal(RT[:, 4, t, 0:1], RT[:, 3, t, 0:1]))
            own.settle()
            for t in range(T):
                own.mark(v.tensor_scalar(RT[:, 5, t, 0:TOPK], RT[:, 2, t, 0:TOPK], RT[:, 4, t, 0:1], None, ALU.mult))
            own.settle()
            for t in range(T):
                own.mark(v.tensor_tensor(OW4[:, t], OH4[:, t], RT[:, 5, t, 0:TOPK].unsqueeze(2)
                                         .to_broadcast([P, TOPK, EXPERTS]), ALU.mult))
            own.settle()
            dve.wait_ge(zero_ready, 1)
            for t in range(T):
                for h in range(2):
                    own.mark(v.tensor_reduce(CWP[:, t, h, 0:EXPERTS], OW4[:, t].rearrange("p q e -> p e q"),
                                             AX.X, ALU.add))
            own.settle()
            dve.sem_inc(cw_ready, 1)
            dve.wait_ge(rk_full, 1)
            own.mark(v.tensor_tensor(SLT, bank(3, T, EXPERTS), MFAR, ALU.add))
            own.mark(v.tensor_reduce(RT[:, 6, 0, 0:1], bank(3, EXPERTS, off=64), AX.X, ALU.max))
            own.settle()

            def gathers(*pairs):
                for t, s in pairs:
                    own.mark(v.tensor_scalar(SPR[:, t, s], IOT[:, 0:CAP], SLT[:, t, s:s + 1], None, ALU.is_equal))

            own.mark(v.tensor_scalar(RT[:, 7, 0, 0:3], TH3[:], RT[:, 6, 0, 0:1], None, ALU.is_lt))
            gathers((0, 0), (0, 1))
            own.settle()
            own.mark(v.tensor_reduce(RT[:, 8, 0, 0:1], RT[:, 7, 0, 0:3], AX.X, ALU.add))
            gathers((1, 0))
            own.settle()
            v.tensor_scalar(RCI[:], RT[:, 8, 0, 0:1], 1.0, None, ALU.add).then_inc(round_ready, 1)
            gathers((1, 1))
            own.settle()
            dve.sem_inc(spr_ready, 1)
            dve.sem_inc(o_read, 1)
            def prepare(e0, base, first=False):
                cols = bass.ds(e0, 2)
                if first:
                    dve.sem_inc(dve_own, 4)
                v.tensor_copy(C2[:, 0], SLT[:, :, cols]).then_inc(dve_own, 1)
                v.tensor_copy(C2[:, 1], CW[:, :, cols]).then_inc(dve_own, 1)
                v.tensor_copy(OHE[0:EXPERTS], IDN[0:EXPERTS, cols].unsqueeze(2)
                              .to_broadcast([EXPERTS, 2, CAP])).then_inc(dve_own, 1)
                dve.wait_ge(dve_own, base + (7 if first else 3))
                if not first:
                    for t in range(T):
                        for s in range(2):
                            v.tensor_scalar(SPR[:, t, s], IOT[:, 0:CAP], C2[:, 0, t, s:s + 1], None,
                                            ALU.is_equal).then_inc(dve_own, 1)
                    dve.wait_ge(dve_own, base + 7)
                    dve.sem_inc(spr_ready, 1)
                v.tensor_scalar(SLT[:, :, cols], SLT[:, :, cols], float(-CAP), None, ALU.add).then_inc(dve_own, 1)
                for t in range(T):
                    for s in range(2):
                        v.tensor_scalar(CPR[:, t, s], IOT[:], C2[:, 0, t, s:s + 1], C2[:, 1, t, s:s + 1],
                                        ALU.is_equal, ALU.mult).then_inc(dve_own, 1)
                dve.wait_ge(dve_own, base + 12)
                dve.sem_inc(prep_done, 1)

            PREP = 12
            prepare(0, own.n, first=True)
            base = own.n + PREP
            per = PREP + 2
            dve.sem_inc(gu_read, 1)
            r = rounds(dve)
            with dve.Fori(0, r * EX2) as i:
                for s in range(2):
                    n = i * 2 + s
                    dve.wait_ge(unit_done, n * UNITS_E + (NU + 8))
                    gu = psum[:, 0:2, :].rearrange("p q (f two) -> p q f two", two=2)
                    v.tensor_scalar(GBU.rearrange("p (q f) -> p q f", q=2), gu[:, :, :, 0], 7.0, None, ALU.min
                                    ).then_inc(g_ready, 1)
                    v.tensor_scalar(LBU.rearrange("p (q f) -> p q f", q=2), gu[:, :, :, 1], 7.0, -7.0,
                                    ALU.min, ALU.max).then_inc(gu_read, 1)
                    dve.wait_ge(sig_ready, n + 1)
                    v.tensor_tensor(GBU, GBU, SGA, ALU.mult).then_inc(dve_own, 1)
                    dve.wait_ge(dve_own, i * per + (base + (1 if s == 0 else 2)))
                    dve.wait_ge(gu_read, n + 2)
                    v.scalar_tensor_tensor(out=ABU, in0=LBU, scalar=1.0, in1=GBU, op0=ALU.add, op1=ALU.mult
                                           ).then_inc(act_ready, 1)
                    for t in range(T):
                        dve.wait_ge(o_full, n * 2 + (t + 1))
                        xo = X[:, t].rearrange("p (a b) -> p a b", a=2)
                        v.tensor_tensor(xo, xo, psum[:, 3 + 2 * t:5 + 2 * t, :], ALU.add).then_inc(o_read, 1)
                    if s == 1:
                        dve.wait_ge(ct_full, n + 1)
                        prepare(((i + 1) % EX2) * 2, i * per + (base + 2))
            nexp = r * EXPERTS
            for t in range(T):
                dve.wait_ge(o_full, nexp * 2 + (t + 1))
                xo = X[:, t].rearrange("p (a b) -> p a b", a=2)
                v.tensor_tensor(xo, xo, psum[:, 3 + 2 * t:5 + 2 * t, :], ALU.add).then_inc(final_in, 1)
            dve.wait_ge(final_in, T)
            dve.wait_ge(ss_ready, 4)
            v.tensor_scalar(ss[:, 0:2], ss[:, 0:2], 1.0 / D, EPS, ALU.mult, ALU.add).then_inc(lg_ready, 2)
            dve.wait_ge(sq_root, 3)
            v.reciprocal(ss[:, 4:6], ss[:, 2:4]).then_inc(lg_ready, 1)
            dve.wait_ge(lg_ready, 4)
            for t in range(T):
                v.scalar_tensor_tensor(out=RJ[:, t], in0=X[:, t], scalar=ss[:, 4 + t:5 + t], in1=WFN,
                                       op0=ALU.mult, op1=ALU.mult).then_inc(norm_ready, 1)


_INS = ['x', 'mix_norm_w', 'w_in', 'conv_w', 'conv_b', 'dt_bias', 'a_log', 'd_skip', 'ssm_norm_w',
        'cmp_pos_k', 'cmp_w1_k', 'cmp_w2_k', 'cmp_pos_v', 'cmp_w1_v', 'cmp_w2_v', 'w_branch_ssm',
        'w_branch_nsa', 'w_out', 'ffn_norm_w', 'router_w', 'router_b', 'w_gate_up', 'b_gate_up', 'w_down',
        'b_down', 'final_norm_w']


def kernel(**inputs):
    import numpy as _np
    import concourse.bacc as _bacc
    from concourse import mybir as _mybir
    from concourse.bass_utils import run_bass_kernel_spmd as _run

    nc = _bacc.Bacc("TRN2", target_bir_lowering=False, num_devices=1)
    arrays, args = {}, []
    for name in _INS:
        a = _np.ascontiguousarray(inputs[name])
        arrays[f"in_{name}_dram"] = a
        args.append(nc.dram_tensor(f"in_{name}_dram", a.shape, _mybir.dt.from_np(a.dtype), kind="ExternalInput").ap())
    args.append(nc.dram_tensor("out_0_dram", (1, 256, 1024), _mybir.dt.float32, kind="ExternalOutput").ap())
    hybrid_block(nc, *args)
    r = _run(nc, [arrays], core_ids=[0])
    return r.results[0]["out_0_dram"]
```
